# Optimizing a Trainium2 kernel written in Bass

```python
import jax
import jax.numpy as jnp
from jax import lax
import numpy as np

D_MODEL = 1024
BATCH = 1
SEQ = 1024
DEPTH = 1

MEM_LEN = 256
ROPE_THETA = 10000.0
MAX_POS_OFFSET = 1024

RET_HEADS = 4
RET_DK = 64
RET_DV = 64
RET_CHUNK = 128
RET_W = RET_HEADS * RET_DV

SGU_GROUPS = 4
SGU_DIM = 64
SGU_CHUNK = 128
SGU_W = SGU_GROUPS * SGU_DIM

MLA_HEADS = 8
MLA_Q_RANK = 256
MLA_KV_RANK = 128
MLA_NOPE = 64
MLA_ROPE = 32
MLA_V = 64
MLA_W = MLA_HEADS * MLA_V
ATTN_BLOCK = 128

D_MIX = RET_W + SGU_W + MLA_W
IN_COLS = 4 * RET_W + 2 * SGU_W + MLA_Q_RANK + MLA_KV_RANK + MLA_ROPE

XA_HEADS = 4
XA_DIM = 128
XA_W = XA_HEADS * XA_DIM

N_EXPERTS = 16
N_GROUPS = 4
EXPERTS_PER_GROUP = N_EXPERTS // N_GROUPS
TOP_K = 2
D_EXPERT = 256

DEEPNORM_ALPHA = (2 * DEPTH) ** 0.25
DEEPNORM_BETA = (8 * DEPTH) ** -0.25
LN_EPS = 1e-5

kernel_name = 'hybrid_retention_sgu_mla_moe'

def layer_norm(x, g, b):
    xf = x.astype(jnp.float32)
    mu = jnp.mean(xf, axis=-1, keepdims=True)
    var = jnp.mean(jnp.square(xf - mu), axis=-1, keepdims=True)
    return ((xf - mu) * lax.rsqrt(var + LN_EPS)).astype(x.dtype) * g + b

def rms_norm(x, g):
    xf = x.astype(jnp.float32)
    ms = jnp.mean(jnp.square(xf), axis=-1, keepdims=True)
    return (xf * lax.rsqrt(ms + LN_EPS)).astype(x.dtype) * g

def head_group_norm(x):
    xf = x.astype(jnp.float32)
    mu = jnp.mean(xf, axis=-1, keepdims=True)
    var = jnp.mean(jnp.square(xf - mu), axis=-1, keepdims=True)
    return ((xf - mu) * lax.rsqrt(var + LN_EPS)).astype(x.dtype)

def rope_cos_sin(positions, dim):
    inv_freq = ROPE_THETA ** (-jnp.arange(0, dim, 2, dtype=jnp.float32) / dim)
    ang = positions.astype(jnp.float32)[..., None] * inv_freq
    return jnp.cos(ang)[:, :, None, :], jnp.sin(ang)[:, :, None, :]

def apply_rope(x, cos, sin):
    x1, x2 = jnp.split(x, 2, axis=-1)
    cos = cos.astype(x.dtype)
    sin = sin.astype(x.dtype)
    return jnp.concatenate([x1 * cos - x2 * sin, x1 * sin + x2 * cos], axis=-1)

def retention_chunkwise(q, k, v):
    b, s, h, dk = q.shape
    dv = v.shape[-1]
    c = RET_CHUNK
    nc = s // c
    log_gamma = jnp.log1p(-(2.0 ** (-5.0 - jnp.arange(h, dtype=jnp.float32))))
    pos = jnp.arange(c, dtype=jnp.float32)
    diff = pos[:, None] - pos[None, :]
    intra_decay = jnp.where(diff >= 0,
                            jnp.exp(log_gamma[:, None, None] * jnp.maximum(diff, 0.0)),
                            0.0).astype(q.dtype)
    inner_decay = jnp.exp(log_gamma[None, :] * (c - 1 - pos)[:, None]).astype(q.dtype)
    query_decay = jnp.exp(log_gamma[None, :] * (pos + 1)[:, None]).astype(q.dtype)
    chunk_decay = jnp.exp(log_gamma * c)
    qc = q.reshape(b, nc, c, h, dk)
    kc = (k * dk ** -0.5).reshape(b, nc, c, h, dk)
    vc = v.reshape(b, nc, c, h, dv)
    scores = jnp.einsum('bcnhd,bcmhd->bchnm', qc, kc) * intra_decay
    intra = jnp.einsum('bchnm,bcmhv->bcnhv', scores, vc)
    chunk_kv = jnp.einsum('bcmhd,mh,bcmhv->bchdv', kc, inner_decay, vc)

    def step(state, kv_c):
        return state * chunk_decay[:, None, None].astype(state.dtype) + kv_c, state

    _, prev = lax.scan(step, jnp.zeros_like(chunk_kv[:, 0]), jnp.moveaxis(chunk_kv, 1, 0))
    prev = jnp.moveaxis(prev, 0, 1)
    cross = jnp.einsum('bcnhd,nh,bchdv->bcnhv', qc, query_decay, prev)
    return (intra + cross).reshape(b, s, h, dv)

def spatial_gating(u, v, w_s, b_s):
    b, s, _ = u.shape
    c = SGU_CHUNK
    nc = s // c
    causal = jnp.tril(jnp.ones((c, c), dtype=bool))
    w = jnp.where(causal[None], w_s, 0.0)
    vc = v.reshape(b, nc, c, SGU_GROUPS, SGU_DIM)
    mixed = jnp.einsum('gts,bcsgd->bctgd', w, vc) + b_s.T[:, :, None]
    return u * mixed.reshape(b, s, SGU_W)

def causal_block_attention(q, k, v, scale):
    b, s, h, d = q.shape
    dv = v.shape[-1]
    nb = s // ATTN_BLOCK
    qb = jnp.moveaxis(q.reshape(b, nb, ATTN_BLOCK, h, d), 1, 0)
    key_pos = jnp.arange(s)

    def one_block(args):
        q_blk, i = args
        sc = jnp.einsum('bqhd,bkhd->bhqk', q_blk, k).astype(jnp.float32) * scale
        q_pos = i * ATTN_BLOCK + jnp.arange(ATTN_BLOCK)
        mask = key_pos[None, :] <= q_pos[:, None]
        p = jax.nn.softmax(jnp.where(mask, sc, -jnp.inf), axis=-1).astype(v.dtype)
        return jnp.einsum('bhqk,bkhd->bqhd', p, v)

    out = lax.map(one_block, (qb, jnp.arange(nb)))
    return jnp.moveaxis(out, 0, 1).reshape(b, s, h, dv)

def latent_attention(c_q, c_kv, k_rope, cos_m, sin_m, q_norm_g, w_uq, kv_norm_g, w_ukv):
    b, s, _ = c_q.shape
    q = (rms_norm(c_q, q_norm_g) @ w_uq).reshape(b, s, MLA_HEADS, MLA_NOPE + MLA_ROPE)
    q_nope, q_rope = jnp.split(q, [MLA_NOPE], axis=-1)
    q = jnp.concatenate([q_nope, apply_rope(q_rope, cos_m, sin_m)], axis=-1)
    kv = (rms_norm(c_kv, kv_norm_g) @ w_ukv).reshape(b, s, MLA_HEADS, MLA_NOPE + MLA_V)
    k_nope, v = jnp.split(kv, [MLA_NOPE], axis=-1)
    k_rope = apply_rope(k_rope[:, :, None, :], cos_m, sin_m)
    k = jnp.concatenate([k_nope, jnp.broadcast_to(k_rope, (b, s, MLA_HEADS, MLA_ROPE))], axis=-1)
    o = causal_block_attention(q, k, v, (MLA_NOPE + MLA_ROPE) ** -0.5)
    return o.reshape(b, s, MLA_W)

def hybrid_mixer(x, cos_r, sin_r, cos_m, sin_m, w_in, w_out, sgu_ln_g, sgu_ln_b, sgu_w, sgu_b,
                 q_norm_g, w_uq, kv_norm_g, w_ukv):
    b, s, _ = x.shape
    sizes = (RET_W, RET_W, RET_W, RET_W, SGU_W, SGU_W, MLA_Q_RANK, MLA_KV_RANK, MLA_ROPE)
    split_points = [int(p) for p in np.cumsum(sizes)[:-1]]
    rq, rk, rv, rg, su, sv, cq, ckv, kr = jnp.split(x @ w_in, split_points, axis=-1)
    rq = apply_rope(rq.reshape(b, s, RET_HEADS, RET_DK), cos_r, sin_r)
    rk = apply_rope(rk.reshape(b, s, RET_HEADS, RET_DK), cos_r, sin_r)
    rv = rv.reshape(b, s, RET_HEADS, RET_DV)
    ret = head_group_norm(retention_chunkwise(rq, rk, rv)).reshape(b, s, RET_W)
    ret = jax.nn.silu(rg) * ret
    sgu = spatial_gating(su, layer_norm(sv, sgu_ln_g, sgu_ln_b), sgu_w, sgu_b)
    mla = latent_attention(cq, ckv, kr, cos_m, sin_m, q_norm_g, w_uq, kv_norm_g, w_ukv)
    return jnp.concatenate([ret, sgu, mla], axis=-1) @ w_out

def memory_cross_attention(x, mem, wq, wk, wv, wo):
    b, s, _ = x.shape
    m = mem.shape[1]
    q = (x @ wq).reshape(b, s, XA_HEADS, XA_DIM)
    k = (mem @ wk).reshape(b, m, XA_HEADS, XA_DIM)
    v = (mem @ wv).reshape(b, m, XA_HEADS, XA_DIM)
    sc = jnp.einsum('bshd,bmhd->bhsm', q, k).astype(jnp.float32) * XA_DIM ** -0.5
    p = jax.nn.softmax(sc, axis=-1).astype(v.dtype)
    o = jnp.einsum('bhsm,bmhd->bshd', p, v).reshape(b, s, XA_W)
    return o @ wo

def grouped_moe(x, router_w, router_bias, w_gate, w_up, w_down):
    b, s, d = x.shape
    t = x.reshape(b * s, d)
    scores = jax.nn.sigmoid((t @ router_w).astype(jnp.float32))
    biased = (scores + router_bias.astype(jnp.float32)).reshape(-1, N_GROUPS, EXPERTS_PER_GROUP)
    group_score = jnp.sum(lax.top_k(biased, TOP_K)[0], axis=-1)
    sel_group = jnp.argmax(group_score, axis=-1)
    in_group = jnp.take_along_axis(biased, sel_group[:, None, None], axis=1)[:, 0]
    _, local_idx = lax.top_k(in_group, TOP_K)
    expert_idx = sel_group[:, None] * EXPERTS_PER_GROUP + local_idx
    gate = jnp.take_along_axis(scores, expert_idx, axis=1)
    gate = gate / jnp.sum(gate, axis=-1, keepdims=True)
    combine = jnp.sum(jax.nn.one_hot(expert_idx, N_EXPERTS, dtype=jnp.float32) * gate[..., None],
                      axis=1).astype(t.dtype)
    y = jnp.zeros_like(t)
    for e in range(N_EXPERTS):
        h = jax.nn.silu(t @ w_gate[e]) * (t @ w_up[e])
        y = y + combine[:, e:e + 1] * (h @ w_down[e])
    return y.reshape(b, s, d)

def setup_inputs(seed: int = 0) -> dict:
    key = jax.random.key(seed)
    ks = iter(jax.random.split(key, 40))

    def nrm(shape, scale):
        return jax.random.normal(next(ks), shape, jnp.float32) * scale

    L = DEPTH
    x = nrm((BATCH, SEQ, D_MODEL), 1.0)
    mem = nrm((BATCH, MEM_LEN, D_MODEL), 1.0)
    offset = jax.random.randint(next(ks), (BATCH, 1), 0, MAX_POS_OFFSET, dtype=jnp.int32)
    positions = offset + jnp.arange(SEQ, dtype=jnp.int32)[None, :]
    return {
        'x': x,
        'mem': mem,
        'positions': positions,
        'w_in': nrm((L, D_MODEL, IN_COLS), D_MODEL ** -0.5),
        'w_out': nrm((L, D_MIX, D_MODEL), DEEPNORM_BETA * D_MIX ** -0.5),
        'sgu_ln_g': 1.0 + nrm((L, SGU_W), 0.01),
        'sgu_ln_b': nrm((L, SGU_W), 0.01),
        'sgu_w': nrm((L, SGU_GROUPS, SGU_CHUNK, SGU_CHUNK), SGU_CHUNK ** -0.5),
        'sgu_b': 1.0 + nrm((L, SGU_GROUPS, SGU_CHUNK), 0.01),
        'mla_q_norm_g': 1.0 + nrm((L, MLA_Q_RANK), 0.01),
        'mla_w_uq': nrm((L, MLA_Q_RANK, MLA_HEADS * (MLA_NOPE + MLA_ROPE)), MLA_Q_RANK ** -0.5),
        'mla_kv_norm_g': 1.0 + nrm((L, MLA_KV_RANK), 0.01),
        'mla_w_ukv': nrm((L, MLA_KV_RANK, MLA_HEADS * (MLA_NOPE + MLA_V)), MLA_KV_RANK ** -0.5),
        'xa_wq': nrm((L, D_MODEL, XA_W), D_MODEL ** -0.5),
        'xa_wk': nrm((L, D_MODEL, XA_W), D_MODEL ** -0.5),
        'xa_wv': nrm((L, D_MODEL, XA_W), D_MODEL ** -0.5),
        'xa_wo': nrm((L, XA_W, D_MODEL), DEEPNORM_BETA * XA_W ** -0.5),
        'ln_mix_g': 1.0 + nrm((L, D_MODEL), 0.01),
        'ln_mix_b': nrm((L, D_MODEL), 0.01),
        'ln_xa_g': 1.0 + nrm((L, D_MODEL), 0.01),
        'ln_xa_b': nrm((L, D_MODEL), 0.01),
        'ln_moe_g': 1.0 + nrm((L, D_MODEL), 0.01),
        'ln_moe_b': nrm((L, D_MODEL), 0.01),
        'router_w': nrm((D_MODEL, N_EXPERTS), D_MODEL ** -0.5),
        'router_bias': nrm((N_EXPERTS,), 0.01),
        'expert_w_gate': nrm((L, N_EXPERTS, D_MODEL, D_EXPERT), D_MODEL ** -0.5),
        'expert_w_up': nrm((L, N_EXPERTS, D_MODEL, D_EXPERT), D_MODEL ** -0.5),
        'expert_w_down': nrm((L, N_EXPERTS, D_EXPERT, D_MODEL), DEEPNORM_BETA * D_EXPERT ** -0.5),
    }

def reference(x, mem, positions, w_in, w_out, sgu_ln_g, sgu_ln_b, sgu_w, sgu_b,
              mla_q_norm_g, mla_w_uq, mla_kv_norm_g, mla_w_ukv,
              xa_wq, xa_wk, xa_wv, xa_wo,
              ln_mix_g, ln_mix_b, ln_xa_g, ln_xa_b, ln_moe_g, ln_moe_b,
              router_w, router_bias, expert_w_gate, expert_w_up, expert_w_down):
    cos_r, sin_r = rope_cos_sin(positions, RET_DK)
    cos_m, sin_m = rope_cos_sin(positions, MLA_ROPE)
    for l in range(DEPTH):
        mix = hybrid_mixer(x, cos_r, sin_r, cos_m, sin_m, w_in[l], w_out[l],
                           sgu_ln_g[l], sgu_ln_b[l], sgu_w[l], sgu_b[l],
                           mla_q_norm_g[l], mla_w_uq[l], mla_kv_norm_g[l], mla_w_ukv[l])
        x = layer_norm(DEEPNORM_ALPHA * x + mix, ln_mix_g[l], ln_mix_b[l])
        xa = memory_cross_attention(x, mem, xa_wq[l], xa_wk[l], xa_wv[l], xa_wo[l])
        x = layer_norm(DEEPNORM_ALPHA * x + xa, ln_xa_g[l], ln_xa_b[l])
        ffn = grouped_moe(x, router_w, router_bias, expert_w_gate[l], expert_w_up[l], expert_w_down[l])
        x = layer_norm(DEEPNORM_ALPHA * x + ffn, ln_moe_g[l], ln_moe_b[l])
    return x


_drawn_inputs = setup_inputs


def setup_inputs(seed=0):
    import zlib

    import numpy as np

    out = dict(_drawn_inputs(seed))
    spreads = {}
    factors = {'sgu_ln_g': 22.836,
     'sgu_ln_b': 22.18,
     'sgu_b': 15.521,
     'mla_q_norm_g': 8.0,
     'mla_kv_norm_g': 7.297,
     'ln_moe_g': 30.191,
     'ln_moe_b': 30.995,
     'ln_xa_g': 2.685}
    for name, (base, spread) in spreads.items():
        noise = np.random.default_rng([zlib.crc32(name.encode()), seed]).standard_normal(out[name].shape)
        drawn = base * np.exp(spread * noise) if base else spread * noise
        out[name] = jnp.asarray(drawn.astype(out[name].dtype))
    for name, factor in factors.items():
        out[name] = (out[name] * factor).astype(out[name].dtype)
    return out
```

```python
import math

import concourse.bass as bass
import numpy as np
from concourse import mybir

f32 = mybir.dt.float32
f32r = mybir.dt.float32r
i32 = mybir.dt.int32
bf16 = mybir.dt.bfloat16
ACT = mybir.ActivationFunctionType
ALU = mybir.AluOpType
AX = mybir.AxisListType

P = 128
S, D = 1024, 1024
NT = S // P
KD = D // P
MEM = 256
RH, RD = 4, 64
RW = RH * RD
SG, SD = 4, 64
SW = SG * SD
MH, NOPE, ROPE, MV = 8, 64, 32, 64
MQ = NOPE + ROPE
QR, KVR = 256, 128
MW = MH * MV
XH, XD = 4, 128
XW = XH * XD
NE, NG, EG, DE = 16, 4, 4, 256
CAP = 192
EPS = 1e-5
ALPHA = 2.0 ** 0.25
MLA_SCALE = MQ ** -0.5
XA_SCALE = XD ** -0.5
NEG = -1.0e30
CH_QK, CH_VG, CH_UV, CH_LAT = range(4)
CHUNK_W = [2 * RW, 2 * RW, 2 * SW, QR + KVR + ROPE]
CHUNK_AT = [0, 2 * RW, 4 * RW, 4 * RW + 2 * SW]
IN_COLS = sum(CHUNK_W)

C_ID, C_MASK, C_DEC, C_QDEC, C_INNER, C_ST, C_FREQ, C_TRI = 0, 128, 256, 768, 1024, 1280, 1282, 1346
C_COLS = 1474
NF = 64

SBUF_BASE = 16640


def constants():
    c = np.zeros((P, C_COLS), np.float64)
    r = np.arange(P)
    lg = np.log1p(-(2.0 ** (-5.0 - np.arange(RH))))
    c[:, C_ID:C_ID + P] = np.eye(P)
    c[:, C_MASK:C_MASK + P] = np.where(r[None, :] <= r[:, None], 0.0, NEG)
    for h in range(RH):
        diff = r[None, :] - r[:, None]
        dec = np.where(diff >= 0, np.exp(lg[h] * np.maximum(diff, 0)), 0.0) * RD ** -0.5
        c[:, C_DEC + P * h:C_DEC + P * (h + 1)] = dec
        c[:, C_INNER + RD * h:C_INNER + RD * (h + 1)] = (np.exp(lg[h] * (P - 1 - r)) * RD ** -0.5)[:, None]
        rows = slice(RD * (h % 2), RD * (h % 2) + RD)
        c[rows, C_QDEC + P * (h // 2):C_QDEC + P * (h // 2) + P] = np.exp(lg[h] * (r + 1))[None, :]
        c[rows, C_ST + h // 2] = np.exp(lg[h] * P)
    fr, fm = ((10000.0 ** (-np.arange(0, d, 2, dtype=np.float32) / np.float32(d)).astype(np.float64))
              .astype(np.float32) for d in (RD, ROPE))
    c[:, C_FREQ:C_FREQ + NF] = np.concatenate([fr, fm, fm])[None, :]
    c[:, C_TRI:C_TRI + P] = (r[:, None] <= r[None, :])
    return c.astype(np.float32)


class Shared:
    pass


def placer(nc):
    def at(name, kib, shape, dt=f32):
        return nc.alloc_sbuf_tensor_at(name, shape, dt, offset=SBUF_BASE + int(kib * 1024))
    return at


def over(ap, shape):
    return ap.broadcast_to(shape)


def project(nc, k):
    at, A = k.at, k.dram
    RAWX, RAWW = 4, 8
    xhi = at("xhi", 73, [P, KD, S], f32r)
    xlo = at("xlo", 105, [P, KD, S], f32r)
    whi = at("whi", 137, [P, KD, 512], f32r)
    wlo = at("wlo", 153, [P, KD, 512], f32r)
    xraw = at("xraw", 169, [P, RAWX, S])
    wraw = at("wraw", 185, [P, RAWW, 512])
    ta = at("rope_a", 201, [P, 512])
    tb = at("rope_b", 203, [P, 512])
    ang = at("ang", 12, [P, NT, NF])
    turns = at("turns", 14, [P, NT, NF])
    posi = at("posi", 205, [P, NT], i32)
    posf = at("posf", 205.125, [P, NT])
    ssq = at("ssq", 205.25, [P, NT, 2])
    stat = at("stat", 205.5, [P, 6])
    mv = at("mv", 205.625, [P, 2])
    rs = at("rs", 205.75, [P, 2])
    halfs = at("halfs", 205.875, [P, 2])
    junk = at("junk", 205.9375, [P, 256])
    gsg = at("sgu_g", 10, [P, SW])
    bsg = at("sgu_bb", 11, [P, SW])

    x_loaded = [k.sem(f"x_loaded{i}") for i in range(RAWX)]
    w_loaded = [k.sem(f"w_loaded{i}") for i in range(RAWW)]
    small_loaded = k.sem("small_loaded")
    norm_loaded = k.sem("norm_loaded")
    x_hi_done = k.sem("x_hi_done")
    x_lo_done = k.sem("x_lo_done")
    w_hi_done = k.sem("w_hi_done")
    w_lo_done = k.sem("w_lo_done")
    w_slice_used = k.sem("w_slice_used")
    unit_summed = k.sem("unit_summed")
    unit_taken = k.sem("unit_taken")
    act_part = k.sem("act_part")
    dve_chain = k.sem("dve_chain")
    var_ready = k.sem("var_ready")
    rstd_ready = k.sem("rstd_ready")
    pool_chain = k.sem("pool_chain")
    angles = k.sem("angles")
    tables = k.sem("tables")
    with nc.psum_tensor("unit_ps", [P, 4, 512], f32) as ps, \
            nc.Block() as block:
        units = [(c, t) for c in (CH_QK, CH_LAT, CH_UV, CH_VG) for t in range(NT)]
        order = [CH_QK, CH_LAT, CH_UV, CH_VG]
        BANKS = 4

        def slice_free(eng, c, s):
            if c and s < KD - 1:
                eng.wait_ge(w_slice_used, (c - 1) * (KD - 1) + s + 1)
            elif c:
                eng.wait_ge(unit_summed, c * NT)

        @block.sync
        def _(sp):
            sp.dma_start(k.cst[:], A["cst"]).then_inc(small_loaded, 16)
            sp.dma_start(posi[:], A["positions"]).then_inc(small_loaded, 16)
            for c in range(4):
                for s in range(KD):
                    n = c * KD + s
                    if c == 0:
                        if s >= RAWX:
                            sp.wait_ge(x_lo_done, s - RAWX + 1)
                        sp.dma_start(xraw[:, s % RAWX, :], A["xT"][s]).then_inc(x_loaded[s % RAWX], 16)
                    if n >= RAWW:
                        sp.wait_ge(w_lo_done, n - RAWW + 1)
                    w = CHUNK_W[order[c]]
                    o = CHUNK_AT[order[c]]
                    sp.dma_start(wraw[:, s, 0:w], A["w_in"][s * P:(s + 1) * P, o:o + w]).then_inc(w_loaded[s], 16)
                if c == 0:
                    sp.dma_start(gsg[:], over(A["sgu_ln_g"], [P, SW])).then_inc(norm_loaded, 16)
                    sp.dma_start(bsg[:], over(A["sgu_ln_b"], [P, SW])).then_inc(norm_loaded, 16)

        @block.scalar
        def _(act):
            def split_w(c, s):
                n = c * KD + s
                w = CHUNK_W[order[c]]
                act.wait_ge(w_loaded[s], 16 * (c + 1))
                slice_free(act, c, s)
                act.activation(whi[:, s, 0:w], wraw[:, s, 0:w], ACT.Copy).then_inc(w_hi_done, 1)

            for s in range(KD):
                act.wait_ge(x_loaded[s % RAWX], 16 * (s // RAWX + 1))
                act.activation(xhi[:, s, :], xraw[:, s % RAWX, :], ACT.Copy).then_inc(x_hi_done, 1)
                split_w(0, s)
                if s == 1:
                    act.wait_ge(angles, 1)
                    act.activation(k.sin[:], ang[:], ACT.Sin).then_inc(tables, 1)
                    act.wait_ge(angles, 2)
                    act.activation(k.cos[:], turns[:], ACT.Sin).then_inc(tables, 1)
            n_part = 0
            for u, (c, t) in enumerate(units):
                b = u % BANKS
                if u and u % NT == 0:
                    for s in range(KD):
                        split_w(u // NT, s)
                act.wait_ge(unit_summed, u + 1)
                if c == CH_VG:
                    act.activation(k.rv[:, t, :], ps[:, b, 0:RW], ACT.Copy).then_inc(act_part, 1)
                    if t >= 2:
                        act.wait_ge(unit_taken, u - 1)
                    act.activation(xraw[:, t % 2, 0:RW], ps[:, b, RW:2 * RW], ACT.Tanh, scale=0.5).then_inc(act_part, 1)
                elif c == CH_UV:
                    act.activation(k.su[:, t, :], ps[:, b, 0:SW], ACT.Copy).then_inc(act_part, 1)
                elif c == CH_LAT:
                    if t:
                        act.wait_ge(act_part, 2 * t)
                    act.activation(junk[:, 0:QR], ps[:, b, 0:QR], ACT.Square, accum_out=ssq[:, t, 0:1]).then_inc(act_part, 1)
                    act.wait_ge(act_part, 2 * t + 1)
                    act.activation(junk[:, 0:KVR], ps[:, b, QR:QR + KVR], ACT.Square, accum_out=ssq[:, t, 1:2]).then_inc(act_part, 1)

        @block.tensor
        def _(pe):
            for u, (c, t) in enumerate(units):
                ci, b, w = u // NT, u % BANKS, CHUNK_W[c]
                if u >= BANKS:
                    pe.wait_ge(unit_taken, u - BANKS + 1)
                for s in range(KD):
                    if ci == 0 and t == 0:
                        pe.wait_ge(x_lo_done, s + 1)
                    if t == 0:
                        pe.wait_ge(w_lo_done, ci * KD + s + 1)
                    hi, lo = xhi[:, s, t * P:(t + 1) * P], xlo[:, s, t * P:(t + 1) * P]
                    o = ps[:, b, 0:w]
                    pe.matmul(o, hi, whi[:, s, 0:w], start=(s == 0), stop=False)
                    pe.matmul(o, hi, wlo[:, s, 0:w], start=False, stop=False)
                    last = pe.matmul(o, lo, whi[:, s, 0:w], start=False, stop=(s == KD - 1))
                    if t == NT - 1 and s < KD - 1:
                        last.then_inc(w_slice_used, 1)
                last.then_inc(unit_summed, 1)

        @block.vector
        def _(dve):
            chain = [0]

            def link(ins):
                chain[0] += 1
                ins.then_inc(dve_chain, 1)
                dve.wait_ge(dve_chain, chain[0])

            def split_w(c, s):
                n = c * KD + s
                w = CHUNK_W[order[c]]
                dve.wait_ge(w_hi_done, n + 1)
                dve.tensor_tensor(wlo[:, s, 0:w], wraw[:, s, 0:w], whi[:, s, 0:w].bitcast(f32), ALU.subtract)\
                   .then_inc(w_lo_done, 1)

            dve.wait_ge(small_loaded, 32)
            link(dve.tensor_copy(posf[:], posi[:]))
            freq = k.cst[:, None, C_FREQ:C_FREQ + NF]
            link(dve.tensor_tensor(ang[:], over(posf[:, :, None], [P, NT, NF]), over(freq, [P, NT, NF]), ALU.mult))
            magic = 1.5 * 2.0 ** 23
            link(dve.tensor_scalar(turns[:], ang[:], 1.0 / (2 * math.pi), magic, ALU.mult, ALU.add))
            link(dve.tensor_scalar(turns[:], turns[:], magic, None, ALU.subtract))
            p1 = 6.28125
            p2 = 0.0019350051879882812
            p3 = 2 * math.pi - p1 - p2
            for part in (p1, p2, p3):
                link(dve.scalar_tensor_tensor(ang[:], turns[:], -part, ang[:], ALU.mult, ALU.add))
            pi = 3.1415925
            link(dve.tensor_scalar(ang[:], ang[:], -pi, pi, ALU.max, ALU.min))
            dve.scalar_tensor_tensor(turns[:], ang[:], -1.0, ang[:], ALU.mult, ALU.min).then_inc(angles, 1)
            dve.wait_ge(angles, 1)
            dve.tensor_scalar(turns[:], turns[:], math.pi / 2, None, ALU.add).then_inc(angles, 1)

            for s in range(KD):
                dve.wait_ge(x_hi_done, s + 1)
                dve.tensor_tensor(xlo[:, s, :], xraw[:, s % RAWX, :], xhi[:, s, :].bitcast(f32), ALU.subtract)\
                   .then_inc(x_lo_done, 1)
                split_w(0, s)
            dve.wait_ge(tables, 2)
            dve.wait_ge(norm_loaded, 32)
            for u, (c, t) in enumerate(units):
                b = u % BANKS
                if u and u % NT == 0:
                    for s in range(KD):
                        split_w(u // NT, s)
                dve.wait_ge(unit_summed, u + 1)
                if c == CH_QK:
                    x = ps[:, b, :].rearrange("p (g f) -> p g f", f=32)
                    cb, sb_ = over(k.cos[:, t:t + 1, 0:32], [P, 16, 32]), over(k.sin[:, t:t + 1, 0:32], [P, 16, 32])
                    a3, b3 = (z[:].rearrange("p (g f) -> p g f", f=32) for z in (ta, tb))
                    dve.tensor_tensor(a3, x, cb, ALU.mult)
                    dve.tensor_tensor(b3, x, sb_, ALU.mult).then_inc(unit_taken, 1)
                    dve.wait_ge(unit_taken, u + 1)
                    a4, b4, o4 = (z.rearrange("p (g i f) -> p g i f", i=2, f=32) for z in (ta[:], tb[:], k.qk[:, t, :]))
                    dve.tensor_tensor(o4[:, :, 0, :], a4[:, :, 0, :], b4[:, :, 1, :], ALU.subtract)
                    link(dve.tensor_tensor(o4[:, :, 1, :], b4[:, :, 0, :], a4[:, :, 1, :], ALU.add))
                elif c == CH_LAT:
                    x = ps[:, b, QR + KVR:QR + KVR + ROPE]
                    dve.wait_ge(act_part, 2 * t + 2)
                    dve.tensor_tensor(ta[:, 0:ROPE], x, k.cos[:, t, 32:64], ALU.mult)
                    link(dve.tensor_tensor(tb[:, 0:ROPE], x, k.sin[:, t, 32:64], ALU.mult))
                    dve.tensor_tensor(k.kr[:, t, 0:16], ta[:, 0:16], tb[:, 16:32], ALU.subtract)
                    link(dve.tensor_tensor(k.kr[:, t, 16:32], tb[:, 0:16], ta[:, 16:32], ALU.add))
                    dve.wait_ge(rstd_ready, t + 1)
                    dve.tensor_scalar(k.cq[:, t, :], ps[:, b, 0:QR], rs[:, 0:1], None, ALU.mult)
                    dve.tensor_scalar(k.ckv[:, t, :], ps[:, b, QR:QR + KVR], rs[:, 1:2], None, ALU.mult)\
                       .then_inc(unit_taken, 1)
                elif c == CH_UV:
                    dve.wait_ge(act_part, 2 * NT + t + 1)
                    link(dve.bn_stats(stat[:], ps[:, b, SW:2 * SW]))
                    dve.bn_aggr(mv[:], stat[:]).then_inc(var_ready, 1)
                    dve.wait_ge(rstd_ready, NT + t + 1)
                    dve.tensor_scalar(ta[:, 0:SW], ps[:, b, SW:2 * SW], mv[:, 0:1], rs[:, 0:1], ALU.subtract, ALU.mult)\
                       .then_inc(unit_taken, 1)
                    dve.wait_ge(unit_taken, u + 1)
                    link(dve.tensor_tensor(tb[:, 0:SW], ta[:, 0:SW], gsg[:], ALU.mult))
                    link(dve.tensor_tensor(k.sv[:, t, :], tb[:, 0:SW], bsg[:], ALU.add))
                else:
                    dve.wait_ge(act_part, 3 * NT + 2 * t + 2)
                    dve.scalar_tensor_tensor(k.sg[:, t, :], xraw[:, t % 2, 0:RW], 1.0, ps[:, b, RW:2 * RW], ALU.add, ALU.mult)\
                       .then_inc(unit_taken, 1)

        @block.gpsimd
        def _(pool):
            chain = [0]

            def link(ins):
                chain[0] += 1
                ins.then_inc(pool_chain, 1)
                pool.wait_ge(pool_chain, chain[0])

            link(pool.memset(halfs[:], -0.5))
            for t in range(NT):
                pool.wait_ge(act_part, 2 * t + 2)
                link(pool.tensor_scalar(ssq[:, t, 0:1], ssq[:, t, 0:1], 1.0 / QR, EPS, ALU.mult, ALU.add))
                link(pool.tensor_scalar(ssq[:, t, 1:2], ssq[:, t, 1:2], 1.0 / KVR, EPS, ALU.mult, ALU.add))
                if t:
                    pool.wait_ge(unit_taken, NT + t)
                pool.tensor_tensor(rs[:], ssq[:, t, :], halfs[:], ALU.pow).then_inc(rstd_ready, 1)
            for t in range(NT):
                pool.wait_ge(var_ready, t + 1)
                link(pool.tensor_scalar(mv[:, 1:2], mv[:, 1:2], EPS, None, ALU.add))
                pool.wait_ge(unit_taken, 2 * NT + t)
                pool.tensor_tensor(rs[:, 0:1], mv[:, 1:2], halfs[:, 0:1], ALU.pow).then_inc(rstd_ready, 1)


def prepare(nc, k):
    at, A, cst = k.at, k.dram, k.cst
    lat = at("lat_T", 185, [P, 2, QR + KVR])
    qkt = at("qk_T", 188, [P, 2, 4 * P])
    wuq = at("w_uq", 192, [P, QR // P, MH * MQ])
    wukv = at("w_ukv", 198, [P, 2 * MW])
    wsg = at("sgu_wT", 202, [P, SG, P])
    sc = at("ret_scores", 204, [P, RH, P])
    qdt = at("ret_qd", 206, [P, 2 * P])
    gq = at("q_norm_g", 10, [P, 2])
    gkv = at("kv_norm_g", 10.0625, [P, 1])
    sgb = at("sgu_bias", 10.125, [P, SG])
    mv4 = at("ret_mv", 10.25, [P, RH, 2])
    st4 = at("ret_stat", 10.375, [P, RH, 6])
    rs4 = at("ret_rstd", 10.5, [P, RH])
    half4 = at("ret_half", 10.5625, [P, RH])
    ve4 = at("ret_var", 10.625, [P, RH])
    state = at("ret_state", 10.75, [P, 2, 2 * RD])
    qtok = at("q_tok", 89, [P, 2, MH, MQ])
    ta = at("mla_rope_a", 95, [P, MH, ROPE])
    tb = at("mla_rope_b", 96, [P, MH, ROPE])
    kd = at("ret_kd", 97, [P, 2, RH, RD])
    on = at("ret_on", 99, [P, RH, RD])
    ident = cst[:, C_ID:C_ID + P]
    HD = 4 * MQ

    loaded = k.sem("loaded2")
    weights_ready = k.sem("weights_ready2")
    lat_t = k.sem("lat_t")
    qk_t = k.sem("qk_t")
    v_sum = k.sem("v_sum")
    q_sum = k.sem("q_sum")
    sc_sum = k.sem("sc_sum")
    kv_sum = k.sem("kv_sum")
    out_sum = k.sem("out_sum")
    kn_sum = k.sem("kn_sum")
    q_t = k.sem("q_t")
    lat_copied = k.sem("lat_copied")
    qk_copied = k.sem("qk_copied")
    v_copied = k.sem("v_copied")
    qn_copied = k.sem("qn_copied")
    kn_copied = k.sem("kn_copied")
    qT_copied = k.sem("qT_copied")
    kr_copied = k.sem("kr_copied")
    qd_made = k.sem("qd_made")
    sc_decayed = k.sem("sc_decayed")
    q_rotated = k.sem("q_rotated")
    var_ready = k.sem("var_ready2")
    rstd_ready = k.sem("rstd_ready2")
    out_taken = k.sem("out_taken")
    state_made = k.sem("state_made")
    kd_made = k.sem("kd_made")
    dve_chain = k.sem("chain2")
    pool_chain = k.sem("pool_chain2")
    with nc.psum_tensor("banks2", [P, 8, 512], f32) as ps, \
            nc.Block() as block:

        @block.sync
        def _(sp):
            sp.dma_start(gq[:], A["q_norm_g"]).then_inc(loaded, 16)
            sp.dma_start(gkv[:], A["kv_norm_g"]).then_inc(loaded, 16)
            sp.dma_start(sgb[:], A["sgu_bT"]).then_inc(loaded, 16)
            sp.dma_start(wuq[:], A["w_uq"].rearrange("(k p) n -> p k n", p=P)).then_inc(loaded, 16)
            sp.dma_start(wukv[:], A["w_ukv"]).then_inc(loaded, 16)
            sp.dma_start(wsg[:], A["sgu_wT"]).then_inc(loaded, 16)

        @block.tensor
        def _(pe):
            def latents_T(t):
                if t:
                    pe.wait_ge(kr_copied, t)
                pe.transpose(ps[:, 0, 0:P], k.cq[:, t, 0:P], ident)
                pe.transpose(ps[:, 0, P:2 * P], k.cq[:, t, P:2 * P], ident)
                pe.transpose(ps[:, 0, 2 * P:3 * P], k.ckv[:, t, :], ident)
                pe.transpose(ps[0:ROPE, 0, 3 * P:4 * P], k.kr[:, t, :], ident).then_inc(lat_t, 1)

            def ret_T(t):
                if t:
                    pe.wait_ge(qk_copied, t)
                for j in range(4):
                    last = pe.transpose(ps[:, 1, j * P:(j + 1) * P], k.qk[:, t, j * P:(j + 1) * P], ident)
                last.then_inc(qk_t, 1)

            latents_T(0)
            ret_T(0)
            for t in range(NT):
                b = t % 2
                if t == 0:
                    pe.wait_ge(weights_ready, 4)
                pe.wait_ge(lat_copied, t + 1)
                if t:
                    pe.wait_ge(v_copied, t)
                pe.matmul(ps[:, 2, :], lat[:, b, QR:QR + KVR], wukv[:, MW:2 * MW], start=True, stop=True).then_inc(v_sum, 1)
                if t:
                    pe.wait_ge(qT_copied, 2 * t)
                for j in range(2):
                    for s in range(QR // P):
                        last = pe.matmul(ps[:, 3 + j, 0:HD], lat[:, b, s * P:(s + 1) * P],
                                         wuq[:, s, j * HD:(j + 1) * HD], start=(s == 0), stop=(s == QR // P - 1))
                last.then_inc(q_sum, 1)
                pe.wait_ge(qk_copied, t + 1)
                if t:
                    pe.wait_ge(kn_copied, 2 * t)
                    pe.wait_ge(state_made, t)
                for h in (0, 2, 1, 3):
                    r = slice(RD * (h % 2), RD * (h % 2) + RD)
                    q, kk = (qkt[r, b, (j + h // 2) * P:(j + h // 2 + 1) * P] for j in (0, 2))
                    o = ps[:, 5 + h % 2, (h % 2) * 2 * P + (h // 2) * P:(h % 2) * 2 * P + (h // 2 + 1) * P]
                    last = pe.matmul(o, kk, q, start=True, stop=True)
                last.then_inc(sc_sum, 1)
                if t:
                    pe.wait_ge(out_taken, t)
                for g in range(SG):
                    pe.matmul(ps[:, 7, RW + g * SD:RW + (g + 1) * SD], wsg[:, g, :],
                              k.sv[:, t, g * SD:(g + 1) * SD], start=True, stop=True)
                pe.wait_ge(sc_decayed, t + 1)
                pe.wait_ge(qd_made, t + 1)
                for j in range(2):
                    pe.matmul(ps[:, 7, j * P:(j + 1) * P], qdt[:, j * P:(j + 1) * P], state[:, j, :], start=True, stop=False)
                    for h in (2 * j, 2 * j + 1):
                        last = pe.matmul(ps[:, 7, h * RD:(h + 1) * RD], sc[:, h, :], k.rv[:, t, h * RD:(h + 1) * RD],
                                         start=False, stop=(h == 2 * j + 1))
                last.then_inc(out_sum, 1)
                pe.wait_ge(kd_made, t + 1)
                for j in range(2):
                    last = pe.matmul(ps[:, 6, j * P:(j + 1) * P],
                                     kd[:, b, 2 * j:2 * j + 2, :].rearrange("p h d -> p (h d)"),
                                     k.rv[:, t, j * P:(j + 1) * P], start=True, stop=True)
                last.then_inc(kv_sum, 1)
                if t + 1 < NT:
                    latents_T(t + 1)
                    ret_T(t + 1)
                for j in range(4):
                    last = pe.matmul(ps[:, 5, j * P:(j + 1) * P], wukv[:, j * P:(j + 1) * P],
                                     lat[:, b, QR:QR + KVR], start=True, stop=True)
                last.then_inc(kn_sum, 1)
                pe.wait_ge(q_rotated, t + 1)
                for h in range(MH):
                    last = pe.transpose(ps[0:MQ, 3 + h // 4, (h % 4) * P:(h % 4 + 1) * P], qtok[:, b, h, :], ident)
                last.then_inc(q_t, 1)

        @block.scalar
        def _(act):
            def copy_latents(t):
                act.wait_ge(lat_t, t + 1)
                act.activation(lat[:, t % 2, :], ps[:, 0, 0:QR + KVR], ACT.Copy).then_inc(lat_copied, 1)
                act.wait_ge(qk_t, t + 1)
                if t >= 2:
                    act.wait_ge(qd_made, t - 1)
                act.activation(qkt[:, t % 2, :], ps[:, 1, :], ACT.Copy).then_inc(qk_copied, 1)

            copy_latents(0)
            for t in range(NT):
                tok = slice(t * P, (t + 1) * P)
                act.wait_ge(v_sum, t + 1)
                act.activation(k.v[:, t, :], ps[:, 2, :], ACT.Copy).then_inc(v_copied, 1)
                act.wait_ge(q_sum, t + 1)
                act.activation(qtok[:, t % 2, :, 0:NOPE].rearrange("p (j h) d -> p j h d", j=2),
                               ps[:, 3:5, 0:HD].rearrange("p j (h d) -> p j h d", d=MQ)[:, :, :, 0:NOPE], ACT.Copy)\
                   .then_inc(qn_copied, 1)
                act.wait_ge(kn_sum, t + 1)
                for j in range(2):
                    act.activation(k.kT[0:NOPE, j:MH:2, tok],
                                   ps[NOPE * j:NOPE * (j + 1), 5, :].rearrange("p (h t) -> p h t", t=P), ACT.Copy)\
                       .then_inc(kn_copied, 1)
                if t + 1 < NT:
                    copy_latents(t + 1)
                act.wait_ge(q_t, t + 1)
                for j in range(2):
                    act.activation(k.qT[0:MQ, 4 * j:4 * j + 4, tok],
                                   ps[0:MQ, 3 + j, :].rearrange("p (h t) -> p h t", t=P), ACT.Copy, scale=MLA_SCALE)\
                       .then_inc(qT_copied, 1)

        @block.vector
        def _(dve):
            chain = [0]

            def link(ins):
                chain[0] += 1
                ins.then_inc(dve_chain, 1)
                dve.wait_ge(dve_chain, chain[0])

            dve.memset(state[:], 0.0).then_inc(weights_ready, 1)
            dve.wait_ge(loaded, 96)
            for s in range(2):
                last = dve.tensor_scalar(wuq[:, s, :], wuq[:, s, :], gq[:, s:s + 1], None, ALU.mult)
            last.then_inc(weights_ready, 1)
            dve.tensor_scalar(wukv[:], wukv[:], gkv[:, 0:1], None, ALU.mult).then_inc(weights_ready, 1)
            dve.tensor_tensor(wsg[:], wsg[:], over(cst[:, None, C_TRI:C_TRI + P], [P, SG, P]), ALU.mult)\
               .then_inc(weights_ready, 1)
            for t in range(NT):
                b = t % 2
                tok = slice(t * P, (t + 1) * P)
                dve.wait_ge(lat_copied, t + 1)
                dve.tensor_copy(k.kT[NOPE:MQ, :, tok], over(ps[0:ROPE, 0:1, 3 * P:4 * P], [ROPE, MH, P]))\
                   .then_inc(kr_copied, 1)
                dve.wait_ge(qk_copied, t + 1)
                if t:
                    dve.wait_ge(out_sum, t)
                dve.tensor_tensor(qdt[:], qkt[:, b, 0:2 * P], cst[:, C_QDEC:C_QDEC + 2 * P], ALU.mult).then_inc(qd_made, 1)
                dve.wait_ge(sc_sum, t + 1)
                decay = cst[:, C_DEC:C_DEC + RH * P].rearrange("p (h n) -> p h n", n=P)
                for j in range(2):
                    last = dve.tensor_tensor(sc[:, j:RH:2, :], ps[:, 5 + j, 2 * P * j:2 * P * (j + 1)].rearrange("p (h n) -> p h n", n=P),
                                             decay[:, j:RH:2, :], ALU.mult)
                last.then_inc(sc_decayed, 1)
                dve.wait_ge(qn_copied, t + 1)
                x = ps[:, 3:5, 0:HD].rearrange("p j (h d) -> p j h d", d=MQ)[:, :, :, NOPE:MQ]
                for j in range(2):
                    cb, sb_ = (over(z[:, t:t + 1, 32:64], [P, 4, ROPE]) for z in (k.cos, k.sin))
                    dve.tensor_tensor(ta[:, 4 * j:4 * j + 4, :], x[:, j], cb, ALU.mult)
                    last = dve.tensor_tensor(tb[:, 4 * j:4 * j + 4, :], x[:, j], sb_, ALU.mult)
                link(last)
                if t >= 2:
                    dve.wait_ge(q_t, t - 1)
                dve.tensor_tensor(qtok[:, b, :, NOPE:NOPE + 16], ta[:, :, 0:16], tb[:, :, 16:32], ALU.subtract)
                dve.tensor_tensor(qtok[:, b, :, NOPE + 16:MQ], tb[:, :, 0:16], ta[:, :, 16:32], ALU.add).then_inc(q_rotated, 1)
                dve.wait_ge(out_sum, t + 1)
                for h in range(RH):
                    last = dve.bn_stats(st4[:, h, :], ps[:, 7, h * RD:(h + 1) * RD])
                link(last)
                for h in range(RH):
                    last = dve.bn_aggr(mv4[:, h, :], st4[:, h, :])
                last.then_inc(var_ready, 1)
                for g in range(SG):
                    dve.scalar_tensor_tensor(k.mixA[:, t, RW + g * SD:RW + (g + 1) * SD], ps[:, 7, RW + g * SD:RW + (g + 1) * SD],
                                             sgb[:, g:g + 1], k.su[:, t, g * SD:(g + 1) * SD], ALU.add, ALU.mult)
                dve.wait_ge(kv_sum, t + 1)
                for h in range(RH):
                    r = slice(RD * (h % 2), RD * (h % 2) + RD)
                    blk = ps[r, 6, (h // 2) * P + RD * (h % 2):(h // 2) * P + RD * (h % 2) + RD]
                    st = state[r, h // 2, r]
                    last = dve.scalar_tensor_tensor(st, st, cst[r, C_ST + h // 2:C_ST + h // 2 + 1], blk, ALU.mult, ALU.add)
                last.then_inc(state_made, 1)
                dve.wait_ge(rstd_ready, t + 1)
                for h in range(RH):
                    last = dve.tensor_scalar(on[:, h, :], ps[:, 7, h * RD:(h + 1) * RD], mv4[:, h, 0:1], rs4[:, h:h + 1],
                                             ALU.subtract, ALU.mult)
                last.then_inc(out_taken, 1)
                dve.wait_ge(out_taken, t + 1)
                link(dve.scalar_tensor_tensor(k.mixA[:, t, 0:RW], on[:].rearrange("p h d -> p (h d)"), 0.5, k.sg[:, t, :],
                                              ALU.mult, ALU.mult))

        @block.gpsimd
        def _(pool):
            chain = [0]

            def link(ins):
                chain[0] += 1
                ins.then_inc(pool_chain, 1)
                pool.wait_ge(pool_chain, chain[0])

            link(pool.memset(half4[:], -0.5))
            for t in range(NT):
                if t >= 2:
                    pool.wait_ge(kv_sum, t - 1)
                pool.tensor_tensor(kd[:, t % 2].rearrange("p h d -> p (h d)"), k.qk[:, t, RW:2 * RW],
                                   cst[:, C_INNER:C_INNER + RW], ALU.mult).then_inc(kd_made, 1)
                pool.wait_ge(var_ready, t + 1)
                link(pool.tensor_scalar(ve4[:, :, None], mv4[:, :, 1:2], EPS, None, ALU.add))
                if t:
                    pool.wait_ge(out_taken, t)
                pool.tensor_tensor(rs4[:], ve4[:], half4[:], ALU.pow).then_inc(rstd_ready, 1)


def attend(nc, k):
    at, A, cst = k.at, k.dram, k.cst
    prob = at("prob", 12, [P, 2, S])
    probT = at("prob_T", 20, [P, 2, S])
    nmx = at("neg_max", 28, [P, 2])
    rsum = at("row_sum", 28.0625, [P, NT, MH])
    rinv = at("row_inv", 28.5, [P, NT, MH])
    ident = cst[:, C_ID:C_ID + P]
    units = [(i, h) for i in range(NT) for h in range(MH)]

    scored = k.sem("scored")
    max_ready = k.sem("max_ready")
    exps = k.sem("exps")
    p_t = k.sem("p_t")
    pT_copied = k.sem("pT_copied")
    pT_copied_act = k.sem("pT_copied_act")
    pv_done = k.sem("pv_done")
    o_taken = k.sem("o_taken")
    dve_chain = k.sem("chain3")
    with nc.psum_tensor("s_ps", [P, 2, 2, 512], f32) as sps, \
            nc.psum_tensor("t_ps", [P, 2, 512], f32) as tps, \
            nc.psum_tensor("o_ps", [P, 2, 512], f32) as ops, \
            nc.Block() as block:

        @block.sync
        def _(sp):
            for s in range(KD):
                sp.dma_start(k.w_out_raw[:, s, :], A["w_out"][s * P:(s + 1) * P, :]).then_inc(k.w_out_loaded, 16)

        def halves(i):
            n = i + 1
            return [(0, min(n, 4))] + ([(4, n)] if n > 4 else [])

        second = [0]
        for i, h in units:
            second.append(second[-1] + (i >= 4))

        @block.tensor
        def _(pe):
            def scores(u):
                i, h = units[u]
                if u >= 2:
                    pe.wait_ge(exps, u - 1)
                q = k.qT[0:MQ, h, i * P:(i + 1) * P]
                for j, (a, z) in enumerate(halves(i)):
                    last = pe.matmul(sps[:, u % 2, j, 0:(z - a) * P], q, k.kT[0:MQ, h, a * P:z * P], start=True, stop=True)
                last.then_inc(scored, 1)

            def turn(u):
                i, h = units[u]
                pe.wait_ge(exps, u + 1)
                for j, (a, z) in enumerate(halves(i)):
                    if j == 0 and u:
                        pe.wait_ge(pT_copied, u)
                    if j == 1 and second[u]:
                        pe.wait_ge(pT_copied_act, second[u])
                    for m in range(a, z):
                        last = pe.transpose(tps[:, j, (m - a) * P:(m - a + 1) * P], prob[:, u % 2, m * P:(m + 1) * P], ident)
                    last.then_inc(p_t, 1)

            def values(u):
                i, h = units[u]
                pe.wait_ge(pT_copied, u + 1)
                if i >= 4:
                    pe.wait_ge(pT_copied_act, second[u + 1])
                if h == 0 and i >= 2:
                    pe.wait_ge(o_taken, i - 1)
                for m in range(i + 1):
                    last = pe.matmul(ops[:, i % 2, h * MV:(h + 1) * MV], probT[:, u % 2, m * P:(m + 1) * P],
                                     k.v[:, m, h * MV:(h + 1) * MV], start=(m == 0), stop=(m == i))
                last.then_inc(pv_done, 1)

            n = len(units)
            for u in range(n + 2):
                if u < n:
                    scores(u)
                if 0 <= u - 2:
                    values(u - 2)
                if 0 <= u - 1 < n:
                    turn(u - 1)

        @block.scalar
        def _(act):
            for u in range(len(units) + 1):
                if u < len(units):
                    i, h = units[u]
                    act.wait_ge(max_ready, u + 1)
                    if u >= 2:
                        act.wait_ge(p_t, u - 1 + second[u - 1])
                    src = sps[:, u % 2].rearrange("p j n -> p (j n)")
                    act.activation(prob[:, u % 2, 0:(i + 1) * P], src[:, 0:(i + 1) * P], ACT.Exp,
                                   bias=nmx[:, u % 2:u % 2 + 1], accum_out=rsum[:, i, h:h + 1]).then_inc(exps, 1)
                if u >= 1 and units[u - 1][0] >= 4:
                    v = u - 1
                    i = units[v][0]
                    act.wait_ge(p_t, v + 1 + second[v + 1])
                    if v >= 2:
                        act.wait_ge(pv_done, v - 1)
                    act.activation(probT[:, v % 2, 4 * P:(i + 1) * P], tps[:, 1, 0:(i - 3) * P], ACT.Copy)\
                       .then_inc(pT_copied_act, 1)

        @block.vector
        def _(dve):
            chain = [0]

            def link(ins):
                chain[0] += 1
                ins.then_inc(dve_chain, 1)
                dve.wait_ge(dve_chain, chain[0])

            def take(i):
                dve.wait_ge(pv_done, (i + 1) * MH)
                link(dve.reciprocal(rinv[:, i, :], rsum[:, i, :]))
                dve.tensor_tensor(k.mixB[:, i, :].rearrange("p (h d) -> p h d", d=MV),
                                  ops[:, i % 2, :].rearrange("p (h d) -> p h d", d=MV),
                                  over(rinv[:, i, :, None], [P, MH, MV]), ALU.mult).then_inc(o_taken, 1)

            for u in range(len(units) + 1):
                if u < len(units):
                    i, h = units[u]
                    dve.wait_ge(scored, u + 1)
                    s = sps[:, u % 2].rearrange("p j n -> p (j n)")
                    d = s[:, i * P:(i + 1) * P]
                    link(dve.tensor_tensor(d, d, cst[:, C_MASK:C_MASK + P], ALU.add))
                    if u >= 2:
                        dve.wait_ge(exps, u - 1)
                    dve.tensor_reduce(nmx[:, u % 2:u % 2 + 1], s[:, 0:(i + 1) * P], AX.X, ALU.max, negate=True).then_inc(max_ready, 1)
                if u >= 1:
                    v = u - 1
                    i = units[v][0]
                    n = min(i + 1, 4) * P
                    dve.wait_ge(p_t, v + 1 + second[v])
                    if v >= 2:
                        dve.wait_ge(pv_done, v - 1)
                    dve.tensor_copy(probT[:, v % 2, 0:n], tps[:, 0, 0:n]).then_inc(pT_copied, 1)
                    if v >= MH and v % MH == 1:
                        take(v // MH - 1)
            take(NT - 1)



def mix_out(nc, k):
    at, A, cst = k.at, k.dram, k.cst
    mhi = at("mixT_hi", 12, [P, 2, KD, P], f32r)
    mlo = at("mixT_lo", 20, [P, 2, KD, P], f32r)
    wraw = k.w_out_raw
    whi = at("wo_hi", 105, [P, KD, D], f32r)
    wlo = at("wo_lo", 137, [P, KD, D], f32r)
    g = at("ln1_g", 62, [P, D])
    b = at("ln1_b", 66, [P, D])
    st = at("ln1_st", 201, [P, 2, 6])
    mv = at("ln1_mv", 201.125, [P, 2, 2])
    rs = at("ln1_rs", 201.25, [P, 2])
    half = at("ln1_half", 201.375, [P, 1])
    ident = cst[:, C_ID:C_ID + P]
    x1 = k.x1
    loaded = k.sem("x_gains_loaded")
    w_hi, w_lo = k.sem("wo_hi_done"), k.sem("wo_lo_done")
    mix_t, m_hi, m_lo = k.sem("mix_t"), k.sem("mix_hi"), k.sem("mix_lo")
    summed, taken = k.sem("mix_summed"), k.sem("mix_taken")
    var_ready, rstd_ready, normed = k.sem("ln1_var"), k.sem("ln1_rstd"), k.sem("ln1_normed")
    dve_chain, pool_chain = k.sem("chain4"), k.sem("pool_chain4")
    with nc.psum_tensor("mixT_ps", [P, 2, 2, 512], f32) as tps, \
            nc.psum_tensor("mix_acc", [P, 2, 2, 512], f32) as acc, \
            nc.Block() as block:

        @block.sync
        def _(sp):
            for t in range(NT):
                sp.dma_start(x1[:, t, :], A["x"][t * P:(t + 1) * P, :]).then_inc(loaded, 16)
            sp.dma_start(g[:], over(A["ln_mix_g"], [P, D])).then_inc(loaded, 16)
            sp.dma_start(b[:], over(A["ln_mix_b"], [P, D])).then_inc(loaded, 16)
            sp.wait_ge(w_lo, KD)
            for s in range(KD):
                sp.dma_start(k.wk[:, s, :], A["xa_wk"][s * P:(s + 1) * P, :]).then_inc(k.kv_loaded, 16)
                sp.dma_start(k.wv[:, s, :], A["xa_wv"][s * P:(s + 1) * P, :]).then_inc(k.kv_loaded, 16)

        @block.tensor
        def _(pe):
            def turn(t):
                if t >= 2:
                    pe.wait_ge(m_lo, t - 1)
                for j in range(KD):
                    src = k.mixA if j < 4 else k.mixB
                    last = pe.transpose(tps[:, t % 2, j // 4, (j % 4) * P:(j % 4 + 1) * P],
                                        src[:, t, (j % 4) * P:(j % 4 + 1) * P], ident)
                last.then_inc(mix_t, 1)

            turn(0)
            for t in range(NT):
                if t + 1 < NT:
                    turn(t + 1)
                pe.wait_ge(m_lo, t + 1)
                if t >= 2:
                    pe.wait_ge(taken, t - 1)
                for s in range(KD):
                    if t == 0:
                        pe.wait_ge(w_lo, s + 1)
                    hi, lo = mhi[:, t % 2, s, :], mlo[:, t % 2, s, :]
                    for j in range(2):
                        o, c = acc[:, t % 2, j, :], slice(512 * j, 512 * j + 512)
                        pe.matmul(o, hi, whi[:, s, c], start=(s == 0), stop=False)
                        pe.matmul(o, hi, wlo[:, s, c], start=False, stop=False)
                        last = pe.matmul(o, lo, whi[:, s, c], start=False, stop=(s == KD - 1))
                last.then_inc(summed, 1)

        @block.scalar
        def _(act):
            act.wait_ge(k.w_out_loaded, 16 * KD)
            for s in range(KD):
                act.activation(whi[:, s, :], wraw[:, s, :], ACT.Copy).then_inc(w_hi, 1)
            for t in range(NT):
                act.wait_ge(mix_t, t + 1)
                if t >= 2:
                    act.wait_ge(summed, t - 1)
                act.activation(mhi[:, t % 2].rearrange("p s c -> p (s c)"), tps[:, t % 2].rearrange("p j c -> p (j c)"), ACT.Copy)\
                   .then_inc(m_hi, 1)

        @block.vector
        def _(dve):
            chain = [0]

            def link(ins):
                chain[0] += 1
                ins.then_inc(dve_chain, 1)
                dve.wait_ge(dve_chain, chain[0])

            def rest(t):
                dve.wait_ge(m_hi, t + 1)
                dve.tensor_tensor(mlo[:, t % 2].rearrange("p s c -> p (s c)"), tps[:, t % 2].rearrange("p j c -> p (j c)"),
                                  mhi[:, t % 2].rearrange("p s c -> p (s c)").bitcast(f32), ALU.subtract).then_inc(m_lo, 1)

            def finish(t):
                dve.wait_ge(rstd_ready, t + 1)
                dve.tensor_scalar(x1[:, t, :], x1[:, t, :], mv[:, t % 2, 0:1], rs[:, t % 2:t % 2 + 1], ALU.subtract, ALU.mult)\
                   .then_inc(normed, 1)

            for s in range(KD):
                if s == 1:
                    rest(0)
                dve.wait_ge(w_hi, s + 1)
                dve.tensor_tensor(wlo[:, s, :], wraw[:, s, :], whi[:, s, :].bitcast(f32), ALU.subtract).then_inc(w_lo, 1)
            dve.wait_ge(loaded, 160)
            for t in range(NT):
                if t + 1 < NT:
                    rest(t + 1)
                dve.wait_ge(summed, t + 1)
                dve.scalar_tensor_tensor(x1[:, t, :], x1[:, t, :], ALPHA, acc[:, t % 2].rearrange("p j c -> p (j c)"), ALU.mult, ALU.add)\
                   .then_inc(taken, 1)
                dve.wait_ge(taken, t + 1)
                for j in range(2):
                    last = dve.bn_stats(st[:, j, :], x1[:, t, 512 * j:512 * j + 512])
                link(last)
                dve.bn_aggr(mv[:, t % 2, :], st[:].rearrange("p j c -> p (j c)")).then_inc(var_ready, 1)
                if t:
                    finish(t - 1)
            finish(NT - 1)

        @block.gpsimd
        def _(pool):
            chain = [0]

            def link(ins):
                chain[0] += 1
                ins.then_inc(pool_chain, 1)
                pool.wait_ge(pool_chain, chain[0])

            def gains(t):
                pool.wait_ge(normed, t + 1)
                link(pool.tensor_tensor(x1[:, t, :], x1[:, t, :], g[:], ALU.mult))
                link(pool.tensor_tensor(x1[:, t, :], x1[:, t, :], b[:], ALU.add))

            link(pool.memset(half[:], -0.5))
            pool.wait_ge(loaded, 160)
            for t in range(NT):
                pool.wait_ge(var_ready, t + 1)
                link(pool.tensor_scalar(mv[:, t % 2, 1:2], mv[:, t % 2, 1:2], EPS, None, ALU.add))
                pool.tensor_tensor(rs[:, t % 2:t % 2 + 1], mv[:, t % 2, 1:2], half[:], ALU.pow).then_inc(rstd_ready, 1)
                if t:
                    gains(t - 1)
            gains(NT - 1)


def memory_keys(nc, k):
    at, A = k.at, k.dram
    memT = at("memT", 62, [P, KD, MEM])
    rawq = at("wq_raw", 70, [P, KD, XW])
    rawo = at("xwo_raw", 86, [P, XH, D])
    q_hi, q_lo = k.sem("wq_hi_done"), k.sem("wq_lo_done")
    mem_loaded, q_loaded, o_loaded = k.sem("mem_loaded"), k.sem("wq_loaded"), k.sem("xwo_loaded")
    kv_sum, kv_taken = k.sem("xkv_sum"), k.sem("xkv_taken")
    with nc.psum_tensor("xkv_ps", [P, 4, 512], f32) as ps, nc.Block() as block:
        @block.sync
        def _(sp):
            sp.dma_start(memT[:], A["memT"].rearrange("(s p) n -> p s n", p=P)).then_inc(mem_loaded, 16)
            sp.dma_start(rawq[:], A["xa_wq"].rearrange("(s p) n -> p s n", p=P)).then_inc(q_loaded, 16)
            sp.dma_start(rawo[:], A["xa_wo"].rearrange("(s p) n -> p s n", p=P)).then_inc(o_loaded, 16)

        @block.tensor
        def _(pe):
            pe.wait_ge(mem_loaded, 16)
            pe.wait_ge(k.kv_loaded, 16 * 2 * KD)
            for u in range(6):
                if u >= 4:
                    pe.wait_ge(kv_taken, u - 3)
                for s in range(KD):
                    if u < XH:
                        o, l, r = ps[:, u % 4, 0:MEM], k.wk[:, s, u * XD:(u + 1) * XD], memT[:, s, :]
                    else:
                        o, l, r = ps[:, u % 4, :], memT[:, s, (u - XH) * P:(u - XH + 1) * P], k.wv[:, s, :]
                    last = pe.matmul(o, l, r, start=(s == 0), stop=(s == KD - 1))
                last.then_inc(kv_sum, 1)

        @block.scalar
        def _(act):
            act.wait_ge(q_loaded, 16)
            for s in range(KD):
                act.activation(k.wq_hi[:, s, :], rawq[:, s, :], ACT.Copy).then_inc(q_hi, 1)
            act.wait_ge(o_loaded, 16)
            for s in range(XH):
                act.activation(k.xwo_hi[:, s, :], rawo[:, s, :], ACT.Copy).then_inc(q_hi, 1)

        @block.vector
        def _(dve):
            def take(u):
                dve.wait_ge(kv_sum, u + 1)
                if u < XH:
                    dve.tensor_copy(k.xkT[:, u, :], ps[:, u % 4, 0:MEM]).then_inc(kv_taken, 1)
                else:
                    dve.tensor_copy(k.xv[:, u - XH, :], ps[:, u % 4, :]).then_inc(kv_taken, 1)

            for s in range(KD):
                dve.wait_ge(q_hi, s + 1)
                dve.tensor_tensor(k.wq_lo[:, s, :], rawq[:, s, :], k.wq_hi[:, s, :].bitcast(f32), ALU.subtract)
            for u in range(2):
                take(u)
            for s in range(XH):
                dve.wait_ge(q_hi, KD + s + 1)
                dve.tensor_tensor(k.xwo_lo[:, s, :], rawo[:, s, :], k.xwo_hi[:, s, :].bitcast(f32), ALU.subtract)
            for u in range(2, 6):
                take(u)


def cross_attend(nc, k):
    at, A, cst = k.at, k.dram, k.cst
    g = at("ln2_g", 30, [P, D])
    b = at("ln2_b", 34, [P, D])
    xhi = at("x1T_hi", 38, [P, KD, P], f32r)
    xlo = at("x1T_lo", 42, [P, KD, P], f32r)
    qtok = at("xq_tok", 54, [P, XW])
    qT = at("xqT", 56, [P, XH, P])
    prob = at("xprob", 58, [P, XH, MEM])
    probT = at("xprobT", 62, [P, XH * 2, P])
    ohi = at("xoT_hi", 66, [P, XH, P], f32r)
    olo = at("xoT_lo", 68, [P, XH, P], f32r)
    st = at("ln2_st", 201, [P, 2, 6])
    mv = at("ln2_mv", 201.125, [P, 2, 2])
    rs = at("ln2_rs", 201.25, [P, 2])
    half = at("ln2_half", 201.375, [P, 1])
    nmx = at("xneg_max", 201.5, [P, XH])
    rsum = at("xrow_sum", 201.5625, [P, XH])
    rinv = at("xrow_inv", 201.625, [P, XH])
    ident = cst[:, C_ID:C_ID + P]
    x1 = k.x1
    loaded = k.sem("gains6_loaded")
    x_t, x_hi, x_lo = k.sem("x1_t"), k.sem("x1_hi"), k.sem("x1_lo")
    q_sum, q_taken, q_t, qT_taken = k.sem("xq_sum"), k.sem("xq_taken"), k.sem("xq_t"), k.sem("xqT_taken")
    scored, maxed, exps, scaled = k.sem("xscored"), k.sem("xmaxed"), k.sem("xexps"), k.sem("xscaled")
    p_t, pT_taken = k.sem("xp_t"), k.sem("xpT_taken")
    o_sum, o_hi, o_lo = k.sem("xo_sum"), k.sem("xo_hi"), k.sem("xo_lo")
    summed, taken = k.sem("xsummed"), k.sem("xtaken")
    var_ready, rstd_ready, normed = k.sem("ln2_var"), k.sem("ln2_rstd"), k.sem("ln2_normed")
    x2_made = k.sem("x2_made")
    dve_chain, pool_chain, stored = k.sem("chain6"), k.sem("pool_chain6"), k.x2_stored
    flat = "p j c -> p (j c)"
    with nc.psum_tensor("x_tps", [P, 2, 512], f32) as tps, nc.psum_tensor("x_qps", [P, 512], f32) as qps, \
            nc.psum_tensor("x_sps", [P, 2, 512], f32) as sps, nc.psum_tensor("x_ops", [P, 512], f32) as ops, \
            nc.psum_tensor("x_acc", [P, 2, 512], f32) as acc, nc.Block() as block:

        @block.sync
        def _(sp):
            sp.dma_start(g[:], over(A["ln_xa_g"], [P, D])).then_inc(loaded, 16)
            sp.dma_start(b[:], over(A["ln_xa_b"], [P, D])).then_inc(loaded, 16)
            for t in range(NT):
                sp.wait_ge(x2_made, t + 1)
                sp.dma_start(k.x2_dram[t * P:(t + 1) * P, 0:D], x1[:, t, :]).then_inc(stored, 16)

        @block.tensor
        def _(pe):
            def turn(t):
                if t >= 2:
                    pe.wait_ge(pT_taken, t - 1)
                for j in range(KD):
                    last = pe.transpose(tps[:, j // 4, (j % 4) * P:(j % 4 + 1) * P], x1[:, t, j * P:(j + 1) * P], ident)
                last.then_inc(x_t, 1)

            def queries(t):
                pe.wait_ge(x_lo, t + 1)
                if t:
                    pe.wait_ge(qT_taken, t)
                for s in range(KD):
                    pe.matmul(qps[:], xhi[:, s, :], k.wq_hi[:, s, :], start=(s == 0), stop=False)
                    pe.matmul(qps[:], xhi[:, s, :], k.wq_lo[:, s, :], start=False, stop=False)
                    last = pe.matmul(qps[:], xlo[:, s, :], k.wq_hi[:, s, :], start=False, stop=(s == KD - 1))
                last.then_inc(q_sum, 1)

            def turn_queries(t):
                pe.wait_ge(q_taken, t + 1)
                for h in range(XH):
                    last = pe.transpose(qps[:, h * P:(h + 1) * P], qtok[:, h * P:(h + 1) * P], ident)
                last.then_inc(q_t, 1)

            def scores(t):
                pe.wait_ge(qT_taken, t + 1)
                if t:
                    pe.wait_ge(exps, XH * t)
                for h in range(XH):
                    last = pe.matmul(sps[:, h // 2, (h % 2) * MEM:(h % 2 + 1) * MEM], qT[:, h, :], k.xkT[:, h, :], start=True, stop=True)
                last.then_inc(scored, 1)

            def turn_probs(t):
                pe.wait_ge(scaled, t + 1)
                pe.wait_ge(x_lo, t + 2 if t + 1 < NT else NT)
                for j in range(2 * XH):
                    last = pe.transpose(tps[:, j // 4, (j % 4) * P:(j % 4 + 1) * P],
                                        prob[:, j // 2, (j % 2) * P:(j % 2 + 1) * P], ident)
                last.then_inc(p_t, 1)

            def values(t):
                pe.wait_ge(pT_taken, t + 1)
                if t:
                    pe.wait_ge(o_lo, t)
                for h in range(XH):
                    for m in range(2):
                        last = pe.matmul(ops[:, h * P:(h + 1) * P], k.xv[:, m, h * XD:(h + 1) * XD], probT[:, 2 * h + m, :],
                                         start=(m == 0), stop=(m == 1))
                last.then_inc(o_sum, 1)

            def outputs(t):
                pe.wait_ge(o_lo, t + 1)
                if t:
                    pe.wait_ge(taken, t)
                for s in range(XH):
                    for j in range(2):
                        o, c = acc[:, j, :], slice(512 * j, 512 * j + 512)
                        pe.matmul(o, ohi[:, s, :], k.xwo_hi[:, s, c], start=(s == 0), stop=False)
                        pe.matmul(o, ohi[:, s, :], k.xwo_lo[:, s, c], start=False, stop=False)
                        last = pe.matmul(o, olo[:, s, :], k.xwo_hi[:, s, c], start=False, stop=(s == XH - 1))
                last.then_inc(summed, 1)

            turn(0)
            for t in range(NT + 1):
                if t < NT:
                    queries(t)
                if t:
                    turn_probs(t - 1)
                if t < NT:
                    turn_queries(t)
                if t:
                    values(t - 1)
                if t < NT:
                    scores(t)
                if t + 1 < NT:
                    turn(t + 1)
                if t:
                    outputs(t - 1)

        @block.scalar
        def _(act):
            def x_high(t):
                act.wait_ge(x_t, t + 1)
                if t:
                    act.wait_ge(q_sum, t)
                act.activation(xhi[:].rearrange(flat), tps[:].rearrange(flat), ACT.Copy).then_inc(x_hi, 1)

            x_high(0)
            for t in range(NT + 1):
                if t < NT:
                    act.wait_ge(q_sum, t + 1)
                    act.activation(qtok[:], qps[:], ACT.Copy, scale=XA_SCALE).then_inc(q_taken, 1)
                if t:
                    act.wait_ge(p_t, t)
                    if t >= 2:
                        act.wait_ge(o_sum, t - 1)
                    act.activation(probT[:].rearrange(flat), tps[:].rearrange(flat), ACT.Copy).then_inc(pT_taken, 1)
                if t < NT:
                    act.wait_ge(q_t, t + 1)
                    act.activation(qT[:].rearrange(flat), qps[:], ACT.Copy).then_inc(qT_taken, 1)
                if t:
                    act.wait_ge(o_sum, t)
                    if t >= 2:
                        act.wait_ge(summed, t - 1)
                    act.activation(ohi[:].rearrange(flat), ops[:], ACT.Copy).then_inc(o_hi, 1)
                if t < NT:
                    act.wait_ge(maxed, t + 1)
                    if t:
                        act.wait_ge(p_t, t)
                    for h in range(XH):
                        act.activation(prob[:, h, :], sps[:, h // 2, (h % 2) * MEM:(h % 2 + 1) * MEM], ACT.Exp,
                                       bias=nmx[:, h:h + 1], accum_out=rsum[:, h:h + 1]).then_inc(exps, 1)
                if t + 1 < NT:
                    x_high(t + 1)

        @block.vector
        def _(dve):
            chain = [0]

            def link(ins):
                chain[0] += 1
                ins.then_inc(dve_chain, 1)
                dve.wait_ge(dve_chain, chain[0])

            def x_rest(t):
                dve.wait_ge(x_hi, t + 1)
                dve.tensor_tensor(xlo[:].rearrange(flat), tps[:].rearrange(flat), xhi[:].rearrange(flat).bitcast(f32), ALU.subtract)\
                   .then_inc(x_lo, 1)

            def residual(t):
                dve.wait_ge(summed, t + 1)
                dve.scalar_tensor_tensor(x1[:, t, :], x1[:, t, :], ALPHA, acc[:].rearrange(flat), ALU.mult, ALU.add).then_inc(taken, 1)
                dve.wait_ge(taken, t + 1)
                for j in range(2):
                    last = dve.bn_stats(st[:, j, :], x1[:, t, 512 * j:512 * j + 512])
                link(last)
                dve.bn_aggr(mv[:, t % 2, :], st[:].rearrange(flat)).then_inc(var_ready, 1)

            def norm(t):
                dve.wait_ge(rstd_ready, t + 1)
                dve.tensor_scalar(x1[:, t, :], x1[:, t, :], mv[:, t % 2, 0:1], rs[:, t % 2:t % 2 + 1], ALU.subtract, ALU.mult)\
                   .then_inc(normed, 1)

            x_rest(0)
            for t in range(NT + 1):
                if t:
                    dve.wait_ge(o_hi, t)
                    dve.tensor_tensor(olo[:].rearrange(flat), ops[:], ohi[:].rearrange(flat).bitcast(f32), ALU.subtract)\
                       .then_inc(o_lo, 1)
                if t < NT:
                    dve.wait_ge(scored, t + 1)
                    for j in range(2):
                        last = dve.tensor_reduce(nmx[:, 2 * j:2 * j + 2], sps[:, j, :].rearrange("p (h m) -> p h m", m=MEM), AX.X, ALU.max, negate=True)
                    last.then_inc(maxed, 1)
                if t + 1 < NT:
                    x_rest(t + 1)
                if t < NT:
                    dve.wait_ge(exps, XH * (t + 1))
                    link(dve.reciprocal(rinv[:], rsum[:]))
                    dve.tensor_tensor(prob[:], prob[:], over(rinv[:, :, None], [P, XH, MEM]), ALU.mult).then_inc(scaled, 1)
                if t >= 2:
                    norm(t - 2)
                if t:
                    residual(t - 1)
            norm(NT - 1)

        @block.gpsimd
        def _(pool):
            chain = [0]

            def link(ins):
                chain[0] += 1
                ins.then_inc(pool_chain, 1)
                pool.wait_ge(pool_chain, chain[0])

            def gains(t):
                pool.wait_ge(normed, t + 1)
                link(pool.tensor_tensor(x1[:, t, :], x1[:, t, :], g[:], ALU.mult))
                pool.tensor_tensor(x1[:, t, :], x1[:, t, :], b[:], ALU.add).then_inc(x2_made, 1)

            link(pool.memset(half[:], -0.5))
            pool.wait_ge(loaded, 32)
            for t in range(NT):
                pool.wait_ge(var_ready, t + 1)
                link(pool.tensor_scalar(mv[:, t % 2, 1:2], mv[:, t % 2, 1:2], EPS, None, ALU.add))
                pool.tensor_tensor(rs[:, t % 2:t % 2 + 1], mv[:, t % 2, 1:2], half[:], ALU.pow).then_inc(rstd_ready, 1)
                if t:
                    gains(t - 1)
            gains(NT - 1)



def route(nc, k):
    at, A, cst = k.at, k.dram, k.cst
    xT = at("x2T", 12, [P, 2, KD, P])
    rw = at("router_w", 20, [P, KD, NE])
    rb = at("router_bias", 20.5, [P, NE])
    ones = at("ones", 21, [P, P])
    score = at("score", 21.5, [P, NT, NE])
    bia = at("biased", 22, [P, NT, NE])
    beats = at("beats", 22.5, [P, EG, NT * NG, EG])
    rank = at("rank", 24.5, [P, NT * NG, EG])
    picked = at("picked", 25, [P, NT * NG, EG])
    gsum = at("group_sum", 25.5, [P, NT, NG])
    gbeats = at("group_beats", 25.75, [P, NG, NT, NG])
    sel = at("selected", 26.25, [P, NT, NE])
    gate = at("gate", 26.75, [P, NT, NE])
    den = at("gate_den", 27.25, [P, NT])
    fits = at("fits", 27.5, [P, NT, NE])
    key = at("slot_key", 28, [P, NT, NE])
    val = at("slot_val", 28.5, [P, NT, NE])
    tot = at("slot_tot", 29, [P, 2, NT])
    over_cap = at("over_cap", 29.25, [P, NT, NE])
    ovsum = at("over_sum", 29.75, [P, 1])
    tok_id = at("token_id", 30, [P, NT, 2], bf16)
    iota = at("slot_iota", 30.25, [P, CAP], bf16)
    onehot = at("onehot", 31, [P, 2, NT, CAP], bf16)
    base = at("expert_base", 37, [P, NE])
    tokf = at("slot_tokens_f", 37.125, [P, NE, 2])
    ident = cst[:, C_ID:C_ID + P]
    loaded = k.sem("router_loaded")
    x_t, xa_copied, xd_copied, logit = k.sem("x2_t"), k.sem("x2_act"), k.sem("x2_dve"), k.sem("logit")
    sig, selected, placed, keyed = k.sem("sigmoids"), k.sem("selected"), k.sem("placed"), k.sem("keyed")
    hot, listed, ov_made, ov_sum = k.sem("onehot_made"), k.sem("listed"), k.sem("over_made"), k.sem("over_summed")
    consts_made, chain_s, comb_made = k.sem("consts7"), k.sem("chain7"), k.sem("comb_made")
    q3 = lambda ap: ap.rearrange("p t (g e) -> p (t g) e", e=EG)
    with nc.psum_tensor("x2T_ps", [P, 2, 2, 512], f32) as tps, nc.psum_tensor("logit_ps", [P, 512], f32) as lps, \
            nc.psum_tensor("place_ps", [P, 512], f32) as pps, nc.psum_tensor("list_ps", [P, 512], f32) as sps, \
            nc.psum_tensor("over_ps", [P, 512], f32) as ops, nc.Block() as block:

        @block.sync
        def _(sp):
            sp.dma_start(rw[:], A["router_w"].rearrange("(s p) e -> p s e", p=P)).then_inc(loaded, 16)
            sp.dma_start(rb[:], over(A["router_bias"], [P, NE])).then_inc(loaded, 16)
            sp.wait_ge(comb_made, 1)
            sp.dma_start(k.x2_dram[:, D:D + NE].rearrange("(t p) e -> p t e", p=P), k.comb[:]).then_inc(k.x2_stored, 16)

        @block.tensor
        def _(pe):
            def turn(t):
                if t >= 2:
                    pe.wait_ge(xa_copied, t - 1)
                    pe.wait_ge(xd_copied, t - 1)
                for j in range(KD):
                    last = pe.transpose(tps[:, t % 2, j // 4, (j % 4) * P:(j % 4 + 1) * P], k.x1[:, t, j * P:(j + 1) * P], ident)
                last.then_inc(x_t, 1)

            turn(0)
            pe.wait_ge(loaded, 32)
            for t in range(NT):
                if t + 1 < NT:
                    turn(t + 1)
                pe.wait_ge(xa_copied, t + 1)
                pe.wait_ge(xd_copied, t + 1)
                for s in range(KD):
                    last = pe.matmul(lps[:, t * NE:(t + 1) * NE], xT[:, t % 2, s, :], rw[:, s, :], start=(s == 0), stop=(s == KD - 1))
                last.then_inc(logit, 1)
            pe.wait_ge(selected, 1)
            pe.wait_ge(consts_made, 4)
            pe.matmul(pps[:, 0:NT * NE], cst[:, C_TRI:C_TRI + P], sel[:].rearrange("p t e -> p (t e)"), start=True, stop=False)
            for t in range(NT - 1):
                n = NT - 1 - t
                last = pe.matmul(pps[:, (t + 1) * NE:NT * NE], ones[:], over(sel[:, t:t + 1, :], [P, n, NE]), start=False, stop=(n == 1))
            last.then_inc(placed, 1)
            for e in range(NE):
                pe.wait_ge(hot, e + 1)
                for b in range(2):
                    n = min(P, CAP - b * P)
                    for t in range(NT):
                        last = pe.matmul(sps[0:n, (2 * e + b) * 2:(2 * e + b) * 2 + 2], onehot[:, e % 2, t, b * P:b * P + n],
                                         tok_id[:, t, :], start=(t == 0), stop=(t == NT - 1))
                last.then_inc(listed, 1)
            pe.wait_ge(ov_made, 1)
            pe.matmul(ops[0:1, 0:1], ovsum[:], ones[:, 0:1], start=True, stop=True).then_inc(ov_sum, 1)

        @block.scalar
        def _(act):
            for t in range(NT):
                act.wait_ge(x_t, t + 1)
                if t >= 2:
                    act.wait_ge(logit, t - 1)
                act.activation(xT[:, t % 2, 0:4, :].rearrange("p s c -> p (s c)"), tps[:, t % 2, 0, :], ACT.Copy).then_inc(xa_copied, 1)
            act.wait_ge(logit, NT)
            act.activation(score[:].rearrange("p t e -> p (t e)"), lps[:, 0:NT * NE], ACT.Sigmoid).then_inc(sig, 1)

        @block.vector
        def _(dve):
            chain = [0]

            def link(ins):
                chain[0] += 1
                ins.then_inc(chain_s, 1)
                dve.wait_ge(chain_s, chain[0])

            dve.memset(beats[:], 0.0)
            dve.memset(gbeats[:], 0.0)
            link(dve.memset(tokf[:], 0.0))
            for t in range(NT):
                dve.wait_ge(x_t, t + 1)
                if t >= 2:
                    dve.wait_ge(logit, t - 1)
                dve.tensor_copy(xT[:, t % 2, 4:8, :].rearrange("p s c -> p (s c)"), tps[:, t % 2, 1, :]).then_inc(xd_copied, 1)
            dve.wait_ge(sig, 1)
            link(dve.tensor_tensor(bia[:], score[:], over(rb[:, None, :], [P, NT, NE]), ALU.add))

            def rank_of(out, b, v):
                n = v.shape[1]
                for j in range(4):
                    if j < 3:
                        dve.tensor_tensor(b[:, j, :, j + 1:4], over(v[:, :, j:j + 1], [P, n, 3 - j]), v[:, :, j + 1:4], ALU.is_ge)
                    if j:
                        dve.tensor_tensor(b[:, j, :, 0:j], over(v[:, :, j:j + 1], [P, n, j]), v[:, :, 0:j], ALU.is_gt)
                link(dve.memset(out, 0.0))
                for j in range(4):
                    link(dve.tensor_tensor(out, out, b[:, j], ALU.add))

            rank_of(rank[:], beats, q3(bia[:]))
            link(dve.tensor_scalar(rank[:], rank[:], 2.0, None, ALU.is_lt))
            link(dve.tensor_tensor(picked[:], rank[:], q3(bia[:]), ALU.mult))
            link(dve.tensor_reduce(gsum[:].rearrange("p t g -> p (t g)"), picked[:], AX.X, ALU.add))
            grank = picked[:, 0:NT, :]
            rank_of(grank, gbeats, gsum[:])
            link(dve.tensor_scalar(grank, grank, 1.0, None, ALU.is_lt))
            dve.tensor_tensor(q3(sel[:]), rank[:], over(picked[:, 0:NT, :].rearrange("p t g -> p (t g)")[:, :, None], [P, NT * NG, EG]),
                              ALU.mult).then_inc(selected, 1)
            dve.wait_ge(selected, 1)
            link(dve.tensor_tensor(gate[:], sel[:], score[:], ALU.mult))
            link(dve.tensor_reduce(den[:], gate[:], AX.X, ALU.add))
            link(dve.reciprocal(den[:], den[:]))
            dve.tensor_tensor(k.comb[:], gate[:], over(den[:, :, None], [P, NT, NE]), ALU.mult).then_inc(comb_made, 1)
            dve.wait_ge(placed, 1)
            place = pps[:, 0:NT * NE].rearrange("p (t e) -> p t e", e=NE)
            link(dve.tensor_tensor(key[:], place, sel[:], ALU.mult))
            link(dve.tensor_scalar(key[:], key[:], -1.0, None, ALU.add))
            dve.wait_ge(consts_made, 4)
            for e in range(NE):
                if e >= 2:
                    dve.wait_ge(listed, e - 1)
                for t in range(NT):
                    last = dve.tensor_scalar(onehot[:, e % 2, t, :], iota[:], key[:, t, e:e + 1], None, ALU.is_equal)
                last.then_inc(hot, 1)
            link(dve.tensor_scalar(fits[:], key[:], float(CAP) - 0.5, None, ALU.is_lt))
            link(dve.tensor_tensor(fits[:], fits[:], sel[:], ALU.mult))
            link(dve.tensor_tensor(over_cap[:], sel[:], fits[:], ALU.subtract))
            link(dve.tensor_tensor(k.comb_over[:], over_cap[:], k.comb[:], ALU.mult))
            dve.tensor_reduce(ovsum[:], over_cap[:], AX.XY, ALU.add).then_inc(ov_made, 1)
            link(dve.tensor_tensor(val[:], key[:], over(base[:, None, :], [P, NT, NE]), ALU.add))
            link(dve.tensor_tensor(val[:], val[:], fits[:], ALU.mult))
            dve.tensor_reduce(tot[:, 0, :], val[:], AX.X, ALU.max)
            link(dve.tensor_reduce(tot[:, 1, :], val[:], AX.X, ALU.add))
            dve.tensor_copy(k.y_row[:, 0, :], tot[:, 0, :])
            link(dve.tensor_tensor(k.y_row[:, 1, :], tot[:, 1, :], tot[:, 0, :], ALU.subtract))
            dve.wait_ge(listed, NE)
            dve.tensor_reduce(tokf[:, :, 0:1], sps[:, 0:4 * NE].rearrange("p (e b c) -> p e b c", b=2, c=2)[:, :, 0, :], AX.X, ALU.add)
            link(dve.tensor_reduce(tokf[0:CAP - P, :, 1:2], sps[0:CAP - P, 0:4 * NE].rearrange("p (e b c) -> p e b c", b=2, c=2)[:, :, 1, :], AX.X, ALU.add))
            dve.tensor_copy(k.tok[:], tokf[:])
            dve.wait_ge(ov_sum, 1)
            link(dve.tensor_copy(k.over_flag[:], ops[0:1, 0:1]))

        @block.gpsimd
        def _(pool):
            pool.memset(ones[:], 1.0).then_inc(consts_made, 1)
            pool.iota(iota[:], [[1, CAP]], base=0, channel_multiplier=0, allow_small_or_imprecise_dtypes=True).then_inc(consts_made, 1)
            pool.iota(tok_id[:, :, 0:1], [[0, NT], [0, 1]], base=0, channel_multiplier=1, allow_small_or_imprecise_dtypes=True)
            pool.iota(tok_id[:, :, 1:2], [[P, NT], [0, 1]], base=0, channel_multiplier=0, allow_small_or_imprecise_dtypes=True)\
                .then_inc(consts_made, 1)
            pool.iota(base[:], [[CAP, NE]], base=1, channel_multiplier=0, allow_small_or_imprecise_dtypes=True).then_inc(consts_made, 1)


def experts(nc, k):
    at, A, cst = k.at, k.dram, k.cst
    GU, DN = KD, 4
    SL = GU + DN
    B1 = CAP - P
    whi = at("e_hi", 12, [P, 2, SL, 512], f32r)
    wlo = at("e_lo", 60, [P, 2, SL, 512], f32r)
    raw = at("e_raw", 108, [P, SL, 512])
    xg = at("x_rows", 132, [P, 2, D + NE])
    zero = at("zero_row", 141, [1, D])
    tk = at("tok_now", 145, [P, 2], i32)
    pause = at("pause", 145.25, [P, 2])
    wgt = at("slot_weight", 145.0625, [P, 2, 2])
    hh = at("h", 145.5, [P, 2, CAP])
    act_g = at("silu_g", 147, [P, 2, CAP])
    xhi = at("xgT_hi", 149, [P, KD, CAP], f32r)
    xlo = at("xgT_lo", 155, [P, KD, CAP], f32r)
    hhi = at("h_hi", 161, [P, 2, CAP], f32r)
    hlo = at("h_lo", 162.5, [P, 2, CAP], f32r)
    yo = [at("y_out_a", 6, [P, D]), at("y_out_b", 201, [P, D])]
    ident = cst[:, C_ID:C_ID + P]
    w_loaded = [k.sem(f"e_loaded{s}") for s in range(SL)]
    hi_done, gu_lo, dn_lo = k.sem("e_hi_done"), k.sem("gu_lo_done"), k.sem("dn_lo_done")
    rows_loaded, tok_copied, wgt_copied = k.sem("rows_loaded"), k.sem("tok_copied"), k.sem("wgt_copied")
    rows_t, xhi_done, xlo_done = k.sem("rows_t"), k.sem("exhi_done"), k.sem("exlo_done")
    gsum = k.sem("gu_sum")
    silu, hmul = k.sem("silu_done"), k.sem("h_mul")
    hhi_done, hlo_done = k.sem("hhi_done"), k.sem("hlo_done")
    ysum, y_taken = k.sem("y_sum"), k.sem("y_taken")
    y_stored = [k.sem("y_stored_a"), k.sem("y_stored_b")]
    zeroed, zstored = k.sem("zeroed"), k.sem("zero_stored")
    blocks = [(0, P), (P, B1)]
    UNITS = [(0, 0), (0, 1), (1, 0), (1, 1)]
    BANK = [0, 1, 2, 0]

    def steps(eng, step):
        with eng.Fori(0, NE // 2 - 1) as i:
            for b in range(2):
                step(lambda a, c: i * (2 * a) + (b * a + c), i * 2 + b, b, False)
        for e in (NE - 2, NE - 1):
            step(lambda a, c: e * a + c, e, e % 2, e == NE - 1)

    with nc.psum_tensor("rowsT_ps", [P, 3, 512], f32) as tps, nc.psum_tensor("h_ps", [P, 2, 512], f32) as hps, \
            nc.psum_tensor("y_ps", [P, 3, 512], f32) as yps, nc.Block() as block:

        @block.sync
        def _(sp):
            def load(s, row):
                src = A["w_gu"] if s < GU else A["w_dn"]
                sp.dma_start(raw[:, s, :], src[bass.ds(row, 1)].rearrange("a p n -> p (a n)")).then_inc(w_loaded[s], 16)

            for s in range(GU):
                load(s, s)
            sp.sem_inc(dn_lo, DN)

            def step(n, e, b, last):
                for s in range(DN):
                    sp.wait_ge(dn_lo, n(DN, s + 1))
                    load(GU + s, n(DN, s))
                if not last:
                    for s in range(GU):
                        sp.wait_ge(gu_lo, n(GU, s + 1))
                        load(s, n(GU, GU + s))

            steps(sp, step)

        @block.gpsimd
        def _(pool):
            def gather(n, e):
                pool.tensor_copy(tk[:], k.tok[:, bass.ds(e, 1), :].rearrange("p a c -> p (a c)")).then_inc(tok_copied, 1)
                pool.wait_ge(tok_copied, n)
                pool.tensor_tensor(pause[:, 0:1], pause[:, 1:2], pause[:, 1:2], ALU.add)
                for c, (_, rows) in enumerate(blocks):
                    pool.indirect_dma_start(xg[0:rows, c, :], None, k.x2_dram, bass.IndirectOffsetOnAxis(ap=tk[0:rows, c:c + 1], axis=0))\
                        .then_inc(rows_loaded, 16)

            pool.wait_ge(k.x2_stored, 16 * (NT + 1))
            pool.memset(pause[:], 0.0)
            pool.memset(zero[:], 0.0).then_inc(zeroed, 1)
            pool.wait_ge(zeroed, 1)
            gather(1, 0)
            pool.dma_start(k.y_dram[0:1, :], zero[:]).then_inc(zstored, 16)

            def step(n, e, b, last):
                if last:
                    return
                pool.wait_ge(rows_t, n(1, 1))
                pool.wait_ge(wgt_copied, n(1, 1))
                gather(n(1, 2), n(1, 1))

            steps(pool, step)
            pool.wait_ge(zstored, 16)

        @block.tensor
        def _(pe):
            def turn(n):
                pe.wait_ge(rows_loaded, n(32, 32))
                for s in range(KD):
                    pe.transpose(tps[:, s // 4, (s % 4) * P:(s % 4 + 1) * P], xg[:, 0, s * P:(s + 1) * P], ident)
                for s in range(KD):
                    last = pe.transpose(tps[:, 2, s * B1:(s + 1) * B1], xg[0:B1, 1, s * P:(s + 1) * P], ident[0:B1, 0:B1])
                last.then_inc(rows_t, 1)

            pe.sem_inc(y_taken, 4)
            turn(lambda a, c: c)

            def step(n, e, b, last):
                pe.wait_ge(xlo_done, n(1, 1))
                for m in range(2):
                    pe.wait_ge(hmul, n(2, m + 1))
                    for gu in range(2):
                        o = hps[:, m, gu * CAP:(gu + 1) * CAP]
                        w = slice(gu * DE + m * P, gu * DE + (m + 1) * P)
                        for s in range(GU):
                            if m == 0 and gu == 0:
                                pe.wait_ge(gu_lo, n(GU, s + 1))
                            hi, lo = whi[:, b, s, w], wlo[:, b, s, w]
                            pe.matmul(o, hi, xhi[:, s, :], start=(s == 0), stop=False)
                            pe.matmul(o, hi, xlo[:, s, :], start=False, stop=False)
                            end = pe.matmul(o, lo, xhi[:, s, :], start=False, stop=(s == GU - 1))
                    end.then_inc(gsum, 1)
                if not last:
                    turn(lambda a, c: n(a, a + c))

                def down(u, f):
                    c, j = UNITS[u]
                    sl = slice(0, P) if c == 0 else slice(CAP - P, CAP)
                    hi, lo, w = hhi[:, f, sl], hlo[:, f, sl], GU + 2 * f + j
                    o = yps[:, BANK[u], :]
                    pe.matmul(o, hi, whi[:, b, w, :], start=(f == 0), stop=False)
                    pe.matmul(o, hi, wlo[:, b, w, :], start=False, stop=False)
                    return pe.matmul(o, lo, whi[:, b, w, :], start=False, stop=(f == 1))

                pe.wait_ge(dn_lo, n(DN, 2 * DN))
                pe.wait_ge(hlo_done, n(2, 1))
                for u, free in ((0, 4), (1, 2), (2, 3)):
                    pe.wait_ge(y_taken, n(4, free))
                    down(u, 0)
                pe.wait_ge(hlo_done, n(2, 2))
                for u in range(3):
                    down(u, 1).then_inc(ysum, 1)
                pe.wait_ge(y_taken, n(4, 5))
                down(3, 0)
                down(3, 1).then_inc(ysum, 1)

            steps(pe, step)

        @block.scalar
        def _(act):
            def rows_high(n):
                for j in range(2):
                    act.activation(xhi[:, 4 * j:4 * j + 4, 0:P], tps[:, j, :].rearrange("p (s c) -> p s c", c=P), ACT.Copy)
                act.activation(xhi[:, :, P:CAP], tps[:, 2, :].rearrange("p (s c) -> p s c", c=B1), ACT.Copy).then_inc(xhi_done, 1)

            def high(b, s):
                act.activation(whi[:, b, s, :], raw[:, s, :], ACT.Copy).then_inc(hi_done, 1)

            act.sem_inc(gsum, 2)
            act.sem_inc(ysum, 8)
            act.sem_inc(y_stored[0], 16)
            act.sem_inc(y_stored[1], 16)
            for s in range(GU):
                act.wait_ge(w_loaded[s], 16)
                high(0, s)
            act.wait_ge(rows_t, 1)
            rows_high(lambda a, c: c)

            def step(n, e, b, last):
                act.wait_ge(ysum, n(4, 4))
                for s in range(GU, SL):
                    act.wait_ge(w_loaded[s], n(16, 16))
                    high(b, s)
                for m in range(2):
                    if not last:
                        act.wait_ge(gsum, n(2, 2))
                        for s in range(4 * m, 4 * m + 4):
                            act.wait_ge(w_loaded[s], n(16, 32))
                            high(1 - b, s)
                    act.wait_ge(gsum, n(2, m + 3))
                    act.wait_ge(hmul, n(2, m + 1))
                    act.activation(act_g[:, m, :], hps[:, m, 0:CAP], ACT.Silu).then_inc(silu, 1)
                    act.wait_ge(hmul, n(2, m + 3))
                    act.activation(hhi[:, m, :], hh[:, m, :], ACT.Copy).then_inc(hhi_done, 1)
                if not last:
                    act.wait_ge(rows_t, n(1, 2))
                    act.wait_ge(gsum, n(2, 4))
                    rows_high(n)
                for u, (c, j) in enumerate(UNITS):
                    if j == 0:
                        act.wait_ge(y_stored[c], n(16, 16))
                        act.wait_ge(wgt_copied, n(1, 1))
                    act.wait_ge(ysum, n(4, u + 9))
                    r = slice(0, P) if c == 0 else slice(P - B1, P)
                    act.activation(yo[c][r, 512 * j:512 * j + 512], yps[r, BANK[u], :], ACT.Copy, scale=wgt[r, b, c:c + 1])\
                       .then_inc(y_taken, 1)
                    if j == 1:
                        act.wait_ge(y_taken, n(4, u + 5))
                        first, rows = blocks[c]
                        act.dma_start(k.y_dram[bass.ds(n(CAP, 1 + first), rows), :], yo[c][r, :]).then_inc(y_stored[c], 16)

            steps(act, step)
            for c in range(2):
                act.wait_ge(y_stored[c], 16 * (NE + 1))

        @block.vector
        def _(dve):
            def rows_rest(n, col, b):
                dve.tensor_copy(wgt[:, b, 0:1], xg[:, 0, bass.ds(col, 1)])
                dve.tensor_copy(wgt[P - B1:P, b, 1:2], xg[0:B1, 1, bass.ds(col, 1)]).then_inc(wgt_copied, 1)
                dve.wait_ge(xhi_done, n(1, 1))
                for j in range(2):
                    dve.tensor_tensor(xlo[:, 4 * j:4 * j + 4, 0:P], tps[:, j, :].rearrange("p (s c) -> p s c", c=P),
                                      xhi[:, 4 * j:4 * j + 4, 0:P].bitcast(f32), ALU.subtract)
                dve.tensor_tensor(xlo[:, :, P:CAP], tps[:, 2, :].rearrange("p (s c) -> p s c", c=B1),
                                  xhi[:, :, P:CAP].bitcast(f32), ALU.subtract).then_inc(xlo_done, 1)

            def rest(b, s, sem):
                dve.tensor_tensor(wlo[:, b, s, :], raw[:, s, :], whi[:, b, s, :].bitcast(f32), ALU.subtract).then_inc(sem, 1)

            dve.sem_inc(hmul, 2)
            for s in range(GU):
                dve.wait_ge(hi_done, s + 1)
                rest(0, s, gu_lo)
            dve.wait_ge(rows_loaded, 32)
            rows_rest(lambda a, c: c, D, 0)

            def step(n, e, b, last):
                for s in range(DN):
                    dve.wait_ge(hi_done, n(SL, GU + s + 1))
                    rest(b, GU + s, dn_lo)
                for m in range(2):
                    if not last:
                        for s in range(4 * m, 4 * m + 4):
                            dve.wait_ge(hi_done, n(SL, SL + s + 1))
                            rest(1 - b, s, gu_lo)
                    dve.wait_ge(silu, n(2, m + 1))
                    dve.tensor_tensor(hh[:, m, :], act_g[:, m, :], hps[:, m, CAP:2 * CAP], ALU.mult).then_inc(hmul, 1)
                    dve.wait_ge(hhi_done, n(2, m + 1))
                    dve.tensor_tensor(hlo[:, m, :], hh[:, m, :], hhi[:, m, :].bitcast(f32), ALU.subtract).then_inc(hlo_done, 1)
                if not last:
                    dve.wait_ge(rows_loaded, n(32, 64))
                    dve.wait_ge(y_taken, n(4, 4))
                    rows_rest(lambda a, c: n(a, a + c), n(1, D + 1), 1 - b)

            steps(dve, step)


def overflow(nc, k):
    at, A, cst = k.at, k.dram, k.cst
    xT = at("ov_x2T", 12, [P, NT, KD, P])
    xs = at("ov_tile", 44, [P, KD, P])
    gu = at("ov_gate_up", 48, [P, KD, 2 * DE])
    dn = at("ov_down", 64, [P, 4, D // 2])
    gate = at("ov_gate", 72, [P, 2, P])
    hid = at("ov_hidden", 73, [P, 2, P])
    wgt = at("ov_weight", 74, [P, 1])
    ysb = at("ov_y", 76, [P, D])
    ident = cst[:, C_ID:C_ID + P]
    x2 = k.x1
    turned, copied, w_loaded = k.sem("ov_turned"), k.sem("ov_copied"), k.sem("ov_loaded")
    staged, h_sum, silu, h_made = k.sem("ov_staged"), k.sem("ov_h_sum"), k.sem("ov_silu"), k.sem("ov_h_made")
    y_sum, y_out, added = k.sem("ov_y_sum"), k.sem("ov_y_out"), k.sem("ov_added")
    weighted, w_used = k.sem("ov_weighted"), k.sem("ov_w_used")

    def over_all(eng, expert, tile):
        with eng.Fori(0, NE) as e:
            expert(e)
            if tile:
                with eng.Fori(0, NT) as t:
                    tile(e * NT + t, e, t)

    with nc.psum_tensor("ovT_ps", [P, 2, 512], f32) as tps, nc.psum_tensor("ov_h_ps", [P, 512], f32) as hps, \
            nc.psum_tensor("ov_y_ps", [P, 2, 512], f32) as yps, nc.Block() as block:

        @block.sync
        def _(sp):
            with sp.If(sp.value_load(k.over_flag[0:1, 0:1], min_val=0, max_val=2 * S) > 0):
                def expert(e):
                    sp.wait_ge(w_used, e + 1)
                    sp.dma_start(gu[:], A["w_gu"][bass.ds(e * KD, KD)].rearrange("s p n -> p s n")).then_inc(w_loaded, 16)
                    sp.dma_start(dn[:], A["w_dn"][bass.ds(e * 4, 4)].rearrange("s p n -> p s n")).then_inc(w_loaded, 16)

                sp.sem_inc(w_used, 1)
                over_all(sp, expert, None)

        @block.tensor
        def _(pe):
            with pe.If(pe.value_load(k.over_flag[0:1, 0:1], min_val=0, max_val=2 * S) > 0):
                for t in range(NT):
                    if t:
                        pe.wait_ge(copied, t)
                    for s in range(KD):
                        last = pe.transpose(tps[:, s // 4, (s % 4) * P:(s % 4 + 1) * P], x2[:, t, s * P:(s + 1) * P], ident)
                    last.then_inc(turned, 1)

                def tile(n, e, t):
                    pe.wait_ge(w_loaded, e * 32 + 32)
                    pe.wait_ge(staged, n + 1)
                    for j in range(4):
                        for s in range(KD):
                            last = pe.matmul(hps[:, j * P:(j + 1) * P], gu[:, s, j * P:(j + 1) * P], xs[:, s, :],
                                             start=(s == 0), stop=(s == KD - 1))
                    last.then_inc(h_sum, 1)
                    pe.wait_ge(h_made, n + 1)
                    for j in range(2):
                        for f in range(2):
                            last = pe.matmul(yps[:, j, :], hid[:, f, :], dn[:, 2 * f + j, :], start=(f == 0), stop=(f == 1))
                    last.then_inc(y_sum, 1)

                with pe.Fori(0, NE) as e:
                    with pe.Fori(0, NT) as t:
                        tile(e * NT + t, e, t)
                    pe.wait_ge(y_sum, e * NT + NT)
                    pe.sem_inc(w_used, 1)

        @block.scalar
        def _(act):
            with act.If(act.value_load(k.over_flag[0:1, 0:1], min_val=0, max_val=2 * S) > 0):
                def tile(n, e, t):
                    act.wait_ge(h_sum, n + 1)
                    act.activation(gate[:].rearrange("p f c -> p (f c)"), hps[:, 0:2 * P], ACT.Silu).then_inc(silu, 1)
                    act.wait_ge(y_sum, n + 1)
                    act.wait_ge(weighted, n + 1)
                    act.wait_ge(added, n + 1)
                    act.activation(ysb[:], yps[:].rearrange("p j c -> p (j c)"), ACT.Copy, scale=wgt[:]).then_inc(y_out, 1)

                over_all(act, lambda e: None, tile)

        @block.vector
        def _(dve):
            with dve.If(dve.value_load(k.over_flag[0:1, 0:1], min_val=0, max_val=2 * S) > 0):
                for t in range(NT):
                    dve.wait_ge(turned, t + 1)
                    dve.tensor_copy(xT[:, t].rearrange("p s c -> p (s c)"), tps[:].rearrange("p j c -> p (j c)")).then_inc(copied, 1)
                dve.tensor_scalar(k.comb_over[:], k.comb_over[:], 1.0 / ALPHA, None, ALU.mult).then_inc(copied, 1)
                dve.wait_ge(copied, NT + 1)

                def tile(n, e, t):
                    dve.wait_ge(y_out, n + 1)
                    dve.tensor_copy(xs[:], xT[:, bass.ds(t, 1)].rearrange("p t s c -> p (t s) c")).then_inc(staged, 1)
                    dve.tensor_copy(wgt[:], k.comb_over[:, bass.ds(t, 1), bass.ds(e, 1)].rearrange("p t e -> p (t e)")).then_inc(weighted, 1)
                    dve.wait_ge(silu, n + 1)
                    dve.tensor_tensor(hid[:].rearrange("p f c -> p (f c)"), gate[:].rearrange("p f c -> p (f c)"), hps[:, 2 * P:4 * P], ALU.mult)\
                       .then_inc(h_made, 1)
                    dve.wait_ge(y_out, n + 2)
                    x = x2[:, bass.ds(t, 1), :].rearrange("p t c -> p (t c)")
                    dve.tensor_tensor(x, x, ysb[:], ALU.add).then_inc(added, 1)

                dve.sem_inc(added, 1)
                dve.sem_inc(y_out, 1)
                over_all(dve, lambda e: None, tile)


def finish(nc, k):
    at, A = k.at, k.dram
    g = at("ln3_g", 12, [P, D])
    b = at("ln3_b", 16, [P, D])
    tmp = at("ln3_tmp", 20, [P, 2, D])
    yt = at("ln3_out", 28, [P, 2, D])
    st = at("ln3_st", 36, [P, 2, 2, 6])
    mv = at("ln3_mv", 36.125, [P, NT, 2])
    rs = at("ln3_rs", 36.25, [P, NT])
    half = at("ln3_half", 36.375, [P, 1])
    loaded, scaled = k.sem("gains10_loaded"), k.sem("x2_scaled")
    added = [k.sem(f"added{t}") for t in range(NT)]
    var_ready, rstd_ready = k.sem("ln3_var"), k.sem("ln3_rstd")
    chain_s, chain_p, made = k.sem("chain10"), k.sem("pool_chain10"), k.sem("out_made")
    stored = [k.sem("out_stored0"), k.sem("out_stored1")]
    x2 = k.x1
    with nc.Block() as block:

        @block.sync
        def _(sp):
            sp.dma_start(g[:], over(A["ln_moe_g"], [P, D])).then_inc(loaded, 16)
            sp.dma_start(b[:], over(A["ln_moe_b"], [P, D])).then_inc(loaded, 16)
            for t in range(NT):
                sp.wait_ge(made, t + 1)
                sp.dma_start(A["out"][t * P:(t + 1) * P, :], yt[:, t % 2, :]).then_inc(stored[t % 2], 16)
            for j in range(2):
                sp.wait_ge(stored[j], 16 * (NT // 2))

        @block.scalar
        def _(act):
            for t in range(NT):
                act.activation(x2[:, t, :], x2[:, t, :], ACT.Copy, scale=ALPHA).then_inc(scaled, 1)

        @block.gpsimd
        def _(pool):
            pool.memset(half[:], -0.5).then_inc(chain_p, 1)
            pool.wait_ge(chain_p, 1)
            n = 1

            def add(t, j):
                pool.indirect_dma_start(x2[:, t, :], None, k.y_dram, bass.IndirectOffsetOnAxis(ap=k.y_row[:, j, t:t + 1], axis=0),
                                        compute_op=ALU.add).then_inc(added[t], 16)

            def rstd(t):
                pool.wait_ge(var_ready, t + 1)
                pool.tensor_scalar(mv[:, t, 1:2], mv[:, t, 1:2], EPS, None, ALU.add).then_inc(chain_p, 1)
                pool.wait_ge(chain_p, t + 2)
                pool.tensor_tensor(rs[:, t:t + 1], mv[:, t, 1:2], half[:], ALU.pow).then_inc(rstd_ready, 1)

            for t in range(NT + 2):
                if t < NT:
                    pool.wait_ge(scaled, t + 1)
                    add(t, 0)
                if 1 <= t <= NT:
                    pool.wait_ge(added[t - 1], 16)
                    add(t - 1, 1)
                if t >= 2:
                    rstd(t - 2)

        @block.vector
        def _(dve):
            chain = [0]

            def link(ins):
                chain[0] += 1
                ins.then_inc(chain_s, 1)
                dve.wait_ge(chain_s, chain[0])

            def norm(t):
                j = t % 2
                dve.wait_ge(rstd_ready, t + 1)
                link(dve.scalar_tensor_tensor(tmp[:, j, :], x2[:, t, :], mv[:, t, 0:1], g[:], ALU.subtract, ALU.mult))
                if t >= 2:
                    dve.wait_ge(stored[j], 16 * (t // 2))
                dve.scalar_tensor_tensor(yt[:, j, :], tmp[:, j, :], rs[:, t:t + 1], b[:], ALU.mult, ALU.add).then_inc(made, 1)

            dve.wait_ge(loaded, 32)
            for t in range(NT + 1):
                if t < NT:
                    dve.wait_ge(added[t], 32)
                    for j in range(2):
                        last = dve.bn_stats(st[:, t % 2, j, :], x2[:, t, 512 * j:512 * j + 512])
                    link(last)
                    dve.bn_aggr(mv[:, t, :], st[:, t % 2].rearrange("p j c -> p (j c)")).then_inc(var_ready, 1)
                if t:
                    norm(t - 1)


def program(nc, A, upto=99):
    k = Shared()
    k.dram = A
    k.at = at = placer(nc)
    k.sem = nc.alloc_semaphore
    k.cst = at("constants", 0, [P, C_COLS])
    k.sin = at("sin", 6, [P, NT, NF])
    k.cos = at("cos", 8, [P, NT, NF])
    k.qk = at("qk", 12, [P, NT, 2 * RW])
    k.rv = at("rv", 28, [P, NT, RW])
    k.sg = at("sg", 36, [P, NT, RW])
    k.su = at("su", 44, [P, NT, SW])
    k.sv = at("sv", 52, [P, NT, SW])
    k.cq = at("cq", 60, [P, NT, QR])
    k.ckv = at("ckv", 68, [P, NT, KVR])
    k.kr = at("kr", 72, [P, NT, ROPE])
    k.mixA = at("mix_ret_sgu", 73, [P, NT, RW + SW])
    k.mixB = at("mix_mla", 89, [P, NT, MW])
    k.kT = at("mla_kT", 105, [P, MH, S])
    k.qT = at("mla_qT", 137, [P, MH, S])
    k.v = at("mla_v", 169, [P, NT, MW])
    k.w_out_raw, k.w_out_loaded = at("w_out_raw", 30, [P, KD, D]), k.sem("w_out_loaded")
    k.x1 = at("x1", 169, [P, NT, D])
    k.wk, k.wv, k.kv_loaded = at("xa_wk_raw", 30, [P, KD, XW]), at("xa_wv_raw", 46, [P, KD, XW]), k.sem("kv_loaded")
    k.wq_hi, k.wq_lo = at("wq_hi", 105, [P, KD, XW], f32r), at("wq_lo", 121, [P, KD, XW], f32r)
    k.xwo_hi, k.xwo_lo = at("xwo_hi", 137, [P, XH, D], f32r), at("xwo_lo", 153, [P, XH, D], f32r)
    k.xkT, k.xv = at("xkT", 12, [P, XH, MEM]), at("xv", 16, [P, 2, XW])
    k.x2_dram = nc.dram_tensor("x2_rows", [S, D + NE], f32).ap()
    k.x2_stored = k.sem("x2_stored")
    k.y_dram = nc.dram_tensor("y_rows", [1 + NE * CAP, D], f32).ap()
    k.tok = at("slot_tokens", 205, [P, NE, 2], i32)
    k.y_row = at("y_row", 205.125, [P, 2, NT], i32)
    k.over_flag = at("over_flag", 205.1875, [1, 1], i32)
    k.comb = at("combine", 205.25, [P, NT, NE])
    k.comb_over = at("combine_over", 205.75, [P, NT, NE])
    phases = [project, prepare, attend, mix_out, memory_keys, cross_attend, route, experts, overflow, finish]
    for i, f in enumerate(phases[:upto]):
        used = []

        def sem(name):
            used.append(nc.alloc_semaphore(name))
            return used[-1]

        k.sem = sem
        f(nc, k)
        if i in (1, 5):
            nc.clear_and_free_semaphores(used)
            nc.all_engine_barrier()
    return k


def layouts(x, mem, positions, w_in, w_out, sgu_ln_g, sgu_ln_b, sgu_w, sgu_b,
            mla_q_norm_g, mla_w_uq, mla_kv_norm_g, mla_w_ukv,
            xa_wq, xa_wk, xa_wv, xa_wo,
            ln_mix_g, ln_mix_b, ln_xa_g, ln_xa_b, ln_moe_g, ln_moe_b,
            router_w, router_bias, expert_w_gate, expert_w_up, expert_w_down):
    c = np.ascontiguousarray
    a = {}
    a["cst"] = constants()
    a["x"] = c(x[0])
    a["xT"] = c(np.transpose(x[0]).reshape(KD, P, S))
    a["positions"] = c(positions.reshape(NT, P).T)
    a["w_in"] = c(w_in[0])
    a["sgu_ln_g"], a["sgu_ln_b"] = c(sgu_ln_g), c(sgu_ln_b)
    a["q_norm_g"] = c(mla_q_norm_g.reshape(QR // P, P).T)
    a["kv_norm_g"] = c(mla_kv_norm_g.reshape(1, P).T)
    a["w_uq"] = c(mla_w_uq[0])
    kv = mla_w_ukv[0].reshape(KVR, MH, 2, NOPE)
    a["w_ukv"] = c(kv.transpose(0, 2, 1, 3).reshape(KVR, 2 * MW))
    a["sgu_bT"] = c(sgu_b[0].T)
    a["sgu_wT"] = c(sgu_w[0].transpose(2, 0, 1))
    a["w_out"] = c(w_out[0])
    a["ln_mix_g"], a["ln_mix_b"], a["ln_xa_g"], a["ln_xa_b"] = c(ln_mix_g), c(ln_mix_b), c(ln_xa_g), c(ln_xa_b)
    a["memT"] = c(np.transpose(mem[0]))
    a["xa_wq"], a["xa_wk"], a["xa_wv"], a["xa_wo"] = c(xa_wq[0]), c(xa_wk[0]), c(xa_wv[0]), c(xa_wo[0])
    a["router_w"], a["router_bias"] = c(router_w), c(router_bias.reshape(1, NE))
    a["w_gu"] = c(np.concatenate([expert_w_gate[0], expert_w_up[0]], axis=2).reshape(NE * KD, P, 2 * DE))
    a["w_dn"] = c(expert_w_down[0].reshape(NE, 2, P, 2, D // 2).transpose(0, 1, 3, 2, 4).reshape(NE * 4, P, D // 2))
    a["ln_moe_g"], a["ln_moe_b"] = c(ln_moe_g), c(ln_moe_b)
    return a


def kernel(**inputs):
    import concourse.bacc as bacc
    from concourse.bass_utils import run_bass_kernel_spmd
    nc = bacc.Bacc("TRN2", target_bir_lowering=False, num_devices=1)
    arrays = layouts(**{n: np.asarray(v) for n, v in inputs.items()})
    aps = {n: nc.dram_tensor(n, a.shape, mybir.dt.from_np(a.dtype), kind="ExternalInput").ap() for n, a in arrays.items()}
    aps["out"] = nc.dram_tensor("out", [S, D], f32, kind="ExternalOutput").ap()
    program(nc, aps)
    r = run_bass_kernel_spmd(nc, [arrays], core_ids=[0])
    return r.results[0]["out"].reshape(1, S, D)
```

```python
import math

import concourse.bass as bass
import numpy as np
from concourse import mybir

f32 = mybir.dt.float32
f32r = mybir.dt.float32r
i32 = mybir.dt.int32
bf16 = mybir.dt.bfloat16
ACT = mybir.ActivationFunctionType
ALU = mybir.AluOpType
AX = mybir.AxisListType

P = 128
S, D = 1024, 1024
NT = S // P
KD = D // P
MEM = 256
RH, RD = 4, 64
RW = RH * RD
SG, SD = 4, 64
SW = SG * SD
MH, NOPE, ROPE, MV = 8, 64, 32, 64
MQ = NOPE + ROPE
QR, KVR = 256, 128
MW = MH * MV
XH, XD = 4, 128
XW = XH * XD
NE, NG, EG, DE = 16, 4, 4, 256
CAP = 192
EPS = 1e-5
ALPHA = 2.0 ** 0.25
MLA_SCALE = MQ ** -0.5
XA_SCALE = XD ** -0.5
NEG = -1.0e30
CH_QK, CH_VG, CH_UV, CH_LAT = range(4)
CHUNK_W = [2 * RW, 2 * RW, 2 * SW, QR + KVR + ROPE]
CHUNK_AT = [0, 2 * RW, 4 * RW, 4 * RW + 2 * SW]
IN_COLS = sum(CHUNK_W)

C_ID, C_MASK, C_DEC, C_QDEC, C_INNER, C_ST, C_FREQ, C_TRI = 0, 128, 256, 768, 1024, 1280, 1282, 1346
C_COLS = 1474
NF = 64

SBUF_BASE = 16640


def constants():
    c = np.zeros((P, C_COLS), np.float64)
    r = np.arange(P)
    lg = np.log1p(-(2.0 ** (-5.0 - np.arange(RH))))
    c[:, C_ID:C_ID + P] = np.eye(P)
    c[:, C_MASK:C_MASK + P] = np.where(r[None, :] <= r[:, None], 0.0, NEG)
    for h in range(RH):
        diff = r[None, :] - r[:, None]
        dec = np.where(diff >= 0, np.exp(lg[h] * np.maximum(diff, 0)), 0.0) * RD ** -0.5
        c[:, C_DEC + P * h:C_DEC + P * (h + 1)] = dec
        c[:, C_INNER + RD * h:C_INNER + RD * (h + 1)] = (np.exp(lg[h] * (P - 1 - r)) * RD ** -0.5)[:, None]
        rows = slice(RD * (h % 2), RD * (h % 2) + RD)
        c[rows, C_QDEC + P * (h // 2):C_QDEC + P * (h // 2) + P] = np.exp(lg[h] * (r + 1))[None, :]
        c[rows, C_ST + h // 2] = np.exp(lg[h] * P)
    fr, fm = ((10000.0 ** (-np.arange(0, d, 2, dtype=np.float32) / np.float32(d)).astype(np.float64))
              .astype(np.float32) for d in (RD, ROPE))
    c[:, C_FREQ:C_FREQ + NF] = np.concatenate([fr, fm, fm])[None, :]
    c[:, C_TRI:C_TRI + P] = (r[:, None] <= r[None, :])
    return c.astype(np.float32)


class Shared:
    pass


def placer(nc):
    def at(name, kib, shape, dt=f32):
        return nc.alloc_sbuf_tensor_at(name, shape, dt, offset=SBUF_BASE + int(kib * 1024))
    return at


def over(ap, shape):
    return ap.broadcast_to(shape)


def project(nc, k):
    at, A = k.at, k.dram
    RAWX, RAWW = 4, 8
    xhi = at("xhi", 73, [P, KD, S], f32r)
    xlo = at("xlo", 105, [P, KD, S], f32r)
    whi = at("whi", 137, [P, KD, 512], f32r)
    wlo = at("wlo", 153, [P, KD, 512], f32r)
    xraw = at("xraw", 169, [P, RAWX, S])
    wraw = at("wraw", 185, [P, RAWW, 512])
    ta = at("rope_a", 201, [P, 512])
    tb = at("rope_b", 203, [P, 512])
    ang = at("ang", 12, [P, NT, NF])
    turns = at("turns", 14, [P, NT, NF])
    posi = at("posi", 205, [P, NT], i32)
    posf = at("posf", 205.125, [P, NT])
    ssq = at("ssq", 205.25, [P, NT, 2])
    stat = at("stat", 205.5, [P, 6])
    mv = at("mv", 205.625, [P, 2])
    rs = at("rs", 205.75, [P, 2])
    halfs = at("halfs", 205.875, [P, 2])
    junk = at("junk", 205.9375, [P, 256])
    gsg = at("sgu_g", 10, [P, SW])
    bsg = at("sgu_bb", 11, [P, SW])

    x_loaded = [k.sem(f"x_loaded{i}") for i in range(RAWX)]
    w_loaded = [k.sem(f"w_loaded{i}") for i in range(RAWW)]
    small_loaded = k.sem("small_loaded")
    norm_loaded = k.sem("norm_loaded")
    x_hi_done = k.sem("x_hi_done")
    x_lo_done = k.sem("x_lo_done")
    w_hi_done = k.sem("w_hi_done")
    w_lo_done = k.sem("w_lo_done")
    w_slice_used = k.sem("w_slice_used")
    unit_summed = k.sem("unit_summed")
    unit_taken = k.sem("unit_taken")
    act_part = k.sem("act_part")
    dve_chain = k.sem("dve_chain")
    var_ready = k.sem("var_ready")
    rstd_ready = k.sem("rstd_ready")
    pool_chain = k.sem("pool_chain")
    angles = k.sem("angles")
    tables = k.sem("tables")
    with nc.psum_tensor("unit_ps", [P, 4, 512], f32) as ps, \
            nc.Block() as block:
        units = [(c, t) for c in (CH_QK, CH_LAT, CH_UV, CH_VG) for t in range(NT)]
        order = [CH_QK, CH_LAT, CH_UV, CH_VG]
        BANKS = 4

        def slice_free(eng, c, s):
            if c and s < KD - 1:
                eng.wait_ge(w_slice_used, (c - 1) * (KD - 1) + s + 1)
            elif c:
                eng.wait_ge(unit_summed, c * NT)

        def next_slices(u, split_w):
            c = u // NT
            if u % NT == NT - 1 and c < 3:
                for s in range(KD - 1):
                    split_w(c + 1, s)
            elif c and u % NT == 0:
                split_w(c, KD - 1)

        @block.sync
        def _(sp):
            for c in range(4):
                for s in range(KD):
                    n = c * KD + s
                    if c == 0:
                        if s >= RAWX:
                            sp.wait_ge(x_lo_done, s - RAWX + 1)
                        sp.dma_start(xraw[:, s % RAWX, :], A["xT"][s]).then_inc(x_loaded[s % RAWX], 16)
                    if n >= RAWW:
                        sp.wait_ge(w_lo_done, n - RAWW + 1)
                    w = CHUNK_W[order[c]]
                    o = CHUNK_AT[order[c]]
                    sp.dma_start(wraw[:, s, 0:w], A["w_in"][s * P:(s + 1) * P, o:o + w]).then_inc(w_loaded[s], 16)
                    if n == 2:
                        sp.dma_start(k.cst[:], A["cst"]).then_inc(small_loaded, 16)
                        sp.dma_start(posi[:], A["positions"]).then_inc(small_loaded, 16)
                if c == 0:
                    sp.dma_start(gsg[:], over(A["sgu_ln_g"], [P, SW])).then_inc(norm_loaded, 16)
                    sp.dma_start(bsg[:], over(A["sgu_ln_b"], [P, SW])).then_inc(norm_loaded, 16)
            sp.wait_ge(w_lo_done, 4 * KD)
            sp.dma_start(k.gq[:], A["q_norm_g"]).then_inc(k.up_loaded, 16)
            sp.dma_start(k.gkv[:], A["kv_norm_g"]).then_inc(k.up_loaded, 16)
            sp.dma_start(k.sgb[:], A["sgu_bT"]).then_inc(k.up_loaded, 16)
            sp.dma_start(k.wuq[:], A["w_uq"].rearrange("(k p) n -> p k n", p=P)).then_inc(k.up_loaded, 16)
            sp.dma_start(k.wukv[:], A["w_ukv"]).then_inc(k.up_loaded, 16)
            sp.dma_start(k.wsg[:], A["sgu_wT"]).then_inc(k.up_loaded, 16)

        @block.scalar
        def _(act):
            def split_w(c, s):
                n = c * KD + s
                w = CHUNK_W[order[c]]
                act.wait_ge(w_loaded[s], 16 * (c + 1))
                slice_free(act, c, s)
                act.activation(whi[:, s, 0:w], wraw[:, s, 0:w], ACT.Copy).then_inc(w_hi_done, 1)

            for s in range(KD):
                act.wait_ge(x_loaded[s % RAWX], 16 * (s // RAWX + 1))
                act.activation(xhi[:, s, :], xraw[:, s % RAWX, :], ACT.Copy).then_inc(x_hi_done, 1)
                split_w(0, s)
                if s == 5:
                    act.wait_ge(angles, 1)
                    act.activation(k.sin[:], ang[:], ACT.Sin).then_inc(tables, 1)
                    act.wait_ge(angles, 2)
                    act.activation(k.cos[:], turns[:], ACT.Sin).then_inc(tables, 1)
            n_part = 0
            for u, (c, t) in enumerate(units):
                b = u % BANKS
                next_slices(u, split_w)
                act.wait_ge(unit_summed, u + 1)
                if c == CH_VG:
                    act.activation(k.rv[:, t, :], ps[:, b, 0:RW], ACT.Copy).then_inc(act_part, 1)
                    if t >= 2:
                        act.wait_ge(unit_taken, u - 1)
                    act.activation(xraw[:, t % 2, 0:RW], ps[:, b, RW:2 * RW], ACT.Tanh, scale=0.5).then_inc(act_part, 1)
                elif c == CH_UV:
                    act.activation(k.su[:, t, :], ps[:, b, 0:SW], ACT.Copy).then_inc(act_part, 1)
                elif c == CH_LAT:
                    if t:
                        act.wait_ge(act_part, 2 * t)
                    act.activation(junk[:, 0:QR], ps[:, b, 0:QR], ACT.Square, accum_out=ssq[:, t, 0:1]).then_inc(act_part, 1)
                    act.wait_ge(act_part, 2 * t + 1)
                    act.activation(junk[:, 0:KVR], ps[:, b, QR:QR + KVR], ACT.Square, accum_out=ssq[:, t, 1:2]).then_inc(act_part, 1)

        @block.tensor
        def _(pe):
            def part(u, s):
                c, t = units[u]
                ci, b, w = u // NT, u % BANKS, CHUNK_W[c]
                if ci == 0 and t == 0:
                    pe.wait_ge(x_lo_done, s + 1)
                if t == 0:
                    pe.wait_ge(w_lo_done, ci * KD + s + 1)
                hi, lo = xhi[:, s, t * P:(t + 1) * P], xlo[:, s, t * P:(t + 1) * P]
                o = ps[:, b, 0:w]
                pe.matmul(o, hi, whi[:, s, 0:w], start=(s == 0), stop=False)
                pe.matmul(o, hi, wlo[:, s, 0:w], start=False, stop=False)
                last = pe.matmul(o, lo, whi[:, s, 0:w], start=False, stop=(s == KD - 1))
                if s == KD - 1:
                    last.then_inc(unit_summed, 1)
                elif t == NT - 1:
                    last.then_inc(w_slice_used, 1)

            for s in range(KD):
                for u in range(BANKS):
                    part(u, s)
            for u in range(BANKS, len(units)):
                pe.wait_ge(unit_taken, u - BANKS + 1)
                for s in range(KD):
                    part(u, s)

        @block.vector
        def _(dve):
            chain = [0]

            def link(ins):
                chain[0] += 1
                ins.then_inc(dve_chain, 1)
                dve.wait_ge(dve_chain, chain[0])

            def split_w(c, s):
                n = c * KD + s
                w = CHUNK_W[order[c]]
                dve.wait_ge(w_hi_done, n + 1)
                dve.tensor_tensor(wlo[:, s, 0:w], wraw[:, s, 0:w], whi[:, s, 0:w].bitcast(f32), ALU.subtract)\
                   .then_inc(w_lo_done, 1)

            def reduce_angles():
                dve.wait_ge(small_loaded, 32)
                link(dve.tensor_copy(posf[:], posi[:]))
                freq = k.cst[:, None, C_FREQ:C_FREQ + NF]
                link(dve.tensor_tensor(ang[:], over(posf[:, :, None], [P, NT, NF]), over(freq, [P, NT, NF]), ALU.mult))
                magic = 1.5 * 2.0 ** 23
                link(dve.tensor_scalar(turns[:], ang[:], 1.0 / (2 * math.pi), magic, ALU.mult, ALU.add))
                link(dve.tensor_scalar(turns[:], turns[:], magic, None, ALU.subtract))
                p1 = 6.28125
                p2 = 0.0019350051879882812
                p3 = 2 * math.pi - p1 - p2
                for part in (p1, p2, p3):
                    link(dve.scalar_tensor_tensor(ang[:], turns[:], -part, ang[:], ALU.mult, ALU.add))
                pi = 3.1415925
                link(dve.tensor_scalar(ang[:], ang[:], -pi, pi, ALU.max, ALU.min))
                dve.scalar_tensor_tensor(turns[:], ang[:], -1.0, ang[:], ALU.mult, ALU.min).then_inc(angles, 1)
                dve.wait_ge(angles, 1)
                dve.tensor_scalar(turns[:], turns[:], math.pi / 2, None, ALU.add).then_inc(angles, 1)

            def prepare_weights():
                dve.wait_ge(k.up_loaded, 96)
                for s in range(2):
                    last = dve.tensor_scalar(k.wuq[:, s, :], k.wuq[:, s, :], k.gq[:, s:s + 1], None, ALU.mult)
                last.then_inc(k.up_ready, 1)
                dve.tensor_scalar(k.wukv[:], k.wukv[:], k.gkv[:, 0:1], None, ALU.mult).then_inc(k.up_ready, 1)
                dve.tensor_tensor(k.wsg[:], k.wsg[:], over(k.cst[:, None, C_TRI:C_TRI + P], [P, SG, P]), ALU.mult)\
                   .then_inc(k.up_ready, 1)

            for s in range(KD):
                dve.wait_ge(x_hi_done, s + 1)
                dve.tensor_tensor(xlo[:, s, :], xraw[:, s % RAWX, :], xhi[:, s, :].bitcast(f32), ALU.subtract)\
                   .then_inc(x_lo_done, 1)
                split_w(0, s)
                if s == 3:
                    reduce_angles()
            dve.wait_ge(tables, 2)
            dve.wait_ge(norm_loaded, 32)
            for u, (c, t) in enumerate(units):
                b = u % BANKS
                next_slices(u, split_w)
                if u == 3 * NT + 3:
                    prepare_weights()
                dve.wait_ge(unit_summed, u + 1)
                if c == CH_QK:
                    x = ps[:, b, :].rearrange("p (g f) -> p g f", f=32)
                    cb, sb_ = over(k.cos[:, t:t + 1, 0:32], [P, 16, 32]), over(k.sin[:, t:t + 1, 0:32], [P, 16, 32])
                    a3, b3 = (z[:].rearrange("p (g f) -> p g f", f=32) for z in (ta, tb))
                    dve.tensor_tensor(a3, x, cb, ALU.mult)
                    dve.tensor_tensor(b3, x, sb_, ALU.mult).then_inc(unit_taken, 1)
                    dve.wait_ge(unit_taken, u + 1)
                    a4, b4, o4 = (z.rearrange("p (g i f) -> p g i f", i=2, f=32) for z in (ta[:], tb[:], k.qk[:, t, :]))
                    dve.tensor_tensor(o4[:, :, 0, :], a4[:, :, 0, :], b4[:, :, 1, :], ALU.subtract)
                    link(dve.tensor_tensor(o4[:, :, 1, :], b4[:, :, 0, :], a4[:, :, 1, :], ALU.add))
                elif c == CH_LAT:
                    x = ps[:, b, QR + KVR:QR + KVR + ROPE]
                    dve.wait_ge(act_part, 2 * t + 2)
                    dve.tensor_tensor(ta[:, 0:ROPE], x, k.cos[:, t, 32:64], ALU.mult)
                    link(dve.tensor_tensor(tb[:, 0:ROPE], x, k.sin[:, t, 32:64], ALU.mult))
                    dve.tensor_tensor(k.kr[:, t, 0:16], ta[:, 0:16], tb[:, 16:32], ALU.subtract)
                    link(dve.tensor_tensor(k.kr[:, t, 16:32], tb[:, 0:16], ta[:, 16:32], ALU.add))
                    dve.wait_ge(rstd_ready, t + 1)
                    dve.tensor_scalar(k.cq[:, t, :], ps[:, b, 0:QR], rs[:, 0:1], None, ALU.mult)
                    dve.tensor_scalar(k.ckv[:, t, :], ps[:, b, QR:QR + KVR], rs[:, 1:2], None, ALU.mult)\
                       .then_inc(unit_taken, 1)
                elif c == CH_UV:
                    dve.wait_ge(act_part, 2 * NT + t + 1)
                    link(dve.bn_stats(stat[:], ps[:, b, SW:2 * SW]))
                    dve.bn_aggr(mv[:], stat[:]).then_inc(var_ready, 1)
                    dve.wait_ge(rstd_ready, NT + t + 1)
                    dve.tensor_scalar(ta[:, 0:SW], ps[:, b, SW:2 * SW], mv[:, 0:1], rs[:, 0:1], ALU.subtract, ALU.mult)\
                       .then_inc(unit_taken, 1)
                    dve.wait_ge(unit_taken, u + 1)
                    link(dve.tensor_tensor(tb[:, 0:SW], ta[:, 0:SW], gsg[:], ALU.mult))
                    link(dve.tensor_tensor(k.sv[:, t, :], tb[:, 0:SW], bsg[:], ALU.add))
                else:
                    dve.wait_ge(act_part, 3 * NT + 2 * t + 2)
                    dve.scalar_tensor_tensor(k.sg[:, t, :], xraw[:, t % 2, 0:RW], 1.0, ps[:, b, RW:2 * RW], ALU.add, ALU.mult)\
                       .then_inc(unit_taken, 1)

        @block.gpsimd
        def _(pool):
            chain = [0]

            def link(ins):
                chain[0] += 1
                ins.then_inc(pool_chain, 1)
                pool.wait_ge(pool_chain, chain[0])

            link(pool.memset(halfs[:], -0.5))
            for t in range(NT):
                pool.wait_ge(act_part, 2 * t + 2)
                link(pool.tensor_scalar(ssq[:, t, 0:1], ssq[:, t, 0:1], 1.0 / QR, EPS, ALU.mult, ALU.add))
                link(pool.tensor_scalar(ssq[:, t, 1:2], ssq[:, t, 1:2], 1.0 / KVR, EPS, ALU.mult, ALU.add))
                if t:
                    pool.wait_ge(unit_taken, NT + t)
                pool.tensor_tensor(rs[:], ssq[:, t, :], halfs[:], ALU.pow).then_inc(rstd_ready, 1)
            for t in range(NT):
                pool.wait_ge(var_ready, t + 1)
                link(pool.tensor_scalar(mv[:, 1:2], mv[:, 1:2], EPS, None, ALU.add))
                pool.wait_ge(unit_taken, 2 * NT + t)
                pool.tensor_tensor(rs[:, 0:1], mv[:, 1:2], halfs[:, 0:1], ALU.pow).then_inc(rstd_ready, 1)


def prepare(nc, k):
    at, A, cst = k.at, k.dram, k.cst
    lat = at("lat_T", 185, [P, 2, QR + KVR])
    qkt = at("qk_T", 188, [P, 2, 4 * P])
    wuq, wukv, wsg, sgb = k.wuq, k.wukv, k.wsg, k.sgb
    sc = at("ret_scores", 204, [P, RH, P])
    qdt = at("ret_qd", 206, [P, 2 * P])
    mv4 = at("ret_mv", 10.25, [P, RH, 2])
    st4 = at("ret_stat", 10.375, [P, RH, 6])
    rs4 = at("ret_rstd", 10.5, [P, RH])
    half4 = at("ret_half", 10.5625, [P, RH])
    ve4 = at("ret_var", 10.625, [P, RH])
    state = at("ret_state", 10.75, [P, 2, 2 * RD])
    qtok = at("q_tok", 89, [P, 2, MH, MQ])
    ta = at("mla_rope_a", 95, [P, MH, ROPE])
    tb = at("mla_rope_b", 96, [P, MH, ROPE])
    kd = at("ret_kd", 97, [P, 2, RH, RD])
    on = at("ret_on", 99, [P, RH, RD])
    ident = cst[:, C_ID:C_ID + P]
    HD = 4 * MQ

    state_zeroed = k.sem("state_zeroed")
    lat_t = k.sem("lat_t")
    qk_t = k.sem("qk_t")
    v_sum = k.sem("v_sum")
    q_sum = k.sem("q_sum")
    sc_sum = k.sem("sc_sum")
    kv_sum = k.sem("kv_sum")
    out_sum = k.sem("out_sum")
    kn_sum = k.sem("kn_sum")
    q_t = k.sem("q_t")
    lat_copied = k.sem("lat_copied")
    qk_copied = k.sem("qk_copied")
    v_copied = k.sem("v_copied")
    qn_copied = k.sem("qn_copied")
    kn_copied = k.sem("kn_copied")
    qT_copied = k.sem("qT_copied")
    kr_copied = k.sem("kr_copied")
    qd_made = k.sem("qd_made")
    sc_decayed = k.sem("sc_decayed")
    q_rotated = k.sem("q_rotated")
    var_ready = k.sem("var_ready2")
    rstd_ready = k.sem("rstd_ready2")
    out_taken = k.sem("out_taken")
    state_made = k.sem("state_made")
    kd_made = k.sem("kd_made")
    dve_chain = k.sem("chain2")
    pool_chain = k.sem("pool_chain2")
    with nc.psum_tensor("banks2", [P, 8, 512], f32) as ps, \
            nc.Block() as block:

        @block.tensor
        def _(pe):
            def latents_T(t):
                if t:
                    pe.wait_ge(kr_copied, t)
                pe.transpose(ps[:, 0, 0:P], k.cq[:, t, 0:P], ident)
                pe.transpose(ps[:, 0, P:2 * P], k.cq[:, t, P:2 * P], ident)
                pe.transpose(ps[:, 0, 2 * P:3 * P], k.ckv[:, t, :], ident)
                pe.transpose(ps[0:ROPE, 0, 3 * P:4 * P], k.kr[:, t, :], ident).then_inc(lat_t, 1)

            def ret_T(t):
                if t:
                    pe.wait_ge(qk_copied, t)
                for j in range(4):
                    last = pe.transpose(ps[:, 1, j * P:(j + 1) * P], k.qk[:, t, j * P:(j + 1) * P], ident)
                last.then_inc(qk_t, 1)

            latents_T(0)
            ret_T(0)
            for t in range(NT):
                b = t % 2
                if t == 0:
                    pe.wait_ge(state_zeroed, 1)
                    pe.wait_ge(k.up_ready, 3)
                pe.wait_ge(lat_copied, t + 1)
                if t:
                    pe.wait_ge(v_copied, t)
                pe.matmul(ps[:, 2, :], lat[:, b, QR:QR + KVR], wukv[:, MW:2 * MW], start=True, stop=True).then_inc(v_sum, 1)
                if t:
                    pe.wait_ge(qT_copied, 2 * t)
                for j in range(2):
                    for s in range(QR // P):
                        last = pe.matmul(ps[:, 3 + j, 0:HD], lat[:, b, s * P:(s + 1) * P],
                                         wuq[:, s, j * HD:(j + 1) * HD], start=(s == 0), stop=(s == QR // P - 1))
                last.then_inc(q_sum, 1)
                pe.wait_ge(qk_copied, t + 1)
                if t:
                    pe.wait_ge(kn_copied, 2 * t)
                    pe.wait_ge(state_made, t)
                for h in (0, 2, 1, 3):
                    r = slice(RD * (h % 2), RD * (h % 2) + RD)
                    q, kk = (qkt[r, b, (j + h // 2) * P:(j + h // 2 + 1) * P] for j in (0, 2))
                    o = ps[:, 5 + h % 2, (h % 2) * 2 * P + (h // 2) * P:(h % 2) * 2 * P + (h // 2 + 1) * P]
                    last = pe.matmul(o, kk, q, start=True, stop=True)
                last.then_inc(sc_sum, 1)
                if t:
                    pe.wait_ge(out_taken, t)
                for g in range(SG):
                    pe.matmul(ps[:, 7, RW + g * SD:RW + (g + 1) * SD], wsg[:, g, :],
                              k.sv[:, t, g * SD:(g + 1) * SD], start=True, stop=True)
                pe.wait_ge(sc_decayed, t + 1)
                pe.wait_ge(qd_made, t + 1)
                for j in range(2):
                    pe.matmul(ps[:, 7, j * P:(j + 1) * P], qdt[:, j * P:(j + 1) * P], state[:, j, :], start=True, stop=False)
                    for h in (2 * j, 2 * j + 1):
                        last = pe.matmul(ps[:, 7, h * RD:(h + 1) * RD], sc[:, h, :], k.rv[:, t, h * RD:(h + 1) * RD],
                                         start=False, stop=(h == 2 * j + 1))
                last.then_inc(out_sum, 1)
                pe.wait_ge(kd_made, t + 1)
                for j in range(2):
                    last = pe.matmul(ps[:, 6, j * P:(j + 1) * P],
                                     kd[:, b, 2 * j:2 * j + 2, :].rearrange("p h d -> p (h d)"),
                                     k.rv[:, t, j * P:(j + 1) * P], start=True, stop=True)
                last.then_inc(kv_sum, 1)
                if t + 1 < NT:
                    latents_T(t + 1)
                    ret_T(t + 1)
                for j in range(4):
                    last = pe.matmul(ps[:, 5, j * P:(j + 1) * P], wukv[:, j * P:(j + 1) * P],
                                     lat[:, b, QR:QR + KVR], start=True, stop=True)
                last.then_inc(kn_sum, 1)
                pe.wait_ge(q_rotated, t + 1)
                for h in range(MH):
                    last = pe.transpose(ps[0:MQ, 3 + h // 4, (h % 4) * P:(h % 4 + 1) * P], qtok[:, b, h, :], ident)
                last.then_inc(q_t, 1)

        @block.scalar
        def _(act):
            def copy_latents(t):
                act.wait_ge(lat_t, t + 1)
                act.activation(lat[:, t % 2, :], ps[:, 0, 0:QR + KVR], ACT.Copy).then_inc(lat_copied, 1)
                act.wait_ge(qk_t, t + 1)
                if t >= 2:
                    act.wait_ge(qd_made, t - 1)
                act.activation(qkt[:, t % 2, :], ps[:, 1, :], ACT.Copy).then_inc(qk_copied, 1)

            copy_latents(0)
            for t in range(NT):
                tok = slice(t * P, (t + 1) * P)
                act.wait_ge(v_sum, t + 1)
                act.activation(k.v[:, t, :], ps[:, 2, :], ACT.Copy).then_inc(v_copied, 1)
                act.wait_ge(q_sum, t + 1)
                act.activation(qtok[:, t % 2, :, 0:NOPE].rearrange("p (j h) d -> p j h d", j=2),
                               ps[:, 3:5, 0:HD].rearrange("p j (h d) -> p j h d", d=MQ)[:, :, :, 0:NOPE], ACT.Copy)\
                   .then_inc(qn_copied, 1)
                act.wait_ge(kn_sum, t + 1)
                for j in range(2):
                    act.activation(k.kT[0:NOPE, j:MH:2, tok],
                                   ps[NOPE * j:NOPE * (j + 1), 5, :].rearrange("p (h t) -> p h t", t=P), ACT.Copy)\
                       .then_inc(kn_copied, 1)
                if t + 1 < NT:
                    copy_latents(t + 1)
                act.wait_ge(q_t, t + 1)
                for j in range(2):
                    act.activation(k.qT[0:MQ, 4 * j:4 * j + 4, tok],
                                   ps[0:MQ, 3 + j, :].rearrange("p (h t) -> p h t", t=P), ACT.Copy, scale=MLA_SCALE)\
                       .then_inc(qT_copied, 1)

        @block.vector
        def _(dve):
            chain = [0]

            def link(ins):
                chain[0] += 1
                ins.then_inc(dve_chain, 1)
                dve.wait_ge(dve_chain, chain[0])

            dve.memset(state[:], 0.0).then_inc(state_zeroed, 1)
            for t in range(NT):
                b = t % 2
                tok = slice(t * P, (t + 1) * P)
                dve.wait_ge(lat_copied, t + 1)
                dve.tensor_copy(k.kT[NOPE:MQ, :, tok], over(ps[0:ROPE, 0:1, 3 * P:4 * P], [ROPE, MH, P]))\
                   .then_inc(kr_copied, 1)
                dve.wait_ge(qk_copied, t + 1)
                if t:
                    dve.wait_ge(out_sum, t)
                dve.tensor_tensor(qdt[:], qkt[:, b, 0:2 * P], cst[:, C_QDEC:C_QDEC + 2 * P], ALU.mult).then_inc(qd_made, 1)
                dve.wait_ge(sc_sum, t + 1)
                decay = cst[:, C_DEC:C_DEC + RH * P].rearrange("p (h n) -> p h n", n=P)
                for j in range(2):
                    last = dve.tensor_tensor(sc[:, j:RH:2, :], ps[:, 5 + j, 2 * P * j:2 * P * (j + 1)].rearrange("p (h n) -> p h n", n=P),
                                             decay[:, j:RH:2, :], ALU.mult)
                last.then_inc(sc_decayed, 1)
                dve.wait_ge(qn_copied, t + 1)
                x = ps[:, 3:5, 0:HD].rearrange("p j (h d) -> p j h d", d=MQ)[:, :, :, NOPE:MQ]
                for j in range(2):
                    cb, sb_ = (over(z[:, t:t + 1, 32:64], [P, 4, ROPE]) for z in (k.cos, k.sin))
                    dve.tensor_tensor(ta[:, 4 * j:4 * j + 4, :], x[:, j], cb, ALU.mult)
                    last = dve.tensor_tensor(tb[:, 4 * j:4 * j + 4, :], x[:, j], sb_, ALU.mult)
                link(last)
                if t >= 2:
                    dve.wait_ge(q_t, t - 1)
                dve.tensor_tensor(qtok[:, b, :, NOPE:NOPE + 16], ta[:, :, 0:16], tb[:, :, 16:32], ALU.subtract)
                dve.tensor_tensor(qtok[:, b, :, NOPE + 16:MQ], tb[:, :, 0:16], ta[:, :, 16:32], ALU.add).then_inc(q_rotated, 1)
                dve.wait_ge(out_sum, t + 1)
                for h in range(RH):
                    last = dve.bn_stats(st4[:, h, :], ps[:, 7, h * RD:(h + 1) * RD])
                link(last)
                for h in range(RH):
                    last = dve.bn_aggr(mv4[:, h, :], st4[:, h, :])
                last.then_inc(var_ready, 1)
                for g in range(SG):
                    dve.scalar_tensor_tensor(k.mixA[:, t, RW + g * SD:RW + (g + 1) * SD], ps[:, 7, RW + g * SD:RW + (g + 1) * SD],
                                             sgb[:, g:g + 1], k.su[:, t, g * SD:(g + 1) * SD], ALU.add, ALU.mult)
                dve.wait_ge(kv_sum, t + 1)
                for h in range(RH):
                    r = slice(RD * (h % 2), RD * (h % 2) + RD)
                    blk = ps[r, 6, (h // 2) * P + RD * (h % 2):(h // 2) * P + RD * (h % 2) + RD]
                    st = state[r, h // 2, r]
                    last = dve.scalar_tensor_tensor(st, st, cst[r, C_ST + h // 2:C_ST + h // 2 + 1], blk, ALU.mult, ALU.add)
                last.then_inc(state_made, 1)
                dve.wait_ge(rstd_ready, t + 1)
                for h in range(RH):
                    last = dve.tensor_scalar(on[:, h, :], ps[:, 7, h * RD:(h + 1) * RD], mv4[:, h, 0:1], rs4[:, h:h + 1],
                                             ALU.subtract, ALU.mult)
                last.then_inc(out_taken, 1)
                dve.wait_ge(out_taken, t + 1)
                link(dve.scalar_tensor_tensor(k.mixA[:, t, 0:RW], on[:].rearrange("p h d -> p (h d)"), 0.5, k.sg[:, t, :],
                                              ALU.mult, ALU.mult))

        @block.gpsimd
        def _(pool):
            chain = [0]

            def link(ins):
                chain[0] += 1
                ins.then_inc(pool_chain, 1)
                pool.wait_ge(pool_chain, chain[0])

            link(pool.memset(half4[:], -0.5))
            for t in range(NT):
                if t >= 2:
                    pool.wait_ge(kv_sum, t - 1)
                pool.tensor_tensor(kd[:, t % 2].rearrange("p h d -> p (h d)"), k.qk[:, t, RW:2 * RW],
                                   cst[:, C_INNER:C_INNER + RW], ALU.mult).then_inc(kd_made, 1)
                pool.wait_ge(var_ready, t + 1)
                link(pool.tensor_scalar(ve4[:, :, None], mv4[:, :, 1:2], EPS, None, ALU.add))
                if t:
                    pool.wait_ge(out_taken, t)
                pool.tensor_tensor(rs4[:], ve4[:], half4[:], ALU.pow).then_inc(rstd_ready, 1)


def attend(nc, k):
    at, A, cst = k.at, k.dram, k.cst
    prob = at("prob", 12, [P, 2, S])
    probT = at("prob_T", 20, [P, 2, S])
    nmx = at("neg_max", 28, [P, 2])
    rsum = at("row_sum", 28.0625, [P, NT, MH])
    rinv = at("row_inv", 28.5, [P, NT, MH])
    zeros = at("zeros", 185, [P, D + NE])
    ident = cst[:, C_ID:C_ID + P]
    units = [(i, h) for i in range(NT) for h in range(MH)]

    scored = k.sem("scored")
    max_ready = k.sem("max_ready")
    exps = k.sem("exps")
    p_t = k.sem("p_t")
    pT_copied = k.sem("pT_copied")
    pT_copied_act = k.sem("pT_copied_act")
    pv_done = k.sem("pv_done")
    o_taken = k.sem("o_taken")
    dve_chain, zeroed = k.sem("chain3"), k.sem("zeroed")
    with nc.psum_tensor("s_ps", [P, 2, 2, 512], f32) as sps, \
            nc.psum_tensor("t_ps", [P, 2, 512], f32) as tps, \
            nc.psum_tensor("o_ps", [P, 2, 512], f32) as ops, \
            nc.Block() as block:

        @block.sync
        def _(sp):
            for s in range(KD):
                sp.dma_start(k.w_out_raw[:, s, :], A["w_out"][s * P:(s + 1) * P, :]).then_inc(k.w_out_loaded, 16)
            sp.wait_ge(zeroed, 1)
            for t in range(NT + 2):
                sp.dma_start(k.y_dram[t * P:(t + 1) * P, :], zeros[:, 0:D]).then_inc(k.rows_zeroed, 16)
            for t in (NT, NT + 1):
                sp.dma_start(k.x2_dram[t * P:(t + 1) * P, :], zeros[:]).then_inc(k.rows_zeroed, 16)

        def halves(i):
            n = i + 1
            return [(0, min(n, 4))] + ([(4, n)] if n > 4 else [])

        second = [0]
        for i, h in units:
            second.append(second[-1] + (i >= 4))

        @block.tensor
        def _(pe):
            def scores(u):
                i, h = units[u]
                if u >= 2:
                    pe.wait_ge(exps, u - 1)
                q = k.qT[0:MQ, h, i * P:(i + 1) * P]
                for j, (a, z) in enumerate(halves(i)):
                    last = pe.matmul(sps[:, u % 2, j, 0:(z - a) * P], q, k.kT[0:MQ, h, a * P:z * P], start=True, stop=True)
                last.then_inc(scored, 1)

            def turn(u):
                i, h = units[u]
                pe.wait_ge(exps, u + 1)
                for j, (a, z) in enumerate(halves(i)):
                    if j == 0 and u:
                        pe.wait_ge(pT_copied, u)
                    if j == 1 and second[u]:
                        pe.wait_ge(pT_copied_act, second[u])
                    for m in range(a, z):
                        last = pe.transpose(tps[:, j, (m - a) * P:(m - a + 1) * P], prob[:, u % 2, m * P:(m + 1) * P], ident)
                    last.then_inc(p_t, 1)

            def values(u):
                i, h = units[u]
                pe.wait_ge(pT_copied, u + 1)
                if i >= 4:
                    pe.wait_ge(pT_copied_act, second[u + 1])
                if h == 0 and i >= 2:
                    pe.wait_ge(o_taken, i - 1)
                for m in range(i + 1):
                    last = pe.matmul(ops[:, i % 2, h * MV:(h + 1) * MV], probT[:, u % 2, m * P:(m + 1) * P],
                                     k.v[:, m, h * MV:(h + 1) * MV], start=(m == 0), stop=(m == i))
                last.then_inc(pv_done, 1)

            n = len(units)
            for u in range(n + 2):
                if u < n:
                    scores(u)
                if 0 <= u - 2:
                    values(u - 2)
                if 0 <= u - 1 < n:
                    turn(u - 1)

        @block.scalar
        def _(act):
            for u in range(len(units) + 1):
                if u < len(units):
                    i, h = units[u]
                    act.wait_ge(max_ready, u + 1)
                    if u >= 2:
                        act.wait_ge(p_t, u - 1 + second[u - 1])
                    src = sps[:, u % 2].rearrange("p j n -> p (j n)")
                    act.activation(prob[:, u % 2, 0:(i + 1) * P], src[:, 0:(i + 1) * P], ACT.Exp,
                                   bias=nmx[:, u % 2:u % 2 + 1], accum_out=rsum[:, i, h:h + 1]).then_inc(exps, 1)
                if u >= 1 and units[u - 1][0] >= 4:
                    v = u - 1
                    i = units[v][0]
                    act.wait_ge(p_t, v + 1 + second[v + 1])
                    if v >= 2:
                        act.wait_ge(pv_done, v - 1)
                    act.activation(probT[:, v % 2, 4 * P:(i + 1) * P], tps[:, 1, 0:(i - 3) * P], ACT.Copy)\
                       .then_inc(pT_copied_act, 1)

        @block.vector
        def _(dve):
            chain = [0]

            def link(ins):
                chain[0] += 1
                ins.then_inc(dve_chain, 1)
                dve.wait_ge(dve_chain, chain[0])

            def take(i):
                dve.wait_ge(pv_done, (i + 1) * MH)
                link(dve.reciprocal(rinv[:, i, :], rsum[:, i, :]))
                dve.tensor_tensor(k.mixB[:, i, :].rearrange("p (h d) -> p h d", d=MV),
                                  ops[:, i % 2, :].rearrange("p (h d) -> p h d", d=MV),
                                  over(rinv[:, i, :, None], [P, MH, MV]), ALU.mult).then_inc(o_taken, 1)

            for u in range(len(units) + 1):
                if u < len(units):
                    i, h = units[u]
                    dve.wait_ge(scored, u + 1)
                    s = sps[:, u % 2].rearrange("p j n -> p (j n)")
                    d = s[:, i * P:(i + 1) * P]
                    link(dve.tensor_tensor(d, d, cst[:, C_MASK:C_MASK + P], ALU.add))
                    if u >= 2:
                        dve.wait_ge(exps, u - 1)
                    dve.tensor_reduce(nmx[:, u % 2:u % 2 + 1], s[:, 0:(i + 1) * P], AX.X, ALU.max, negate=True).then_inc(max_ready, 1)
                if u >= 1:
                    v = u - 1
                    i = units[v][0]
                    n = min(i + 1, 4) * P
                    dve.wait_ge(p_t, v + 1 + second[v])
                    if v >= 2:
                        dve.wait_ge(pv_done, v - 1)
                    dve.tensor_copy(probT[:, v % 2, 0:n], tps[:, 0, 0:n]).then_inc(pT_copied, 1)
                    if v >= MH and v % MH == 1:
                        take(v // MH - 1)
            take(NT - 1)

        @block.gpsimd
        def _(pool):
            pool.memset(zeros[:], 0.0).then_inc(zeroed, 1)


def mix_out(nc, k):
    at, A, cst = k.at, k.dram, k.cst
    mhi = at("mixT_hi", 12, [P, 2, KD, P], f32r)
    mlo = at("mixT_lo", 20, [P, 2, KD, P], f32r)
    wraw = k.w_out_raw
    whi = at("wo_hi", 105, [P, KD, D], f32r)
    wlo = at("wo_lo", 137, [P, KD, D], f32r)
    g = at("ln1_g", 62, [P, D])
    b = at("ln1_b", 66, [P, D])
    st = at("ln1_st", 201, [P, 2, 6])
    mv = at("ln1_mv", 201.125, [P, 2, 2])
    rs = at("ln1_rs", 201.25, [P, 2])
    half = at("ln1_half", 201.375, [P, 1])
    ident = cst[:, C_ID:C_ID + P]
    x1 = k.x1
    tmp = at("ln1_tmp", 201.5, [P, D])
    memT = at("memT", 73, [P, KD, MEM])
    rawq = at("wq_raw", 89, [P, KD, XW])
    q_hi, mem_loaded, q_loaded = k.sem("wq_hi_done"), k.sem("mem_loaded"), k.sem("wq_loaded")
    kv_sum, kv_taken = k.sem("xkv_sum"), k.sem("xkv_taken")
    loaded = k.sem("x_gains_loaded")
    w_hi, w_lo = k.sem("wo_hi_done"), k.sem("wo_lo_done")
    mix_t, m_hi, m_lo = k.sem("mix_t"), k.sem("mix_hi"), k.sem("mix_lo")
    summed, taken = k.sem("mix_summed"), k.sem("mix_taken")
    var_ready, rstd_ready = k.sem("ln1_var"), k.sem("ln1_rstd")
    dve_chain, pool_chain = k.sem("chain4"), k.sem("pool_chain4")
    with nc.psum_tensor("mixT_ps", [P, 2, 2, 512], f32) as tps, \
            nc.psum_tensor("mix_acc", [P, 2, 2, 512], f32) as acc, \
            nc.Block() as block:

        @block.sync
        def _(sp):
            for t in range(NT):
                sp.dma_start(x1[:, t, :], A["x"][t * P:(t + 1) * P, :]).then_inc(loaded, 16)
            sp.dma_start(g[:], over(A["ln_mix_g"], [P, D])).then_inc(loaded, 16)
            sp.dma_start(b[:], over(A["ln_mix_b"], [P, D])).then_inc(loaded, 16)
            sp.wait_ge(w_lo, KD)
            for s in range(KD):
                sp.dma_start(k.wk[:, s, :], A["xa_wk"][s * P:(s + 1) * P, :]).then_inc(k.kv_loaded, 16)
                sp.dma_start(k.wv[:, s, :], A["xa_wv"][s * P:(s + 1) * P, :]).then_inc(k.kv_loaded, 16)
            sp.wait_ge(mix_t, 4)
            sp.dma_start(memT[:], A["memT"].rearrange("(s p) n -> p s n", p=P)).then_inc(mem_loaded, 16)
            sp.wait_ge(mix_t, NT)
            sp.dma_start(rawq[:], A["xa_wq"].rearrange("(s p) n -> p s n", p=P)).then_inc(q_loaded, 16)

        @block.tensor
        def _(pe):
            def turn(t):
                if t >= 2:
                    pe.wait_ge(m_lo, t - 1)
                for j in range(KD):
                    src = k.mixA if j < 4 else k.mixB
                    last = pe.transpose(tps[:, t % 2, j // 4, (j % 4) * P:(j % 4 + 1) * P],
                                        src[:, t, (j % 4) * P:(j % 4 + 1) * P], ident)
                last.then_inc(mix_t, 1)

            turn(0)
            for t in range(NT):
                if t + 1 < NT:
                    turn(t + 1)
                pe.wait_ge(m_lo, t + 1)
                if t >= 2:
                    pe.wait_ge(taken, t - 1)
                for s in range(KD):
                    if t == 0:
                        pe.wait_ge(w_lo, s + 1)
                    hi, lo = mhi[:, t % 2, s, :], mlo[:, t % 2, s, :]
                    for j in range(2):
                        o, c = acc[:, t % 2, j, :], slice(512 * j, 512 * j + 512)
                        pe.matmul(o, hi, whi[:, s, c], start=(s == 0), stop=False)
                        pe.matmul(o, hi, wlo[:, s, c], start=False, stop=False)
                        last = pe.matmul(o, lo, whi[:, s, c], start=False, stop=(s == KD - 1))
                last.then_inc(summed, 1)
            pe.wait_ge(mem_loaded, 16)
            pe.wait_ge(k.kv_loaded, 16 * 2 * KD)
            for u in range(6):
                if u >= 4:
                    pe.wait_ge(kv_taken, u - 3)
                bank = tps[:, (u % 4) // 2, u % 2, :]
                for s in range(KD):
                    if u < XH:
                        o, l, r = bank[:, 0:MEM], k.wk[:, s, u * XD:(u + 1) * XD], memT[:, s, :]
                    else:
                        o, l, r = bank, memT[:, s, (u - XH) * P:(u - XH + 1) * P], k.wv[:, s, :]
                    last = pe.matmul(o, l, r, start=(s == 0), stop=(s == KD - 1))
                last.then_inc(kv_sum, 1)

        @block.scalar
        def _(act):
            for t in range(NT):
                if t == 1:
                    act.wait_ge(k.w_out_loaded, 16 * KD)
                    for s in range(KD):
                        act.activation(whi[:, s, :], wraw[:, s, :], ACT.Copy).then_inc(w_hi, 1)
                act.wait_ge(mix_t, t + 1)
                if t >= 2:
                    act.wait_ge(summed, t - 1)
                act.activation(mhi[:, t % 2].rearrange("p s c -> p (s c)"), tps[:, t % 2].rearrange("p j c -> p (j c)"), ACT.Copy)\
                   .then_inc(m_hi, 1)
            act.wait_ge(q_loaded, 16)
            act.wait_ge(summed, NT)
            for s in range(KD):
                act.activation(k.wq_hi[:, s, :], rawq[:, s, :], ACT.Copy).then_inc(q_hi, 1)

        @block.vector
        def _(dve):
            chain = [0]

            def link(ins):
                chain[0] += 1
                ins.then_inc(dve_chain, 1)
                dve.wait_ge(dve_chain, chain[0])

            def rest(t):
                dve.wait_ge(m_hi, t + 1)
                dve.tensor_tensor(mlo[:, t % 2].rearrange("p s c -> p (s c)"), tps[:, t % 2].rearrange("p j c -> p (j c)"),
                                  mhi[:, t % 2].rearrange("p s c -> p (s c)").bitcast(f32), ALU.subtract).then_inc(m_lo, 1)

            def norm(t):
                dve.wait_ge(rstd_ready, t + 1)
                link(dve.scalar_tensor_tensor(tmp[:], x1[:, t, :], mv[:, t % 2, 0:1], g[:], ALU.subtract, ALU.mult))
                link(dve.scalar_tensor_tensor(x1[:, t, :], tmp[:], rs[:, t % 2:t % 2 + 1], b[:], ALU.mult, ALU.add))

            def take(u):
                dve.wait_ge(kv_sum, u + 1)
                bank = tps[:, (u % 4) // 2, u % 2, :]
                if u < XH:
                    dve.tensor_copy(k.xkT[:, u, :], bank[:, 0:MEM]).then_inc(kv_taken, 1)
                else:
                    dve.tensor_copy(k.xv[:, u - XH, :], bank).then_inc(kv_taken, 1)

            rest(0)
            for s in range(KD):
                dve.wait_ge(w_hi, s + 1)
                dve.tensor_tensor(wlo[:, s, :], wraw[:, s, :], whi[:, s, :].bitcast(f32), ALU.subtract).then_inc(w_lo, 1)
            dve.wait_ge(loaded, 160)
            for t in range(NT):
                if t + 1 < NT:
                    rest(t + 1)
                dve.wait_ge(summed, t + 1)
                dve.scalar_tensor_tensor(x1[:, t, :], x1[:, t, :], ALPHA, acc[:, t % 2].rearrange("p j c -> p (j c)"), ALU.mult, ALU.add)\
                   .then_inc(taken, 1)
                dve.wait_ge(taken, t + 1)
                for j in range(2):
                    last = dve.bn_stats(st[:, j, :], x1[:, t, 512 * j:512 * j + 512])
                link(last)
                dve.bn_aggr(mv[:, t % 2, :], st[:].rearrange("p j c -> p (j c)")).then_inc(var_ready, 1)
                if t:
                    norm(t - 1)
            norm(NT - 1)
            for s in range(KD):
                dve.wait_ge(q_hi, s + 1)
                dve.tensor_tensor(k.wq_lo[:, s, :], rawq[:, s, :], k.wq_hi[:, s, :].bitcast(f32), ALU.subtract)
            for u in range(6):
                take(u)

        @block.gpsimd
        def _(pool):
            chain = [0]

            def link(ins):
                chain[0] += 1
                ins.then_inc(pool_chain, 1)
                pool.wait_ge(pool_chain, chain[0])

            link(pool.memset(half[:], -0.5))
            for t in range(NT):
                pool.wait_ge(var_ready, t + 1)
                link(pool.tensor_scalar(mv[:, t % 2, 1:2], mv[:, t % 2, 1:2], EPS, None, ALU.add))
                pool.tensor_tensor(rs[:, t % 2:t % 2 + 1], mv[:, t % 2, 1:2], half[:], ALU.pow).then_inc(rstd_ready, 1)


def cross_attend(nc, k):
    at, A, cst = k.at, k.dram, k.cst
    g = at("ln2_g", 30, [P, D])
    b = at("ln2_b", 34, [P, D])
    xhi = at("x1T_hi", 38, [P, KD, P], f32r)
    xlo = at("x1T_lo", 42, [P, KD, P], f32r)
    qtok = at("xq_tok", 54, [P, XW])
    qT = at("xqT", 56, [P, XH, P])
    prob = at("xprob", 58, [P, XH, MEM])
    probT = at("xprobT", 62, [P, XH * 2, P])
    ohi = at("xoT_hi", 66, [P, XH, P], f32r)
    olo = at("xoT_lo", 68, [P, XH, P], f32r)
    x2T = at("x2T", 46, [P, KD, P])
    rw = at("router_w", 50, [P, KD, NE])
    tmp = at("ln2_tmp", 89, [P, D])
    rawo = at("xwo_raw", 73, [P, XH, D])
    o_loaded, w_hi, w_lo = k.sem("xwo_loaded"), k.sem("xwo_hi_done"), k.sem("xwo_lo_done")
    rw_loaded, x2_t, x2_copied, logit, lg_copied = (k.sem(n) for n in ("rw_loaded", "x2_t", "x2_copied", "logit", "lg_copied"))
    st = at("ln2_st", 201, [P, 2, 6])
    mv = at("ln2_mv", 201.125, [P, 2, 2])
    rs = at("ln2_rs", 201.25, [P, 2])
    half = at("ln2_half", 201.375, [P, 1])
    nmx = at("xneg_max", 201.5, [P, XH])
    rsum = at("xrow_sum", 201.5625, [P, XH])
    rinv = at("xrow_inv", 201.625, [P, XH])
    ident = cst[:, C_ID:C_ID + P]
    x1 = k.x1
    loaded = k.sem("gains6_loaded")
    x_t, x_hi, x_lo = k.sem("x1_t"), k.sem("x1_hi"), k.sem("x1_lo")
    q_sum, q_taken, q_t, qT_taken = k.sem("xq_sum"), k.sem("xq_taken"), k.sem("xq_t"), k.sem("xqT_taken")
    scored, maxed, exps, scaled = k.sem("xscored"), k.sem("xmaxed"), k.sem("xexps"), k.sem("xscaled")
    p_t, pT_taken = k.sem("xp_t"), k.sem("xpT_taken")
    o_sum, o_hi, o_lo = k.sem("xo_sum"), k.sem("xo_hi"), k.sem("xo_lo")
    summed, taken = k.sem("xsummed"), k.sem("xtaken")
    var_ready, rstd_ready = k.sem("ln2_var"), k.sem("ln2_rstd")
    x2_made = k.sem("x2_made")
    dve_chain, pool_chain, stored = k.sem("chain6"), k.sem("pool_chain6"), k.x2_stored
    flat = "p j c -> p (j c)"
    with nc.psum_tensor("x_tps", [P, 2, 512], f32) as tps, nc.psum_tensor("x_qps", [P, 512], f32) as qps, \
            nc.psum_tensor("x_sps", [P, 2, 512], f32) as sps, nc.psum_tensor("x_ops", [P, 512], f32) as ops, \
            nc.psum_tensor("x_acc", [P, 2, 512], f32) as acc, nc.Block() as block:

        @block.sync
        def _(sp):
            for s in range(XH):
                sp.dma_start(rawo[:, s, :], A["xa_wo"][s * P:(s + 1) * P, :]).then_inc(o_loaded, 16)
            sp.dma_start(rw[:], A["router_w"].rearrange("(s p) e -> p s e", p=P)).then_inc(rw_loaded, 16)
            sp.dma_start(g[:], over(A["ln_xa_g"], [P, D])).then_inc(loaded, 16)
            sp.dma_start(b[:], over(A["ln_xa_b"], [P, D])).then_inc(loaded, 16)
            for t in range(NT):
                sp.wait_ge(x2_made, t + 1)
                sp.dma_start(k.x2_dram[t * P:(t + 1) * P, 0:D], x1[:, t, :]).then_inc(stored, 16)

        @block.tensor
        def _(pe):
            def turn(t):
                if t >= 2:
                    pe.wait_ge(pT_taken, t - 1)
                if t >= 4:
                    pe.wait_ge(x2_copied, t - 3)
                for j in range(KD):
                    last = pe.transpose(tps[:, j // 4, (j % 4) * P:(j % 4 + 1) * P], x1[:, t, j * P:(j + 1) * P], ident)
                last.then_inc(x_t, 1)

            def queries(t):
                pe.wait_ge(x_lo, t + 1)
                if t:
                    pe.wait_ge(qT_taken, t)
                if t >= 4:
                    pe.wait_ge(lg_copied, t - 3)
                for s in range(KD):
                    pe.matmul(qps[:], xhi[:, s, :], k.wq_hi[:, s, :], start=(s == 0), stop=False)
                    pe.matmul(qps[:], xhi[:, s, :], k.wq_lo[:, s, :], start=False, stop=False)
                    last = pe.matmul(qps[:], xlo[:, s, :], k.wq_hi[:, s, :], start=False, stop=(s == KD - 1))
                last.then_inc(q_sum, 1)

            def turn_queries(t):
                pe.wait_ge(q_taken, t + 1)
                for h in range(XH):
                    last = pe.transpose(qps[:, h * P:(h + 1) * P], qtok[:, h * P:(h + 1) * P], ident)
                last.then_inc(q_t, 1)

            def scores(t):
                pe.wait_ge(qT_taken, t + 1)
                if t:
                    pe.wait_ge(exps, XH * t)
                for h in range(XH):
                    last = pe.matmul(sps[:, h // 2, (h % 2) * MEM:(h % 2 + 1) * MEM], qT[:, h, :], k.xkT[:, h, :], start=True, stop=True)
                last.then_inc(scored, 1)

            def turn_probs(t):
                pe.wait_ge(scaled, t + 1)
                pe.wait_ge(x_lo, t + 2 if t + 1 < NT else NT)
                for j in range(2 * XH):
                    last = pe.transpose(tps[:, j // 4, (j % 4) * P:(j % 4 + 1) * P],
                                        prob[:, j // 2, (j % 2) * P:(j % 2 + 1) * P], ident)
                last.then_inc(p_t, 1)

            def values(t):
                pe.wait_ge(pT_taken, t + 1)
                if t:
                    pe.wait_ge(o_lo, t)
                for h in range(XH):
                    for m in range(2):
                        last = pe.matmul(ops[:, h * P:(h + 1) * P], k.xv[:, m, h * XD:(h + 1) * XD], probT[:, 2 * h + m, :],
                                         start=(m == 0), stop=(m == 1))
                last.then_inc(o_sum, 1)

            def turn_x2(t):
                pe.wait_ge(x2_made, t + 1)
                if t > NT - 3:
                    pe.wait_ge(x2_copied, t)
                pe.wait_ge(pT_taken, min(NT, t + 3))
                for j in range(KD):
                    last = pe.transpose(tps[:, j // 4, (j % 4) * P:(j % 4 + 1) * P], x1[:, t, j * P:(j + 1) * P], ident)
                last.then_inc(x2_t, 1)

            def logits(t):
                pe.wait_ge(x2_copied, t + 1)
                if t == 0:
                    pe.wait_ge(rw_loaded, 16)
                pe.wait_ge(qT_taken, min(NT, t + 4))
                if t > NT - 4:
                    pe.wait_ge(lg_copied, t)
                for s in range(KD):
                    last = pe.matmul(qps[:, 0:NE], x2T[:, s, :], rw[:, s, :], start=(s == 0), stop=(s == KD - 1))
                last.then_inc(logit, 1)

            def outputs(t):
                pe.wait_ge(o_lo, t + 1)
                if t == 0:
                    pe.wait_ge(w_lo, XH)
                if t:
                    pe.wait_ge(taken, t)
                for s in range(XH):
                    for j in range(2):
                        o, c = acc[:, j, :], slice(512 * j, 512 * j + 512)
                        pe.matmul(o, ohi[:, s, :], k.xwo_hi[:, s, c], start=(s == 0), stop=False)
                        pe.matmul(o, ohi[:, s, :], k.xwo_lo[:, s, c], start=False, stop=False)
                        last = pe.matmul(o, olo[:, s, :], k.xwo_hi[:, s, c], start=False, stop=(s == XH - 1))
                last.then_inc(summed, 1)

            turn(0)
            for t in range(NT + 1):
                if t < NT:
                    queries(t)
                if t:
                    turn_probs(t - 1)
                if t < NT:
                    turn_queries(t)
                if t:
                    values(t - 1)
                if t >= 3:
                    turn_x2(t - 3)
                if t < NT:
                    scores(t)
                if t >= 3:
                    logits(t - 3)
                if t + 1 < NT:
                    turn(t + 1)
                if t:
                    outputs(t - 1)
            for t in (NT - 2, NT - 1):
                turn_x2(t)
                logits(t)

        @block.scalar
        def _(act):
            def x_high(t):
                act.wait_ge(x_t, t + 1)
                if t:
                    act.wait_ge(q_sum, t)
                act.activation(xhi[:].rearrange(flat), tps[:].rearrange(flat), ACT.Copy).then_inc(x_hi, 1)

            def copy_x2(t):
                act.wait_ge(x2_t, t + 1)
                if t:
                    act.wait_ge(logit, t)
                act.activation(x2T[:].rearrange("p s c -> p (s c)"), tps[:].rearrange(flat), ACT.Copy).then_inc(x2_copied, 1)

            x_high(0)
            for t in range(NT + 1):
                if t < NT:
                    act.wait_ge(q_sum, t + 1)
                    act.activation(qtok[:], qps[:], ACT.Copy, scale=XA_SCALE).then_inc(q_taken, 1)
                if t:
                    act.wait_ge(p_t, t)
                    if t >= 2:
                        act.wait_ge(o_sum, t - 1)
                    act.activation(probT[:].rearrange(flat), tps[:].rearrange(flat), ACT.Copy).then_inc(pT_taken, 1)
                if t < NT:
                    act.wait_ge(q_t, t + 1)
                    act.activation(qT[:].rearrange(flat), qps[:], ACT.Copy).then_inc(qT_taken, 1)
                if t:
                    act.wait_ge(o_sum, t)
                    if t >= 2:
                        act.wait_ge(summed, t - 1)
                    act.activation(ohi[:].rearrange(flat), ops[:], ACT.Copy).then_inc(o_hi, 1)
                if t >= 3:
                    copy_x2(t - 3)
                if t < NT:
                    act.wait_ge(maxed, t + 1)
                    if t:
                        act.wait_ge(p_t, t)
                    for h in range(XH):
                        act.activation(prob[:, h, :], sps[:, h // 2, (h % 2) * MEM:(h % 2 + 1) * MEM], ACT.Exp,
                                       bias=nmx[:, h:h + 1], accum_out=rsum[:, h:h + 1]).then_inc(exps, 1)
                if t + 1 < NT:
                    x_high(t + 1)
                if t == 0:
                    for s in range(XH):
                        act.wait_ge(o_loaded, 16 * XH)
                        act.activation(k.xwo_hi[:, s, :], rawo[:, s, :], ACT.Copy).then_inc(w_hi, 1)
            for t in (NT - 2, NT - 1):
                copy_x2(t)

        @block.vector
        def _(dve):
            chain = [0]

            def link(ins):
                chain[0] += 1
                ins.then_inc(dve_chain, 1)
                dve.wait_ge(dve_chain, chain[0])

            def x_rest(t):
                dve.wait_ge(x_hi, t + 1)
                dve.tensor_tensor(xlo[:].rearrange(flat), tps[:].rearrange(flat), xhi[:].rearrange(flat).bitcast(f32), ALU.subtract)\
                   .then_inc(x_lo, 1)

            def residual(t):
                dve.wait_ge(summed, t + 1)
                dve.scalar_tensor_tensor(x1[:, t, :], x1[:, t, :], ALPHA, acc[:].rearrange(flat), ALU.mult, ALU.add).then_inc(taken, 1)
                dve.wait_ge(taken, t + 1)
                for j in range(2):
                    last = dve.bn_stats(st[:, j, :], x1[:, t, 512 * j:512 * j + 512])
                link(last)
                dve.bn_aggr(mv[:, t % 2, :], st[:].rearrange(flat)).then_inc(var_ready, 1)

            def norm(t):
                if t == 0:
                    dve.wait_ge(loaded, 32)
                dve.wait_ge(rstd_ready, t + 1)
                link(dve.scalar_tensor_tensor(tmp[:], x1[:, t, :], mv[:, t % 2, 0:1], g[:], ALU.subtract, ALU.mult))
                dve.scalar_tensor_tensor(x1[:, t, :], tmp[:], rs[:, t % 2:t % 2 + 1], b[:], ALU.mult, ALU.add).then_inc(x2_made, 1)
                dve.wait_ge(x2_made, t + 1)

            def copy_logits(t):
                dve.wait_ge(logit, t + 1)
                dve.tensor_copy(k.logits[:, t, :], qps[:, 0:NE]).then_inc(lg_copied, 1)

            x_rest(0)
            for t in range(NT + 1):
                if t:
                    dve.wait_ge(o_hi, t)
                    dve.tensor_tensor(olo[:].rearrange(flat), ops[:], ohi[:].rearrange(flat).bitcast(f32), ALU.subtract)\
                       .then_inc(o_lo, 1)
                if t < NT:
                    dve.wait_ge(scored, t + 1)
                    for j in range(2):
                        last = dve.tensor_reduce(nmx[:, 2 * j:2 * j + 2], sps[:, j, :].rearrange("p (h m) -> p h m", m=MEM), AX.X, ALU.max, negate=True)
                    last.then_inc(maxed, 1)
                if t >= 3:
                    copy_logits(t - 3)
                if t + 1 < NT:
                    x_rest(t + 1)
                if t < NT:
                    dve.wait_ge(exps, XH * (t + 1))
                    link(dve.reciprocal(rinv[:], rsum[:]))
                    dve.tensor_tensor(prob[:], prob[:], over(rinv[:, :, None], [P, XH, MEM]), ALU.mult).then_inc(scaled, 1)
                if t >= 2:
                    norm(t - 2)
                if t == 0:
                    for s in range(XH):
                        dve.wait_ge(w_hi, s + 1)
                        dve.tensor_tensor(k.xwo_lo[:, s, :], rawo[:, s, :], k.xwo_hi[:, s, :].bitcast(f32), ALU.subtract).then_inc(w_lo, 1)
                if t:
                    residual(t - 1)
            copy_logits(NT - 2)
            norm(NT - 1)
            copy_logits(NT - 1)

        @block.gpsimd
        def _(pool):
            chain = [0]

            def link(ins):
                chain[0] += 1
                ins.then_inc(pool_chain, 1)
                pool.wait_ge(pool_chain, chain[0])

            link(pool.memset(half[:], -0.5))
            for t in range(NT):
                pool.wait_ge(var_ready, t + 1)
                link(pool.tensor_scalar(mv[:, t % 2, 1:2], mv[:, t % 2, 1:2], EPS, None, ALU.add))
                pool.tensor_tensor(rs[:, t % 2:t % 2 + 1], mv[:, t % 2, 1:2], half[:], ALU.pow).then_inc(rstd_ready, 1)



def route(nc, k):
    at, A, cst = k.at, k.dram, k.cst
    NB = 2 * NE
    rb = at("router_bias", 20.5, [P, NE])
    ones = at("ones", 21, [P, P], bf16)
    tri = at("up_to", 21.25, [P, P], bf16)
    sel_b = at("selected_b", 26, [P, NT, NE], bf16)
    score = at("score", 21.5, [P, NT, NE])
    bia = at("biased", 22, [P, NT, NE])
    beats = at("beats", 22.5, [P, EG, NT * NG, EG])
    rank = at("rank", 24.5, [P, NT * NG, EG])
    picked = at("picked", 25, [P, NT * NG, EG])
    gsum = at("group_sum", 25.5, [P, NT, NG])
    gbeats = at("group_beats", 25.75, [P, NG, NT, NG])
    sel = at("selected", 26.25, [P, NT, NE])
    gate = at("gate", 26.75, [P, NT, NE])
    den = at("gate_den", 27.25, [P, NT])
    fits = at("fits", 27.5, [P, NT, NE])
    key = at("slot_key", 28, [P, NT, NE])
    val = at("slot_val", 28.5, [P, NT, NE])
    code = at("slot_code", 29, [P, 2, NT])
    over_cap = at("over_cap", 29.25, [P, NT, NE])
    ovsum = at("over_sum", 29.75, [P, 1], bf16)
    row_id = at("row_id", 30, [P, 1])
    tile_id = at("tile_id", 30.0625, [P, NT])
    base = at("expert_base", 30.125, [P, NE])
    starts = at("block_starts", 30.25, [P, NB + 1])
    rows1 = at("block_rows", 30.5, [P, P])
    reached = at("reached", 31, [P, 2 * NT, NB + 1])
    inblock = at("in_block", 33.25, [P, 2 * NT, NB])
    passed = at("passed", 35.25, [P, 2 * NT])
    row = at("slot_row", 35.375, [P, 2 * NT])
    tokf = at("slot_tokens_f", 35.5, [P, NB])
    spare = at("spare_row", 35.75, [P, NB])
    spare_id = at("spare_id", 35.875, [P, NB])
    hot_row = at("row_onehot", 36, [P, 2 * NT, P], bf16)
    numbers = at("block_numbers", 40, [P, 2 * NT, 2, NB], bf16)
    loaded = k.sem("router_loaded")
    sig, selected, placed = k.sem("sigmoids"), k.sem("selected"), k.sem("placed")
    hot, listed, ov_made, ov_sum = k.sem("onehot_made"), k.sem("listed"), k.sem("over_made"), k.sem("over_summed")
    consts_made, chain_s, comb_made = k.sem("consts7"), k.sem("chain7"), k.sem("comb_made")
    q3 = lambda ap: ap.rearrange("p t (g e) -> p (t g) e", e=EG)
    with nc.psum_tensor("place_ps", [P, 512], f32) as pps, nc.psum_tensor("list_ps", [P, 512], f32) as sps, \
            nc.psum_tensor("over_ps", [P, 512], f32) as ops, nc.Block() as block:

        @block.sync
        def _(sp):
            sp.dma_start(rb[:], over(A["router_bias"], [P, NE])).then_inc(loaded, 16)
            for s in range(KD):
                sp.dma_start(k.e_raw[:, s, :], A["w_gu"][s]).then_inc(k.e_loaded[s], 16)
            sp.wait_ge(comb_made, 1)
            sp.dma_start(k.x2_dram[0:S, D:D + NE].rearrange("(t p) e -> p t e", p=P), k.comb[:]).then_inc(k.x2_stored, 16)

        @block.tensor
        def _(pe):
            pe.wait_ge(selected, 2)
            pe.wait_ge(consts_made, 8)
            pe.matmul(pps[:, 0:NT * NE], tri[:], sel_b[:].rearrange("p t e -> p (t e)"), start=True, stop=False)
            for t in range(NT - 1):
                n = NT - 1 - t
                last = pe.matmul(pps[:, (t + 1) * NE:NT * NE], ones[:], over(sel_b[:, t:t + 1, :], [P, n, NE]), start=False, stop=(n == 1))
            last.then_inc(placed, 1)
            pe.wait_ge(hot, 3)
            for q in range(2 * NT):
                last = pe.matmul(sps[:, 0:2 * NB], hot_row[:, q, :], numbers[:, q].rearrange("p c b -> p (c b)"),
                                 start=(q == 0), stop=(q == 2 * NT - 1))
            last.then_inc(listed, 1)
            pe.wait_ge(ov_made, 1)
            pe.matmul(ops[0:1, 0:1], ovsum[:], ones[:, 0:1], start=True, stop=True).then_inc(ov_sum, 1)

        @block.scalar
        def _(act):
            act.activation(score[:], k.logits[:], ACT.Sigmoid).then_inc(sig, 1)

        @block.vector
        def _(dve):
            chain = [0]

            def link(ins):
                chain[0] += 1
                ins.then_inc(chain_s, 1)
                dve.wait_ge(chain_s, chain[0])

            dve.memset(beats[:], 0.0)
            link(dve.memset(gbeats[:], 0.0))
            dve.wait_ge(loaded, 16)
            dve.wait_ge(sig, 1)
            link(dve.tensor_tensor(bia[:], score[:], over(rb[:, None, :], [P, NT, NE]), ALU.add))

            def rank_of(out, b, v):
                n = v.shape[1]
                for j in range(4):
                    if j < 3:
                        last = dve.tensor_tensor(b[:, j, :, j + 1:4], over(v[:, :, j:j + 1], [P, n, 3 - j]), v[:, :, j + 1:4], ALU.is_ge)
                    if j:
                        last = dve.tensor_tensor(b[:, j, :, 0:j], over(v[:, :, j:j + 1], [P, n, j]), v[:, :, 0:j], ALU.is_gt)
                link(last)
                link(dve.tensor_reduce(out, b[:].rearrange("p j n i -> p n i j"), AX.X, ALU.add))

            rank_of(rank[:], beats, q3(bia[:]))
            link(dve.tensor_scalar(rank[:], rank[:], 2.0, None, ALU.is_lt))
            link(dve.tensor_tensor(picked[:], rank[:], q3(bia[:]), ALU.mult))
            link(dve.tensor_reduce(gsum[:].rearrange("p t g -> p (t g)"), picked[:], AX.X, ALU.add))
            grank = picked[:, 0:NT, :]
            rank_of(grank, gbeats, gsum[:])
            link(dve.tensor_scalar(grank, grank, 1.0, None, ALU.is_lt))
            dve.tensor_tensor(q3(sel[:]), rank[:], over(picked[:, 0:NT, :].rearrange("p t g -> p (t g)")[:, :, None], [P, NT * NG, EG]),
                              ALU.mult).then_inc(selected, 1)
            dve.wait_ge(selected, 1)
            dve.tensor_copy(sel_b[:], sel[:]).then_inc(selected, 1)
            link(dve.tensor_tensor(gate[:], sel[:], score[:], ALU.mult))
            link(dve.tensor_reduce(den[:], gate[:], AX.X, ALU.add))
            link(dve.reciprocal(den[:], den[:]))
            dve.tensor_tensor(k.comb[:], gate[:], over(den[:, :, None], [P, NT, NE]), ALU.mult).then_inc(comb_made, 1)
            dve.wait_ge(placed, 1)
            dve.wait_ge(consts_made, 8)
            place = pps[:, 0:NT * NE].rearrange("p (t e) -> p t e", e=NE)
            link(dve.tensor_tensor(key[:], place, sel[:], ALU.mult))
            dve.tensor_tensor(val[:], key[:], over(base[:, None, :], [P, NT, NE]), ALU.add)
            link(dve.tensor_scalar(fits[:], key[:], float(CAP) + 0.5, None, ALU.is_lt))
            link(dve.tensor_tensor(fits[:], fits[:], sel[:], ALU.mult))
            link(dve.tensor_tensor(val[:], val[:], fits[:], ALU.mult))
            dve.tensor_reduce(code[:, 0, :], val[:], AX.X, ALU.max)
            link(dve.tensor_reduce(code[:, 1, :], val[:], AX.X, ALU.add))
            link(dve.tensor_tensor(code[:, 1, :], code[:, 1, :], code[:, 0, :], ALU.subtract))
            codes = code[:].rearrange("p j t -> p (j t)")
            link(dve.tensor_tensor(reached[:], over(codes[:, :, None], [P, 2 * NT, NB + 1]), over(starts[:, None, :], [P, 2 * NT, NB + 1]), ALU.is_ge))
            dve.tensor_tensor(inblock[:], reached[:, :, 0:NB], reached[:, :, 1:NB + 1], ALU.subtract)
            link(dve.tensor_reduce(passed[:], reached[:, :, 1:NB + 1], AX.X, ALU.add))
            link(dve.scalar_tensor_tensor(row[:], passed[:], -float(P), codes, ALU.mult, ALU.add))
            dve.tensor_tensor(hot_row[:], over(row[:, :, None], [P, 2 * NT, P]), over(rows1[:, None, :], [P, 2 * NT, P]), ALU.is_equal)\
               .then_inc(hot, 1)
            dve.tensor_scalar(numbers[:, :, 0, :], inblock[:], row_id[:, 0:1], None, ALU.mult).then_inc(hot, 1)
            dve.tensor_tensor(numbers[:, :, 1, :].rearrange("p (j t) b -> p j t b", j=2), inblock[:].rearrange("p (j t) b -> p j t b", j=2),
                              over(tile_id[:, None, :, None], [P, 2, NT, NB]), ALU.mult).then_inc(hot, 1)
            link(dve.tensor_tensor(over_cap[:], sel[:], fits[:], ALU.subtract))
            link(dve.tensor_reduce(den[:, 0:1], over_cap[:], AX.XY, ALU.add))
            link(dve.tensor_copy(ovsum[:], den[:, 0:1]))
            dve.tensor_tensor(k.comb_over[:], over_cap[:], k.comb[:], ALU.mult).then_inc(ov_made, 1)
            dve.wait_ge(listed, 1)
            link(dve.tensor_reduce(tokf[:], sps[:, 0:2 * NB].rearrange("p (c b) -> p b c", c=2), AX.X, ALU.add))
            link(dve.scalar_tensor_tensor(spare[:], tokf[:], 0.0, spare_id[:], ALU.is_ge, ALU.mult))
            link(dve.scalar_tensor_tensor(tokf[:], tokf[:], float(S), spare[:], ALU.add, ALU.add))
            dve.tensor_copy(k.tok[:].rearrange("p e b -> p (e b)"), tokf[:])
            dve.wait_ge(ov_sum, 1)
            link(dve.tensor_copy(k.over_flag[:], ops[0:1, 0:1]))

        @block.gpsimd
        def _(pool):
            imprecise = dict(allow_small_or_imprecise_dtypes=True)
            pool.memset(ones[:], 1.0).then_inc(consts_made, 1)
            pool.tensor_copy(tri[:], cst[:, C_TRI:C_TRI + P]).then_inc(consts_made, 1)
            pool.iota(base[:], [[2 * P, NE]], base=0, channel_multiplier=0, **imprecise).then_inc(consts_made, 1)
            pool.iota(starts[:], [[P, NB + 1]], base=1, channel_multiplier=0, **imprecise).then_inc(consts_made, 1)
            pool.iota(rows1[:], [[1, P]], base=1, channel_multiplier=0, **imprecise).then_inc(consts_made, 1)
            pool.iota(row_id[:], [[0, 1]], base=0, channel_multiplier=1, **imprecise).then_inc(consts_made, 1)
            pool.iota(spare_id[:], [[0, NE], [P, 2]], base=0, channel_multiplier=1, **imprecise).then_inc(consts_made, 1)
            pool.iota(tile_id[:], [[P, NT]], base=-S, channel_multiplier=0, **imprecise).then_inc(consts_made, 1)


def experts(nc, k):
    at, A, cst = k.at, k.dram, k.cst
    GU, DN = KD, 4
    SL = GU + DN
    B1 = CAP - P
    whi = at("e_hi", 12, [P, 2, SL, 512], f32r)
    wlo = at("e_lo", 60, [P, 2, SL, 512], f32r)
    raw = k.e_raw
    xg = [[at(f"x_rows{b}{c}", kib, [P, D + NE]) for c, kib in enumerate(two)] for b, two in enumerate(((132, 136.0625), (140.125, 164)))]
    tk = at("tok_gather", 145, [P, 2], i32)
    sk = at("tok_add", 145.03125, [P, 2], i32)
    wgt = at("slot_weight", 145.0625, [P, 2, 2])
    hh = at("h", 145.5, [P, 2, CAP])
    act_g = at("silu_g", 147, [P, 2, CAP])
    xhi = at("xgT_hi", 149, [P, KD, CAP], f32r)
    xlo = at("xgT_lo", 155, [P, KD, CAP], f32r)
    hhi = at("h_hi", 161, [P, 2, CAP], f32r)
    hlo = at("h_lo", 162.5, [P, 2, CAP], f32r)
    yo = [at("y_out_a", 6, [P, D]), at("y_out_b", 201, [P, D])]
    ident = cst[:, C_ID:C_ID + P]
    w_loaded = k.e_loaded
    hi_done, gu_lo, dn_lo = k.sem("e_hi_done"), k.sem("gu_lo_done"), k.sem("dn_lo_done")
    rows_loaded = [k.sem("rows_loaded_even"), k.sem("rows_loaded_odd")]
    tok_copied, wgt_copied = k.sem("tok_copied"), k.sem("wgt_copied")
    rows_t, xhi_done, xlo_done = k.sem("rows_t"), k.sem("exhi_done"), k.sem("exlo_done")
    gsum = k.sem("gu_sum")
    silu, hmul = k.sem("silu_done"), k.sem("h_mul")
    hhi_done, hlo_done = k.sem("hhi_done"), k.sem("hlo_done")
    ysum, y_taken = k.sem("y_sum"), k.sem("y_taken")
    held, y_added, y_free = k.sem("held"), k.sem("y_added"), k.sem("y_free")
    blocks = [(0, P), (P, B1)]
    UNITS = [(0, 0), (0, 1), (1, 0), (1, 1)]
    BANK = [0, 1, 2, 0]

    def steps(eng, step):
        with eng.Fori(0, NE // 2 - 1) as i:
            for b in range(2):
                step(lambda a, c: i * (2 * a) + (b * a + c), lambda a, c: i * a + c, i * 2 + b, b, False)
        for e in (NE - 2, NE - 1):
            step(lambda a, c: e * a + c, lambda a, c: e // 2 * a + c, e, e % 2, e == NE - 1)

    with nc.psum_tensor("rowsT_ps", [P, 3, 512], f32) as tps, nc.psum_tensor("h_ps", [P, 2, 512], f32) as hps, \
            nc.psum_tensor("y_ps", [P, 3, 512], f32) as yps, nc.Block() as block:

        @block.sync
        def _(sp):
            def load(s, row):
                src = A["w_gu"] if s < GU else A["w_dn"]
                sp.dma_start(raw[:, s, :], src[bass.ds(row, 1)].rearrange("a p n -> p (a n)")).then_inc(w_loaded[s], 16)

            sp.sem_inc(dn_lo, DN)

            def step(n, h, e, b, last):
                for s in range(DN):
                    sp.wait_ge(dn_lo, n(DN, s + 1))
                    load(GU + s, n(DN, s))
                if not last:
                    for s in range(GU):
                        sp.wait_ge(gu_lo, n(GU, s + 1))
                        load(s, n(GU, GU + s))

            steps(sp, step)

        @block.gpsimd
        def _(pool):
            def hold(sem, value):
                pool.wait_ge(sem, value)
                pool.sem_inc(held, 1)

            def list_of(dst, e, n):
                pool.tensor_copy(dst[:], k.tok[:, bass.ds(e, 1), :].rearrange("p a c -> p (a c)")).then_inc(tok_copied, 1)
                hold(tok_copied, n)

            def gather(b):
                for c, (_, rows) in enumerate(blocks):
                    pool.indirect_dma_start(xg[b][c][0:rows, :], None, k.x2_dram, bass.IndirectOffsetOnAxis(ap=tk[0:rows, c:c + 1], axis=0))\
                        .then_inc(rows_loaded[b], 16)

            pool.sem_inc(y_free, 1)
            pool.wait_ge(k.x2_stored, 16 * (NT + 1))
            pool.wait_ge(k.rows_zeroed, 16 * (NT + 4))
            for e in range(2):
                if e:
                    pool.wait_ge(rows_loaded[0], 32)
                list_of(tk, e, e + 1)
                gather(e)

            def step(n, h, e, b, last):
                ahead = not isinstance(e, int)
                if ahead:
                    pool.wait_ge(rows_t, n(1, 1))
                    pool.wait_ge(wgt_copied, n(1, 1))
                    pool.wait_ge(rows_loaded[1 - b], h(32, 32 * (1 + b)))
                    list_of(tk, n(1, 2), n(2, 3))
                    gather(b)
                list_of(sk, e, n(2, 4) if ahead else e + NE + 1)
                for c, (_, rows) in enumerate(blocks):
                    hold(y_taken, n(4, 2 * c + 6))
                    pool.indirect_dma_start(k.y_dram, bass.IndirectOffsetOnAxis(ap=sk[0:rows, c:c + 1], axis=0),
                                            yo[c][slice(0, P) if c == 0 else slice(P - B1, P), :], None, compute_op=ALU.add)\
                        .then_inc(y_added, 16)
                pool.wait_ge(y_added, n(32, 32))
                pool.sem_inc(y_free, 1)

            steps(pool, step)

        @block.tensor
        def _(pe):
            def turn(b, n):
                pe.wait_ge(rows_loaded[b], n)
                for s in range(KD):
                    pe.transpose(tps[:, s // 4, (s % 4) * P:(s % 4 + 1) * P], xg[b][0][:, s * P:(s + 1) * P], ident)
                for s in range(KD):
                    last = pe.transpose(tps[:, 2, s * B1:(s + 1) * B1], xg[b][1][0:B1, s * P:(s + 1) * P], ident[0:B1, 0:B1])
                last.then_inc(rows_t, 1)

            pe.sem_inc(y_taken, 4)
            turn(0, 32)

            def step(n, h, e, b, last):
                pe.wait_ge(xlo_done, n(1, 1))
                for m in range(2):
                    pe.wait_ge(hmul, n(2, m + 1))
                    for gu in range(2):
                        o = hps[:, m, gu * CAP:(gu + 1) * CAP]
                        w = slice(gu * DE + m * P, gu * DE + (m + 1) * P)
                        for s in range(GU):
                            if m == 0 and gu == 0:
                                pe.wait_ge(gu_lo, n(GU, s + 1))
                            hi, lo = whi[:, b, s, w], wlo[:, b, s, w]
                            pe.matmul(o, hi, xhi[:, s, :], start=(s == 0), stop=False)
                            pe.matmul(o, hi, xlo[:, s, :], start=False, stop=False)
                            end = pe.matmul(o, lo, xhi[:, s, :], start=False, stop=(s == GU - 1))
                    end.then_inc(gsum, 1)
                if not last:
                    turn(1 - b, h(32, 32 * (1 + b)))

                def down(u, f):
                    c, j = UNITS[u]
                    sl = slice(0, P) if c == 0 else slice(CAP - P, CAP)
                    hi, lo, w = hhi[:, f, sl], hlo[:, f, sl], GU + 2 * f + j
                    o = yps[:, BANK[u], :]
                    pe.matmul(o, hi, whi[:, b, w, :], start=(f == 0), stop=False)
                    pe.matmul(o, hi, wlo[:, b, w, :], start=False, stop=False)
                    return pe.matmul(o, lo, whi[:, b, w, :], start=False, stop=(f == 1))

                pe.wait_ge(dn_lo, n(DN, 2 * DN))
                pe.wait_ge(hlo_done, n(2, 1))
                for u, free in ((0, 4), (1, 2), (2, 3)):
                    pe.wait_ge(y_taken, n(4, free))
                    down(u, 0)
                pe.wait_ge(hlo_done, n(2, 2))
                for u in range(3):
                    down(u, 1).then_inc(ysum, 1)
                pe.wait_ge(y_taken, n(4, 5))
                down(3, 0)
                down(3, 1).then_inc(ysum, 1)

            steps(pe, step)

        @block.scalar
        def _(act):
            def rows_high(n):
                for j in range(2):
                    act.activation(xhi[:, 4 * j:4 * j + 4, 0:P], tps[:, j, :].rearrange("p (s c) -> p s c", c=P), ACT.Copy)
                act.activation(xhi[:, :, P:CAP], tps[:, 2, :].rearrange("p (s c) -> p s c", c=B1), ACT.Copy).then_inc(xhi_done, 1)

            def high(b, s):
                act.activation(whi[:, b, s, :], raw[:, s, :], ACT.Copy).then_inc(hi_done, 1)

            act.sem_inc(gsum, 2)
            act.sem_inc(ysum, 8)
            for s in range(GU):
                act.wait_ge(w_loaded[s], 16)
                high(0, s)
            act.wait_ge(rows_t, 1)
            rows_high(lambda a, c: c)

            def step(n, h, e, b, last):
                act.wait_ge(ysum, n(4, 4))
                for s in range(GU, SL):
                    act.wait_ge(w_loaded[s], n(16, 16))
                    high(b, s)
                for m in range(2):
                    if not last:
                        act.wait_ge(gsum, n(2, 2))
                        for s in range(4 * m, 4 * m + 4):
                            act.wait_ge(w_loaded[s], n(16, 32))
                            high(1 - b, s)
                    act.wait_ge(gsum, n(2, m + 3))
                    act.wait_ge(hmul, n(2, m + 1))
                    act.activation(act_g[:, m, :], hps[:, m, 0:CAP], ACT.Silu).then_inc(silu, 1)
                    act.wait_ge(hmul, n(2, m + 3))
                    act.activation(hhi[:, m, :], hh[:, m, :], ACT.Copy).then_inc(hhi_done, 1)
                if not last:
                    act.wait_ge(rows_t, n(1, 2))
                    act.wait_ge(gsum, n(2, 4))
                    rows_high(n)
                for u, (c, j) in enumerate(UNITS):
                    if j == 0:
                        act.wait_ge(y_free, n(1, 1))
                        act.wait_ge(wgt_copied, n(1, 1))
                    act.wait_ge(ysum, n(4, u + 9))
                    r = slice(0, P) if c == 0 else slice(P - B1, P)
                    act.activation(yo[c][r, 512 * j:512 * j + 512], yps[r, BANK[u], :], ACT.Copy, scale=wgt[r, b, c:c + 1])\
                       .then_inc(y_taken, 1)

            steps(act, step)

        @block.vector
        def _(dve):
            def rows_rest(n, col, b):
                dve.tensor_copy(wgt[:, b, 0:1], xg[b][0][:, bass.ds(col, 1)])
                dve.tensor_copy(wgt[P - B1:P, b, 1:2], xg[b][1][0:B1, bass.ds(col, 1)]).then_inc(wgt_copied, 1)
                dve.wait_ge(xhi_done, n(1, 1))
                for j in range(2):
                    dve.tensor_tensor(xlo[:, 4 * j:4 * j + 4, 0:P], tps[:, j, :].rearrange("p (s c) -> p s c", c=P),
                                      xhi[:, 4 * j:4 * j + 4, 0:P].bitcast(f32), ALU.subtract)
                dve.tensor_tensor(xlo[:, :, P:CAP], tps[:, 2, :].rearrange("p (s c) -> p s c", c=B1),
                                  xhi[:, :, P:CAP].bitcast(f32), ALU.subtract).then_inc(xlo_done, 1)

            def rest(b, s, sem):
                dve.tensor_tensor(wlo[:, b, s, :], raw[:, s, :], whi[:, b, s, :].bitcast(f32), ALU.subtract).then_inc(sem, 1)

            dve.sem_inc(hmul, 2)
            for s in range(GU):
                dve.wait_ge(hi_done, s + 1)
                rest(0, s, gu_lo)
            dve.wait_ge(rows_loaded[0], 32)
            rows_rest(lambda a, c: c, D, 0)

            def step(n, h, e, b, last):
                for s in range(DN):
                    dve.wait_ge(hi_done, n(SL, GU + s + 1))
                    rest(b, GU + s, dn_lo)
                for m in range(2):
                    if not last:
                        for s in range(4 * m, 4 * m + 4):
                            dve.wait_ge(hi_done, n(SL, SL + s + 1))
                            rest(1 - b, s, gu_lo)
                    dve.wait_ge(silu, n(2, m + 1))
                    dve.tensor_tensor(hh[:, m, :], act_g[:, m, :], hps[:, m, CAP:2 * CAP], ALU.mult).then_inc(hmul, 1)
                    dve.wait_ge(hhi_done, n(2, m + 1))
                    dve.tensor_tensor(hlo[:, m, :], hh[:, m, :], hhi[:, m, :].bitcast(f32), ALU.subtract).then_inc(hlo_done, 1)
                if not last:
                    dve.wait_ge(rows_loaded[1 - b], h(32, 32 * (1 + b)))
                    dve.wait_ge(y_taken, n(4, 4))
                    rows_rest(lambda a, c: n(a, a + c), n(1, D + 1), 1 - b)

            steps(dve, step)


def overflow(nc, k):
    at, A, cst = k.at, k.dram, k.cst
    xT = at("ov_x2T", 12, [P, NT, KD, P])
    xs = at("ov_tile", 44, [P, KD, P])
    gu = at("ov_gate_up", 48, [P, KD, 2 * DE])
    dn = at("ov_down", 64, [P, 4, D // 2])
    gate = at("ov_gate", 72, [P, 2, P])
    hid = at("ov_hidden", 73, [P, 2, P])
    wgt = at("ov_weight", 74, [P, 1])
    ysb = at("ov_y", 76, [P, D])
    ident = cst[:, C_ID:C_ID + P]
    x2 = k.x1
    turned, copied, w_loaded = k.sem("ov_turned"), k.sem("ov_copied"), k.sem("ov_loaded")
    staged, h_sum, silu, h_made = k.sem("ov_staged"), k.sem("ov_h_sum"), k.sem("ov_silu"), k.sem("ov_h_made")
    y_sum, y_out, added = k.sem("ov_y_sum"), k.sem("ov_y_out"), k.sem("ov_added")
    weighted, w_used = k.sem("ov_weighted"), k.sem("ov_w_used")

    def over_all(eng, expert, tile):
        with eng.Fori(0, NE) as e:
            expert(e)
            if tile:
                with eng.Fori(0, NT) as t:
                    tile(e * NT + t, e, t)

    with nc.psum_tensor("ovT_ps", [P, 2, 512], f32) as tps, nc.psum_tensor("ov_h_ps", [P, 512], f32) as hps, \
            nc.psum_tensor("ov_y_ps", [P, 2, 512], f32) as yps, nc.Block() as block:

        @block.sync
        def _(sp):
            with sp.If(sp.value_load(k.over_flag[0:1, 0:1], min_val=0, max_val=2 * S) > 0):
                def expert(e):
                    sp.wait_ge(w_used, e + 1)
                    sp.dma_start(gu[:], A["w_gu"][bass.ds(e * KD, KD)].rearrange("s p n -> p s n")).then_inc(w_loaded, 16)
                    sp.dma_start(dn[:], A["w_dn"][bass.ds(e * 4, 4)].rearrange("s p n -> p s n")).then_inc(w_loaded, 16)

                sp.sem_inc(w_used, 1)
                over_all(sp, expert, None)

        @block.tensor
        def _(pe):
            with pe.If(pe.value_load(k.over_flag[0:1, 0:1], min_val=0, max_val=2 * S) > 0):
                for t in range(NT):
                    if t:
                        pe.wait_ge(copied, t)
                    for s in range(KD):
                        last = pe.transpose(tps[:, s // 4, (s % 4) * P:(s % 4 + 1) * P], x2[:, t, s * P:(s + 1) * P], ident)
                    last.then_inc(turned, 1)

                def tile(n, e, t):
                    pe.wait_ge(w_loaded, e * 32 + 32)
                    pe.wait_ge(staged, n + 1)
                    for j in range(4):
                        for s in range(KD):
                            last = pe.matmul(hps[:, j * P:(j + 1) * P], gu[:, s, j * P:(j + 1) * P], xs[:, s, :],
                                             start=(s == 0), stop=(s == KD - 1))
                    last.then_inc(h_sum, 1)
                    pe.wait_ge(h_made, n + 1)
                    for j in range(2):
                        for f in range(2):
                            last = pe.matmul(yps[:, j, :], hid[:, f, :], dn[:, 2 * f + j, :], start=(f == 0), stop=(f == 1))
                    last.then_inc(y_sum, 1)

                with pe.Fori(0, NE) as e:
                    with pe.Fori(0, NT) as t:
                        tile(e * NT + t, e, t)
                    pe.wait_ge(y_sum, e * NT + NT)
                    pe.sem_inc(w_used, 1)

        @block.scalar
        def _(act):
            with act.If(act.value_load(k.over_flag[0:1, 0:1], min_val=0, max_val=2 * S) > 0):
                def tile(n, e, t):
                    act.wait_ge(h_sum, n + 1)
                    act.activation(gate[:].rearrange("p f c -> p (f c)"), hps[:, 0:2 * P], ACT.Silu).then_inc(silu, 1)
                    act.wait_ge(y_sum, n + 1)
                    act.wait_ge(weighted, n + 1)
                    act.wait_ge(added, n + 1)
                    act.activation(ysb[:], yps[:].rearrange("p j c -> p (j c)"), ACT.Copy, scale=wgt[:]).then_inc(y_out, 1)

                over_all(act, lambda e: None, tile)

        @block.vector
        def _(dve):
            with dve.If(dve.value_load(k.over_flag[0:1, 0:1], min_val=0, max_val=2 * S) > 0):
                for t in range(NT):
                    dve.wait_ge(turned, t + 1)
                    dve.tensor_copy(xT[:, t].rearrange("p s c -> p (s c)"), tps[:].rearrange("p j c -> p (j c)")).then_inc(copied, 1)
                dve.tensor_scalar(k.comb_over[:], k.comb_over[:], 1.0 / ALPHA, None, ALU.mult).then_inc(copied, 1)
                dve.wait_ge(copied, NT + 1)

                def tile(n, e, t):
                    dve.wait_ge(y_out, n + 1)
                    dve.tensor_copy(xs[:], xT[:, bass.ds(t, 1)].rearrange("p t s c -> p (t s) c")).then_inc(staged, 1)
                    dve.tensor_copy(wgt[:], k.comb_over[:, bass.ds(t, 1), bass.ds(e, 1)].rearrange("p t e -> p (t e)")).then_inc(weighted, 1)
                    dve.wait_ge(silu, n + 1)
                    dve.tensor_tensor(hid[:].rearrange("p f c -> p (f c)"), gate[:].rearrange("p f c -> p (f c)"), hps[:, 2 * P:4 * P], ALU.mult)\
                       .then_inc(h_made, 1)
                    dve.wait_ge(y_out, n + 2)
                    x = x2[:, bass.ds(t, 1), :].rearrange("p t c -> p (t c)")
                    dve.tensor_tensor(x, x, ysb[:], ALU.add).then_inc(added, 1)

                dve.sem_inc(added, 1)
                dve.sem_inc(y_out, 1)
                over_all(dve, lambda e: None, tile)


def finish(nc, k):
    at, A = k.at, k.dram
    g = at("ln3_g", 12, [P, D])
    b = at("ln3_b", 16, [P, D])
    tmp = at("ln3_tmp", 20, [P, 2, D])
    nrm = at("ln3_norm", 40, [P, 2, D])
    nmr = at("ln3_neg_mu_rs", 36.5, [P, NT])
    yt = at("ln3_out", 48, [P, NT, D])
    own = at("ln3_own", 28, [P, D])
    st = at("ln3_st", 36, [P, 2, 2, 6])
    mv = at("ln3_mv", 36.125, [P, NT, 2])
    rs = at("ln3_rs", 36.25, [P, NT])
    half = at("ln3_half", 36.375, [P, 1])
    loaded, scaled = k.sem("gains10_loaded"), k.sem("x2_scaled")
    added = [k.sem(f"added{t}") for t in range(NT)]
    var_ready, rstd_ready = k.sem("ln3_var"), k.sem("ln3_rstd")
    chain_s, chain_p, made = k.sem("chain10"), k.sem("pool_chain10"), k.sem("out_made")
    shifts, normed, gained = k.sem("ln3_shifts"), k.sem("ln3_normed"), k.sem("ln3_gained")
    own_made, stored = k.sem("own_out_made"), k.sem("out_stored")
    x2 = k.x1
    with nc.Block() as block:

        @block.sync
        def _(sp):
            sp.dma_start(g[:], over(A["ln_moe_g"], [P, D])).then_inc(loaded, 16)
            sp.dma_start(b[:], over(A["ln_moe_b"], [P, D])).then_inc(loaded, 16)
            for t in range(NT):
                sp.wait_ge(made if t % 2 == 0 else own_made, t // 2 + 1)
                sp.dma_start(A["out"][t * P:(t + 1) * P, :], yt[:, t, :]).then_inc(stored, 16)
            sp.wait_ge(stored, 16 * NT)

        @block.scalar
        def _(act):
            for t in range(NT):
                act.activation(x2[:, t, :], x2[:, t, :], ACT.Copy, scale=ALPHA).then_inc(scaled, 1)
            for n in range(NT // 2):
                t = 2 * n
                act.wait_ge(shifts, n + 1)
                if n >= 2:
                    act.wait_ge(gained, n - 1)
                act.activation(nrm[:, n % 2, :], x2[:, t, :], ACT.Identity, scale=rs[:, t:t + 1], bias=nmr[:, t:t + 1]).then_inc(normed, 1)

        @block.gpsimd
        def _(pool):
            pool.memset(half[:], -0.5).then_inc(chain_p, 1)
            pool.wait_ge(chain_p, 1)
            n = 1

            def add(t):
                pool.wait_ge(scaled, t + 1)
                pool.dma_start(x2[:, t, :], k.y_dram[t * P:(t + 1) * P, :], accum_op=ALU.add).then_inc(added[t], 16)

            def rstd(t):
                pool.wait_ge(var_ready, t + 1)
                pool.tensor_scalar(mv[:, t, 1:2], mv[:, t, 1:2], EPS, None, ALU.add).then_inc(chain_p, 1)
                pool.wait_ge(chain_p, t + 2)
                pool.tensor_tensor(rs[:, t:t + 1], mv[:, t, 1:2], half[:], ALU.pow).then_inc(rstd_ready, 1)
                if t % 2 == 0:
                    pool.wait_ge(rstd_ready, t + 1)
                    pool.tensor_scalar(nmr[:, t:t + 1], mv[:, t, 0:1], rs[:, t:t + 1], -1.0, ALU.mult, ALU.mult).then_inc(shifts, 1)

            def bias(n):
                pool.wait_ge(gained, n + 1)
                pool.tensor_tensor(yt[:, 2 * n, :], tmp[:, n % 2, :], b[:], ALU.add).then_inc(made, 1)

            AHEAD = 4
            for t in range(AHEAD):
                add(t)
            pool.wait_ge(loaded, 32)
            for t in range(NT):
                rstd(t)
                if t + AHEAD < NT:
                    add(t + AHEAD)
                if t % 2:
                    bias(t // 2)

        @block.vector
        def _(dve):
            chain = [0]

            def link(ins):
                chain[0] += 1
                ins.then_inc(chain_s, 1)
                dve.wait_ge(chain_s, chain[0])

            def gain(n):
                dve.wait_ge(normed, n + 1)
                if n >= 2:
                    dve.wait_ge(made, n - 1)
                dve.tensor_tensor(tmp[:, n % 2, :], nrm[:, n % 2, :], g[:], ALU.mult).then_inc(gained, 1)

            def norm(t):
                dve.wait_ge(rstd_ready, t + 1)
                link(dve.scalar_tensor_tensor(own[:], x2[:, t, :], mv[:, t, 0:1], g[:], ALU.subtract, ALU.mult))
                dve.scalar_tensor_tensor(yt[:, t, :], own[:], rs[:, t:t + 1], b[:], ALU.mult, ALU.add).then_inc(own_made, 1)
                dve.wait_ge(own_made, t // 2 + 1)

            dve.wait_ge(loaded, 32)
            for t in range(NT + 1):
                if t < NT:
                    dve.wait_ge(added[t], 16)
                    for j in range(2):
                        last = dve.bn_stats(st[:, t % 2, j, :], x2[:, t, 512 * j:512 * j + 512])
                    link(last)
                    dve.bn_aggr(mv[:, t, :], st[:, t % 2].rearrange("p j c -> p (j c)")).then_inc(var_ready, 1)
                if t % 2:
                    gain(t // 2)
                elif t:
                    norm(t - 1)


def program(nc, A, upto=99):
    k = Shared()
    k.dram = A
    k.at = at = placer(nc)
    k.sem = nc.alloc_semaphore
    k.cst = at("constants", 0, [P, C_COLS])
    k.sin = at("sin", 6, [P, NT, NF])
    k.cos = at("cos", 8, [P, NT, NF])
    k.qk = at("qk", 12, [P, NT, 2 * RW])
    k.rv = at("rv", 28, [P, NT, RW])
    k.sg = at("sg", 36, [P, NT, RW])
    k.su = at("su", 44, [P, NT, SW])
    k.sv = at("sv", 52, [P, NT, SW])
    k.cq = at("cq", 60, [P, NT, QR])
    k.ckv = at("ckv", 68, [P, NT, KVR])
    k.kr = at("kr", 72, [P, NT, ROPE])
    k.mixA = at("mix_ret_sgu", 73, [P, NT, RW + SW])
    k.mixB = at("mix_mla", 89, [P, NT, MW])
    k.kT = at("mla_kT", 105, [P, MH, S])
    k.qT = at("mla_qT", 137, [P, MH, S])
    k.v = at("mla_v", 169, [P, NT, MW])
    k.w_out_raw, k.w_out_loaded = at("w_out_raw", 30, [P, KD, D]), k.sem("w_out_loaded")
    k.wuq = at("w_uq", 192, [P, QR // P, MH * MQ])
    k.wukv = at("w_ukv", 198, [P, 2 * MW])
    k.wsg = at("sgu_wT", 202, [P, SG, P])
    k.gq, k.gkv, k.sgb = at("q_norm_g", 10, [P, 2]), at("kv_norm_g", 10.0625, [P, 1]), at("sgu_bias", 10.125, [P, SG])
    k.up_loaded, k.up_ready = k.sem("up_loaded"), k.sem("up_ready")
    k.x1 = at("x1", 169, [P, NT, D])
    k.wk, k.wv, k.kv_loaded = at("xa_wk_raw", 30, [P, KD, XW]), at("xa_wv_raw", 46, [P, KD, XW]), k.sem("kv_loaded")
    k.wq_hi, k.wq_lo = at("wq_hi", 105, [P, KD, XW], f32r), at("wq_lo", 121, [P, KD, XW], f32r)
    k.xwo_hi, k.xwo_lo = at("xwo_hi", 137, [P, XH, D], f32r), at("xwo_lo", 153, [P, XH, D], f32r)
    k.xkT, k.xv = at("xkT", 12, [P, XH, MEM]), at("xv", 16, [P, 2, XW])
    k.x2_dram = nc.dram_tensor("x2_rows", [S + 2 * P, D + NE], f32).ap()
    k.x2_stored, k.rows_zeroed = k.sem("x2_stored"), k.sem("rows_zeroed")
    k.logits = at("logits", 204.5, [P, NT, NE])
    k.y_dram = nc.dram_tensor("y_rows", [S + 2 * P, D], f32).ap()
    k.tok = at("slot_tokens", 205, [P, NE, 2], i32)
    k.over_flag = at("over_flag", 205.1875, [1, 1], i32)
    k.e_raw, k.e_loaded = at("e_raw", 108, [P, KD + 4, 512]), [k.sem(f"e_loaded{s}") for s in range(KD + 4)]
    k.comb = at("combine", 205.25, [P, NT, NE])
    k.comb_over = at("combine_over", 205.75, [P, NT, NE])
    phases = [project, prepare, attend, mix_out, cross_attend, route, experts, overflow, finish]
    for i, f in enumerate(phases[:upto]):
        used = []

        def sem(name):
            used.append(nc.alloc_semaphore(name))
            return used[-1]

        k.sem = sem
        f(nc, k)
        if i in (1, 4):
            nc.clear_and_free_semaphores(used)
            nc.all_engine_barrier()
    return k


def layouts(x, mem, positions, w_in, w_out, sgu_ln_g, sgu_ln_b, sgu_w, sgu_b,
            mla_q_norm_g, mla_w_uq, mla_kv_norm_g, mla_w_ukv,
            xa_wq, xa_wk, xa_wv, xa_wo,
            ln_mix_g, ln_mix_b, ln_xa_g, ln_xa_b, ln_moe_g, ln_moe_b,
            router_w, router_bias, expert_w_gate, expert_w_up, expert_w_down):
    c = np.ascontiguousarray
    a = {}
    a["cst"] = constants()
    a["x"] = c(x[0])
    a["xT"] = c(np.transpose(x[0]).reshape(KD, P, S))
    a["positions"] = c(positions.reshape(NT, P).T)
    a["w_in"] = c(w_in[0])
    a["sgu_ln_g"], a["sgu_ln_b"] = c(sgu_ln_g), c(sgu_ln_b)
    a["q_norm_g"] = c(mla_q_norm_g.reshape(QR // P, P).T)
    a["kv_norm_g"] = c(mla_kv_norm_g.reshape(1, P).T)
    a["w_uq"] = c(mla_w_uq[0])
    kv = mla_w_ukv[0].reshape(KVR, MH, 2, NOPE)
    a["w_ukv"] = c(kv.transpose(0, 2, 1, 3).reshape(KVR, 2 * MW))
    a["sgu_bT"] = c(sgu_b[0].T)
    a["sgu_wT"] = c(sgu_w[0].transpose(2, 0, 1))
    a["w_out"] = c(w_out[0])
    a["ln_mix_g"], a["ln_mix_b"], a["ln_xa_g"], a["ln_xa_b"] = c(ln_mix_g), c(ln_mix_b), c(ln_xa_g), c(ln_xa_b)
    a["memT"] = c(np.transpose(mem[0]))
    a["xa_wq"], a["xa_wk"], a["xa_wv"], a["xa_wo"] = c(xa_wq[0]), c(xa_wk[0]), c(xa_wv[0]), c(xa_wo[0])
    a["router_w"], a["router_bias"] = c(router_w), c(router_bias.reshape(1, NE))
    a["w_gu"] = c(np.concatenate([expert_w_gate[0], expert_w_up[0]], axis=2).reshape(NE * KD, P, 2 * DE))
    a["w_dn"] = c(expert_w_down[0].reshape(NE, 2, P, 2, D // 2).transpose(0, 1, 3, 2, 4).reshape(NE * 4, P, D // 2))
    a["ln_moe_g"], a["ln_moe_b"] = c(ln_moe_g), c(ln_moe_b)
    return a


def kernel(**inputs):
    import concourse.bacc as bacc
    from concourse.bass_utils import run_bass_kernel_spmd
    nc = bacc.Bacc("TRN2", target_bir_lowering=False, num_devices=1)
    arrays = layouts(**{n: np.asarray(v) for n, v in inputs.items()})
    aps = {n: nc.dram_tensor(n, a.shape, mybir.dt.from_np(a.dtype), kind="ExternalInput").ap() for n, a in arrays.items()}
    aps["out"] = nc.dram_tensor("out", [S, D], f32, kind="ExternalOutput").ap()
    program(nc, aps)
    r = run_bass_kernel_spmd(nc, [arrays], core_ids=[0])
    return r.results[0]["out"].reshape(1, S, D)
```
